# Optimizing a Trainium2 kernel written in Bass

```python
import math
import jax, jax.numpy as jnp
from jax import lax
import numpy as np

D_MODEL = 1024
BATCH = 1
SEQ = 256
DEPTH = 1

ATT_WIDTH = D_MODEL // 2
ATT_HEAD_DIM = 64
ATT_HEADS = ATT_WIDTH // ATT_HEAD_DIM
MOBA_BLOCK = 256
MOBA_TOPK = 3
MOBA_QCHUNK = 64
SSM_WIDTH = D_MODEL // 2
SSM_GROUP = 16
SSM_GROUPS = SSM_WIDTH // SSM_GROUP
SSM_STATE = 64
IN_WIDTH = 3 * ATT_WIDTH + SSM_WIDTH + 2 * D_MODEL
MEM_LEN = 256
XATTN_HEADS = 4
XATTN_HEAD_DIM = D_MODEL // 8
XATTN_WIDTH = XATTN_HEADS * XATTN_HEAD_DIM
N_EXPERTS = 32
EXPERT_TOPK = 4
D_FF = D_MODEL
SWIGLU_LIMIT = 7.0
SWIGLU_ALPHA = 1.702
MOE_BLOCK = 256
RMS_EPS = 1e-6
NEG_INF = -1e30

kernel_name = "hybrid_moba_s5_xattn_moe_layer"

def rmsnorm(x, g):
    xf = x.astype(jnp.float32)
    y = xf * lax.rsqrt(jnp.mean(xf * xf, axis=-1, keepdims=True) + RMS_EPS)
    return (y * g.astype(jnp.float32)).astype(x.dtype)

def moba_attention(q, k, v):
    B, H, S, Dh = q.shape
    nb = -(-S // MOBA_BLOCK)
    sp = nb * MOBA_BLOCK
    pad = ((0, 0), (0, 0), (0, sp - S), (0, 0))
    q, k, v = jnp.pad(q, pad), jnp.pad(k, pad), jnp.pad(v, pad)
    kb = k.reshape(B, H, nb, MOBA_BLOCK, Dh)
    vb = v.reshape(B, H, nb, MOBA_BLOCK, Dh)
    kmean = jnp.mean(kb.astype(jnp.float32), axis=3)
    topk = min(MOBA_TOPK, nb)
    nc = sp // MOBA_QCHUNK
    qc = q.reshape(B, H, nc, MOBA_QCHUNK, Dh).transpose(2, 0, 1, 3, 4)
    scale = Dh ** -0.5
    gather_blocks = jax.vmap(jax.vmap(lambda blocks, idx: blocks[idx]))

    def chunk(args):
        qi, ci = args
        qf = qi.astype(jnp.float32)
        start = ci * MOBA_QCHUNK
        own = start // MOBA_BLOCK
        qpos = start + jnp.arange(MOBA_QCHUNK)
        gate = jnp.einsum('bhqd,bhnd->bhqn', qf, kmean)
        gate = jnp.where(jnp.arange(nb) < own, gate, NEG_INF)
        _, sel = lax.top_k(gate, topk)
        valid = sel < own
        ks = gather_blocks(kb, sel)
        vs = gather_blocks(vb, sel)
        s_sel = jnp.einsum('bhqd,bhqkjd->bhqkj', qf, ks.astype(jnp.float32)) * scale
        s_sel = jnp.where(valid[..., None], s_sel, NEG_INF).reshape(B, H, MOBA_QCHUNK, topk * MOBA_BLOCK)
        k_own = lax.dynamic_index_in_dim(kb, own, axis=2, keepdims=False)
        v_own = lax.dynamic_index_in_dim(vb, own, axis=2, keepdims=False)
        s_own = jnp.einsum('bhqd,bhjd->bhqj', qf, k_own.astype(jnp.float32)) * scale
        kpos = own * MOBA_BLOCK + jnp.arange(MOBA_BLOCK)
        s_own = jnp.where(kpos[None, :] <= qpos[:, None], s_own, NEG_INF)
        p = jax.nn.softmax(jnp.concatenate([s_sel, s_own], axis=-1), axis=-1)
        p_sel = p[..., :topk * MOBA_BLOCK].reshape(B, H, MOBA_QCHUNK, topk, MOBA_BLOCK)
        p_own = p[..., topk * MOBA_BLOCK:]
        out = (jnp.einsum('bhqkj,bhqkjd->bhqd', p_sel, vs.astype(jnp.float32))
               + jnp.einsum('bhqj,bhjd->bhqd', p_own, v_own.astype(jnp.float32)))
        return out.astype(q.dtype)

    outs = lax.map(chunk, (qc, jnp.arange(nc)))
    return outs.transpose(1, 2, 0, 3, 4).reshape(B, H, sp, Dh)[:, :, :S]

def s5_ssm(u, a_re, a_im, log_dt, b_re, b_im, c_re, c_im, d_skip):
    B, S, G, C = u.shape
    uf = u.astype(jnp.float32)
    lam = lax.complex(jnp.minimum(a_re.astype(jnp.float32), -1e-4), a_im.astype(jnp.float32))
    dt = jnp.exp(log_dt.astype(jnp.float32))[:, None]
    lam_bar = jnp.exp(lam * dt)
    b_c = lax.complex(b_re.astype(jnp.float32), b_im.astype(jnp.float32))
    c_c = lax.complex(c_re.astype(jnp.float32), c_im.astype(jnp.float32))
    b_bar = ((lam_bar - 1.0) / lam)[..., None] * b_c
    bu = jnp.einsum('gpc,bsgc->sbgp', b_bar, uf.astype(jnp.complex64))
    a = jnp.broadcast_to(lam_bar[None, None], (S, 1, G, SSM_STATE))

    def combine(left, right):
        a1, b1 = left
        a2, b2 = right
        return a1 * a2, a2 * b1 + b2

    _, xs = lax.associative_scan(combine, (a, bu), axis=0)
    y = jnp.einsum('gcp,sbgp->bsgc', c_c, xs).real + d_skip.astype(jnp.float32) * uf
    return y.astype(u.dtype)

def hybrid_mixer(h, g, w_in, a_re, a_im, log_dt, b_re, b_im, c_re, c_im, d_skip,
                 w_glu, w_proj_a, w_out):
    B, S, _ = h.shape
    n = rmsnorm(h, g)
    z = n @ w_in
    splits = [ATT_WIDTH, 2 * ATT_WIDTH, 3 * ATT_WIDTH, 3 * ATT_WIDTH + SSM_WIDTH,
              3 * ATT_WIDTH + SSM_WIDTH + D_MODEL]
    q, k, v, u, ga, gb = jnp.split(z, splits, axis=-1)
    to_heads = lambda t: t.reshape(B, S, ATT_HEADS, ATT_HEAD_DIM).transpose(0, 2, 1, 3)
    ya = moba_attention(to_heads(q), to_heads(k), to_heads(v))
    ya = ya.transpose(0, 2, 1, 3).reshape(B, S, ATT_WIDTH) @ w_proj_a
    yb = s5_ssm(u.reshape(B, S, SSM_GROUPS, SSM_GROUP), a_re, a_im, log_dt,
                b_re, b_im, c_re, c_im, d_skip).reshape(B, S, SSM_WIDTH)
    zb = jax.nn.gelu(yb) @ w_glu
    yb = zb[..., :D_MODEL] * jax.nn.sigmoid(zb[..., D_MODEL:])
    merged = jax.nn.sigmoid(ga) * ya + jax.nn.sigmoid(gb) * yb
    return merged @ w_out

def cross_attention(h, mem, g, g_mem, w_xq, w_xkv, w_xo):
    B, S, _ = h.shape
    M = mem.shape[1]
    n = rmsnorm(h, g)
    mn = rmsnorm(mem, g_mem)
    q = (n @ w_xq).reshape(B, S, XATTN_HEADS, XATTN_HEAD_DIM)
    kv = mn @ w_xkv
    k = kv[..., :XATTN_WIDTH].reshape(B, M, XATTN_HEADS, XATTN_HEAD_DIM)
    v = kv[..., XATTN_WIDTH:].reshape(B, M, XATTN_HEADS, XATTN_HEAD_DIM)
    s = jnp.einsum('bshd,bmhd->bhsm', q, k).astype(jnp.float32) * (XATTN_HEAD_DIM ** -0.5)
    p = jax.nn.softmax(s, axis=-1).astype(v.dtype)
    o = jnp.einsum('bhsm,bmhd->bshd', p, v).reshape(B, S, XATTN_WIDTH)
    return o @ w_xo

def moe_ffn(x2, w_router, b_router, w_gu, b_gu, w_dn, b_dn):
    T, D = x2.shape
    logits = (x2 @ w_router + b_router).astype(jnp.float32)
    top_v, top_i = lax.top_k(logits, EXPERT_TOPK)
    gates = jax.nn.softmax(top_v, axis=-1)
    N = T * EXPERT_TOPK
    e_flat = top_i.reshape(N)
    order = jnp.argsort(e_flat)
    e_sorted = e_flat[order]
    tok_sorted = order // EXPERT_TOPK
    gate_sorted = gates.reshape(N)[order]
    counts = jnp.bincount(e_flat, length=N_EXPERTS)
    starts = jnp.cumsum(counts) - counts
    padded = ((counts + MOE_BLOCK - 1) // MOE_BLOCK) * MOE_BLOCK
    pends = jnp.cumsum(padded)
    pstarts = pends - padded
    dest = pstarts[e_sorted] + jnp.arange(N) - starts[e_sorted]
    nblk = -(-N // MOE_BLOCK) + N_EXPERTS
    buf = jnp.zeros((nblk * MOE_BLOCK, D), x2.dtype).at[dest].set(x2[tok_sorted])
    blk_expert = jnp.clip(jnp.searchsorted(pends, jnp.arange(nblk) * MOE_BLOCK, side='right'),
                          0, N_EXPERTS - 1)

    def expert_block(args):
        xb, e = args
        gu = xb @ w_gu[e] + b_gu[e]
        gate = jnp.minimum(gu[:, :D_FF], SWIGLU_LIMIT)
        up = jnp.clip(gu[:, D_FF:], -SWIGLU_LIMIT, SWIGLU_LIMIT)
        hid = (up + 1.0) * gate * jax.nn.sigmoid(SWIGLU_ALPHA * gate)
        return hid @ w_dn[e] + b_dn[e]

    out = lax.map(expert_block, (buf.reshape(nblk, MOE_BLOCK, D), blk_expert)).reshape(nblk * MOE_BLOCK, D)
    y = out[dest] * gate_sorted.astype(out.dtype)[:, None]
    return jax.ops.segment_sum(y, tok_sorted, num_segments=T)

def setup_inputs(seed: int = 0) -> dict:
    key = jax.random.key(seed)
    ks = jax.random.split(key, 32)
    L = DEPTH
    f32 = jnp.float32
    nrm = lambda k, shape, scale: jax.random.normal(k, shape, f32) * scale
    gain = lambda k, shape: 1.0 + 0.02 * jax.random.normal(k, shape, f32)
    return {
        "x": nrm(ks[0], (BATCH, SEQ, D_MODEL), 1.0),
        "mem": nrm(ks[1], (BATCH, MEM_LEN, D_MODEL), 1.0),
        "g_mix": gain(ks[2], (L, D_MODEL)),
        "w_in": nrm(ks[3], (L, D_MODEL, IN_WIDTH), D_MODEL ** -0.5),
        "a_re": -0.5 + nrm(ks[4], (L, SSM_GROUPS, SSM_STATE), 0.01),
        "a_im": math.pi * jnp.arange(SSM_STATE, dtype=f32)[None, None, :]
                + nrm(ks[5], (L, SSM_GROUPS, SSM_STATE), 0.01),
        "log_dt": jax.random.uniform(ks[6], (L, SSM_GROUPS), f32, math.log(1e-3), math.log(1e-1)),
        "b_re": nrm(ks[7], (L, SSM_GROUPS, SSM_STATE, SSM_GROUP), (2 * SSM_GROUP) ** -0.5),
        "b_im": nrm(ks[8], (L, SSM_GROUPS, SSM_STATE, SSM_GROUP), (2 * SSM_GROUP) ** -0.5),
        "c_re": nrm(ks[9], (L, SSM_GROUPS, SSM_GROUP, SSM_STATE), (2 * SSM_STATE) ** -0.5),
        "c_im": nrm(ks[10], (L, SSM_GROUPS, SSM_GROUP, SSM_STATE), (2 * SSM_STATE) ** -0.5),
        "d_skip": nrm(ks[11], (L, SSM_GROUPS, SSM_GROUP), 1.0),
        "w_glu": nrm(ks[12], (L, SSM_WIDTH, 2 * D_MODEL), SSM_WIDTH ** -0.5),
        "w_proj_a": nrm(ks[13], (L, ATT_WIDTH, D_MODEL), ATT_WIDTH ** -0.5),
        "w_out": nrm(ks[14], (L, D_MODEL, D_MODEL), D_MODEL ** -0.5),
        "g_xattn": gain(ks[15], (L, D_MODEL)),
        "g_mem": gain(ks[16], (L, D_MODEL)),
        "w_xq": nrm(ks[17], (L, D_MODEL, XATTN_WIDTH), D_MODEL ** -0.5),
        "w_xkv": nrm(ks[18], (L, D_MODEL, 2 * XATTN_WIDTH), D_MODEL ** -0.5),
        "w_xo": nrm(ks[19], (L, XATTN_WIDTH, D_MODEL), XATTN_WIDTH ** -0.5),
        "g_moe": gain(ks[20], (L, D_MODEL)),
        "w_router": nrm(ks[21], (L, D_MODEL, N_EXPERTS), D_MODEL ** -0.5),
        "b_router": nrm(ks[22], (L, N_EXPERTS), 0.01),
        "w_gu": nrm(ks[23], (L, N_EXPERTS, D_MODEL, 2 * D_FF), D_MODEL ** -0.5),
        "b_gu": nrm(ks[24], (L, N_EXPERTS, 2 * D_FF), 0.01),
        "w_dn": nrm(ks[25], (L, N_EXPERTS, D_FF, D_MODEL), D_FF ** -0.5),
        "b_dn": nrm(ks[26], (L, N_EXPERTS, D_MODEL), 0.01),
        "g_final": gain(ks[27], (D_MODEL,)),
    }

def reference(x, mem, g_mix, w_in, a_re, a_im, log_dt, b_re, b_im, c_re, c_im, d_skip,
              w_glu, w_proj_a, w_out, g_xattn, g_mem, w_xq, w_xkv, w_xo,
              g_moe, w_router, b_router, w_gu, b_gu, w_dn, b_dn, g_final):
    h = x
    for l in range(DEPTH):
        h = h + hybrid_mixer(h, g_mix[l], w_in[l], a_re[l], a_im[l], log_dt[l], b_re[l], b_im[l],
                             c_re[l], c_im[l], d_skip[l], w_glu[l], w_proj_a[l], w_out[l])
        h = h + cross_attention(h, mem, g_xattn[l], g_mem[l], w_xq[l], w_xkv[l], w_xo[l])
        n = rmsnorm(h, g_moe[l]).reshape(-1, D_MODEL)
        h = h + moe_ffn(n, w_router[l], b_router[l], w_gu[l], b_gu[l], w_dn[l], b_dn[l]).reshape(h.shape)
    return rmsnorm(h, g_final)


_drawn_inputs = setup_inputs


def setup_inputs(seed=0):
    import zlib

    import numpy as np

    out = dict(_drawn_inputs(seed))
    spreads = {}
    factors = {'g_mix': 2.851,
     'a_re': 64.0,
     'c_im': 4.448,
     'g_xattn': 8.0,
     'g_mem': 4.612,
     'b_gu': 44.001,
     'b_dn': 50.538,
     'g_final': 9.724,
     'g_moe': 5.639,
     'b_router': 8.0}
    for name, (base, spread) in spreads.items():
        noise = np.random.default_rng([zlib.crc32(name.encode()), seed]).standard_normal(out[name].shape)
        drawn = base * np.exp(spread * noise) if base else spread * noise
        out[name] = __import__('jax').numpy.asarray(drawn.astype(out[name].dtype))
    for name, factor in factors.items():
        out[name] = (out[name] * factor).astype(out[name].dtype)
    return out
```

```python
from contextlib import ExitStack

import concourse.bass as bass
from concourse import mybir

F32 = mybir.dt.float32
I32 = mybir.dt.int32
U32 = mybir.dt.uint32
ALU = mybir.AluOpType
ACT = mybir.ActivationFunctionType
AX = mybir.AxisListType.X

P = 128
D = 1024
S = 256
TT = S // P
KD = D // P
HEADS, DH = 8, 64
XH, XDH = 4, 128
G, NS, GC = 32, 64, 16
PAIRS = G // 2
QG = 4
E, TOPK, FF = 32, 4, 1024
SLOTS = 64
ROUNDS = S // SLOTS
HALF = 512
EPS = 1e-6
NEG = -1e30
LIMIT, ALPHA = 7.0, 1.702
ROUND = 12582912.0
TWO_PI = 6.2831850
OFF = 16384.0
FW = 6
SLOT = 2048
STEPS = PAIRS + 4
MM = 4

R_ARE, R_LDT, R_DSK, R_AIM, R_GAIN = 0, 32, 48, 64, 80
N_ROWS = R_GAIN + 4 * KD


def dense_weights():
    order = [("w_in", "cols", 1536 + 256 * i) for i in range(2)]
    order += [("w_in", "cols", 256 * i) for i in range(6)]
    order += [("w_in", "cols", 2048 + 256 * i) for i in range(8)]
    order += [("w_proj_a", "wide", 512 * i) for i in range(2)]
    order += [("w_glu", "wide", c) for c in (0, 1024, 512, 1536)]
    order += [("w_xkv", "cols", 256 * i) for i in range(4)]
    order += [("w_out", "rows", 2 * i) for i in range(4)]
    order += [("w_xq", "cols", 256 * i) for i in range(2)]
    order += [("w_xo", "rows", 2 * i) for i in range(2)]
    return order


def units():
    out = [(("rows",), "dve")] + [(("nT", k), "dve") for k in range(4)]
    out += [(("Bd", 0), "dve"), (("Bd", 1), "dve"), (("C", 0), "dve"), (("C", 1), "dve")]
    out += [(("u", c), "act") for c in range(4)]
    out += [(("q", c), "act") for c in range(4)] + [(("k", c), "act") for c in range(4)]
    out += [(("v", hf, t), "act") for hf in range(2) for t in range(TT)]
    for j in range(STEPS):
        if j % 2 == 0 and j < PAIRS:
            out.append((("S", j // 2), "dve"))
        if j % 2 == 0 and 2 <= j <= PAIRS:
            out.append((("T", j // 2 - 1), "act"))
        if j % 2 == 1 and 3 <= j <= PAIRS + 1:
            out.append((("O", (j - 3) // 2), "act"))
        if j < PAIRS:
            out.append((("z", j), "act"))
    out += [(("ya", c), "dve") for c in range(KD)]
    out += [((w, c), e) for c in range(KD) for w, e in (("zb", "dve"), ("zg", "act"))]
    out += [(("memT", k), "dve") for k in range(4)]
    out += [(("xk", c), "act") for c in range(4)] + [(("xv", hf, t), "act") for hf in range(2) for t in range(TT)]
    out += [(("out", t, hf), "dve") for t in range(TT) for hf in range(2)]
    out += [(("n2T", k), "dve") for k in range(4)] + [(("xq", c), "act") for c in range(4)]
    out += [(("XS", 0), "act"), (("XS", 1), "act")]
    for h in range(XH):
        out += [(("XT", h), "act"), (("XO", h), "act")]
        if h + 2 < XH:
            out.append((("XS", h + 2), "act"))
    out += [(("xo", t, hf), "dve") for t in range(TT) for hf in range(2)]
    out += [(("n3T", k), "dve") for k in range(4)]
    out += [(("logits",), "dve"), (("pos",), "dve"), (("GT",), "dve")]
    return out


def build_layer(nc, x, mem, g_mix, w_in, a_re, a_im, log_dt, b_re, b_im, c_re, c_im, d_skip, w_glu, w_proj_a,
                w_out, g_xattn, g_mem, w_xq, w_xkv, w_xo, g_moe, w_router, b_router, w_gu, b_gu, w_dn, b_dn,
                g_final, out):
    weights = dict(w_in=w_in[0], w_xkv=w_xkv[0], w_proj_a=w_proj_a[0], w_glu=w_glu[0], w_out=w_out[0],
                   w_xq=w_xq[0], w_xo=w_xo[0])
    order = dense_weights()
    plan = units()
    number = {u: n for n, (u, _) in enumerate(plan)}
    reader = dict(plan)
    rank = {u: sum(e == reader[u] for _, e in plan[:number[u]]) for u, _ in plan}
    last_user = [(n, c) for n in ("u", "q", "k") for c in (1, 3)] + [("v", hf, 1) for hf in range(2)]
    last_user += [("z", c) for c in range(1, PAIRS, 2)]
    last_user += [("ya", 3), ("ya", 7), ("zb", 3), ("zg", 3), ("zb", 7), ("zg", 7)]
    last_user += [("xk", 1), ("xk", 3), ("xv", 0, 1), ("xv", 1, 1)]
    last_user += [None, None, None, ("out", 1, 1), ("xq", 1), ("xq", 3), None, ("xo", 1, 1)]

    with ExitStack() as ctx:
        sem_names = {}

        def sem(name):
            sem_names[name] = ctx.enter_context(nc.semaphore(name))
            return sem_names[name]

        words = {}
        top = [0]
        total = 53110
        arena = ctx.enter_context(nc.sbuf_tensor("arena", [P, total], F32))

        def at(start, n):
            return arena[:, start:start + n]

        def take(n):
            top[0] += n
            assert top[0] <= total, top[0]
            return top[0] - n

        ring0 = take(KD * 2 * FF + (FF // P) * D)
        gu_ring = [at(ring0 + k * 2 * FF, 2 * FF) for k in range(KD)]
        dn_ring = [at(ring0 + KD * 2 * FF + k * D, D) for k in range(FF // P)]
        a0 = ring0
        turns = at(a0, PAIRS * 512).rearrange("p (j c s) -> p j c s", j=PAIRS, c=2)
        a0 += PAIRS * 512
        p_base = a0
        prod = at(a0, 4096).rearrange("p (b w c s) -> p b w c s", b=4, w=2, c=2)
        a0 += 4096
        gate_base = a0
        gates = at(a0, 4096).rearrange("p (c s) -> p c s", c=16)
        a0 += 4096
        qT = at(a0, 1024).rearrange("p (c s) -> p c s", c=4)
        kT = at(a0 + 1024, 1024).rearrange("p (c s) -> p c s", c=4)
        v_sb = at(a0 + 2048, 1024).rearrange("p (t n) -> p t n", t=TT)
        uT = at(a0 + 3072, 1024).rearrange("p (c s) -> p c s", c=4)
        a0 += 4096
        m_cos = at(a0, 512).rearrange("p (c s) -> p c s", c=2)
        m_sin = at(a0 + 512, 512).rearrange("p (c s) -> p c s", c=2)
        drive = at(a0 + 1024, 512).rearrange("p (c s) -> p c s", c=2)
        state = at(a0 + 1536, 1024).rearrange("p (b c s) -> p b c s", b=2, c=2)
        a0 += 3072
        Bd = at(a0, 1024).rearrange("p (w q m) -> p w q m", w=2, q=QG)
        a0 += 1024
        assert a0 <= ring0 + 24576
        b_raw = at(p_base, 1024).rearrange("p (w j c) -> p w j c", w=2, j=PAIRS)
        b_bar = at(p_base + 1024, 1024).rearrange("p (w j c) -> p w j c", w=2, j=PAIRS)
        c_raw = at(p_base + 2048, 1024).rearrange("p (w q m) -> p w q m", w=2, q=QG)
        b_tmp = at(p_base + 3072, 1024).rearrange("p (w j c) -> p w j c", w=2, j=PAIRS)
        g1 = gate_base + 9 * 256
        turn_a = at(g1, 512).rearrange("p (j c a) -> p j c a", j=PAIRS, c=2)
        turn_b = at(g1 + 512, 256).rearrange("p (j b) -> p j b", j=PAIRS)
        phase = at(g1 + 768, 512)
        whole = at(g1 + 1280, 512)

        front0 = take(FW * SLOT)
        front = [at(front0 + s * SLOT, SLOT) for s in range(FW)]
        h_base = take(TT * D)
        h = at(h_base, TT * D).rearrange("p (t n) -> p t n", t=TT)
        xn = at(take(TT * D), TT * D).rearrange("p (t n) -> p t n", t=TT)
        nT = at(take(KD * S), KD * S).rearrange("p (k s) -> p k s", k=KD)
        attnT = at(take(4 * S), 4 * S).rearrange("p (c s) -> p c s", c=4)
        kx_base = take(4 * S)
        kxT = at(kx_base, 4 * S).rearrange("p (c s) -> p c s", c=4)
        geluT = at(kx_base, 4 * S).rearrange("p (c s) -> p c s", c=4)
        vx = at(take(TT * 512), TT * 512).rearrange("p (t n) -> p t n", t=TT)
        merged_base = take(KD * S)
        mergedT = at(merged_base, KD * S).rearrange("p (k s) -> p k s", k=KD)
        junk = at(merged_base, TT * D).rearrange("p (t n) -> p t n", t=TT)
        xp = at(merged_base, 1024).rearrange("p (b t s) -> p b t s", b=2, t=TT)
        xpT = at(merged_base + 1024, 1024).rearrange("p (b m s) -> p b m s", b=2, m=TT)
        gfin = at(merged_base, D)
        ct_base = take(3 * PAIRS * 32)
        Ct = at(ct_base, 3 * PAIRS * 32).rearrange("p (w j m) -> p w j m", w=3, j=PAIRS)
        router = at(ct_base, KD * E).rearrange("p (k e) -> p k e", k=KD)
        bdn = at(ct_base + 256, D)
        ident = at(take(P), P)
        ones = at(take(P), P)
        tri = at(take(P), P)
        mask = at(take(384), 384)
        sc = at(take(768), 768).rearrange("p (b n) -> p b n", b=2)
        scT = at(take(384), 384)
        yskip = at(take(S), S)
        gtmp = at(take(S), S)
        cols = at(take(N_ROWS), N_ROWS)
        rows_base = take(P)
        rows = at(rows_base, P)
        ldt = at(take(2), 2)
        par = at(take(14 * 16), 14 * 16).rearrange("p (n j) -> p n j", n=14)
        iota16 = at(take(16), 16)
        slot_no = at(take(2 * SLOTS), 2 * SLOTS)
        exp_no = at(rows_base, E)
        stat = at(take(64), 64)
        logit = at(take(2 * E), 2 * E).rearrange("p (t e) -> p t e", t=TT)
        chosen = at(take(2 * E), 2 * E).rearrange("p (t e) -> p t e", t=TT)
        gate_w = at(take(2 * 33), 2 * 33).rearrange("p (t e) -> p t e", t=TT)
        pos = at(take(2 * 33), 2 * 33).rearrange("p (t e) -> p t e", t=TT)
        top8 = at(take(16), 16).rearrange("p (t e) -> p t e", t=TT)
        topi = ctx.enter_context(nc.sbuf_tensor("topi", [P, TT, 8], U32))
        topf = at(take(16), 16).rearrange("p (t e) -> p t e", t=TT)
        brt = at(take(E), E)
        rounds_i = ctx.enter_context(nc.sbuf_tensor("rounds_i", [P, 1], I32))
        f0 = [front0]

        def moe(n):
            f0[0] += n
            assert f0[0] <= front0 + FW * SLOT
            return at(f0[0] - n, n)

        xeT = [moe(KD * SLOTS).rearrange("p (k s) -> p k s", k=KD) for _ in range(2)]
        pick = [moe(TT * SLOTS).rearrange("p (t s) -> p t s", t=TT) for _ in range(2)]
        spread = [moe(TT * 2 * SLOTS).rearrange("p (t s) -> p t s", t=TT) for _ in range(2)]
        spreadT = [moe(TT * P).rearrange("p (t s) -> p t s", t=TT) for _ in range(2)]
        gate_c, up_c, gate_t, gated, hid = [moe(HALF) for _ in range(5)]
        hidT = moe(HALF).rearrange("p (b s) -> p b s", b=4)
        y_sb = [moe(HALF) for _ in range(2)]
        bias_row = moe(2 * FF)
        GT = moe(S)

        psum = ctx.enter_context(nc.psum_tensor("psum", [P, 8, HALF], F32))
        BU, Y, DN = 4, 6, 7

        x_in, mem_in, rows_in, b_in, c_in = sem("x_in"), sem("mem_in"), sem("rows_in"), sem("b_in"), sem("c_in")
        w_in_s = [sem(f"weights_in{s}") for s in range(FW)]
        router_in, gfin_in = sem("router_in"), sem("gfin_in")
        consts = sem("consts")
        ldt_rows = sem("ldt_rows")
        cleared = sem("cleared")
        rows_used = sem("rows_used")
        mm = sem("mm")
        unit_read = {"dve": sem("dve_read"), "act": sem("act_read")}
        sq = sem("sq")
        ms = sem("ms")
        rstd_s = sem("rstd_s")
        xn_s = sem("xn_s")
        par_s = sem("par_s")
        apar_s = sem("apar_s")
        bbar_s = sem("bbar_s")
        ang_s = sem("ang_s")
        turn_s = sem("turn_s")
        bu_s, bu_read = sem("bu_s"), sem("bu_read")
        state_s, prod_s = sem("state_s"), sem("prod_s")
        y_s, y_read = sem("y_s"), sem("y_read")
        gl1, gl2, gl3, gelu_s = sem("gl1"), sem("gl2"), sem("gl3"), sem("gelu_s")
        smax_s, exp_s, prob_s = sem("smax_s"), sem("exp_s"), sem("prob_s")
        merged_s = sem("merged_s")
        h_s = sem("h_s")
        xmax_s, xprob_s = sem("xmax_s"), sem("xprob_s")
        rt1, rt2, chosen_s, rounds_s, GT_s = sem("rt1"), sem("rt2"), sem("chosen_s"), sem("rounds_s"), sem("GT_s")
        gu_in = [sem(f"gu_in{k}") for k in range(KD)]
        dn_in = [sem(f"dn_in{k}") for k in range(FF // P)]
        bias_in = sem("bias_in")
        bias_used, gu_used, dn_used = sem("bias_used"), sem("gu_used"), sem("dn_used")
        pick_s, gather_s, xe_s = sem("pick_s"), sem("gather_s"), sem("xe_s")
        gu_read, gate_cs, tanh_s, hid_s = sem("gu_read"), sem("gate_cs"), sem("tanh_s"), sem("hid_s")
        hidT_ps, hidT_s, spT_ps, spT_s, y_ready = sem("hidT_ps"), sem("hidT_s"), sem("spT_ps"), sem("spT_s"), sem("y_ready")
        acc_s, outd, outn = sem("acc_s"), sem("outd"), sem("outn")
        y_zero = sem("y_zero")

        block = ctx.enter_context(nc.Block())

        def bank_of(u):
            return number[u] % MM

        def arrived(eng, n):
            eng.wait_ge(w_in_s[n % FW], 16 * (n // FW + 1))

        def ready(eng, u):
            eng.wait_ge(mm, number[u] + 1)

        def evacuated(eng, u):
            eng.wait_ge(unit_read[reader[u]], rank[u] + 1)

        def later_rounds(eng, body):
            eng.wait_ge(rounds_s, 1)
            n = eng.value_load(rounds_i[0:1, 0:1], min_val=1, max_val=ROUNDS)
            with eng.Fori(1, ROUNDS) as r:
                with eng.If(n > r):
                    body(r)
            return n

        def expert_loads(sp, i, e, first):
            gu = w_gu[0].rearrange("e (k p) n -> (e k) p n", p=P)
            dn = w_dn[0].rearrange("e (k p) n -> (e k) p n", p=P)
            if not first:
                sp.wait_ge(bias_used, i)
                sp.dma_start(bias_row[0:1, :], b_gu[0, bass.ds(e, 1), :]).then_inc(bias_in, 16)
            for k in range(KD):
                if first:
                    sp.dma_start(gu_ring[k], gu[k]).then_inc(gu_in[k], 16)
                else:
                    sp.wait_ge(gu_used, (i - 1) * KD + k + 1)
                    sp.dma_start(gu_ring[k], gu[bass.ds(e * KD + k, 1)].rearrange("a p n -> p (a n)")).then_inc(gu_in[k], 16)
            for k in range(FF // P):
                if first:
                    sp.dma_start(dn_ring[k], dn[k]).then_inc(dn_in[k], 16)
                else:
                    sp.wait_ge(dn_used, (i - 1) * (FF // P) + k + 1)
                    sp.dma_start(dn_ring[k], dn[bass.ds(e * (FF // P) + k, 1)].rearrange("a p n -> p (a n)")).then_inc(dn_in[k], 16)

        @block.sync
        def _(sp):
            sp.dma_start(h[:, 0, :], x[0, 0:P, :]).then_inc(x_in, 16)
            sp.dma_start(h[:, 1, :], x[0, P:S, :]).then_inc(x_in, 16)

            def load(n):
                name, cut, c = order[n]
                if n >= FW:
                    if last_user[n - FW] is None:
                        sp.wait_ge(rows_used, last_user[:n - FW + 1].count(None))
                    else:
                        ready(sp, last_user[n - FW])
                w, dst = weights[name], front[n % FW]
                if cut == "rows":
                    sp.dma_start(dst.rearrange("p (k n) -> p k n", k=2),
                                 w.rearrange("(k p) n -> p k n", p=P)[:, c:c + 2, :]).then_inc(w_in_s[n % FW], 16)
                else:
                    k = 8 if cut == "cols" else 4
                    sp.dma_start(dst.rearrange("p (k n) -> p k n", k=k),
                                 w.rearrange("(k p) n -> p k n", p=P)[:, :, c:c + SLOT // k]).then_inc(w_in_s[n % FW], 16)

            for n in range(FW):
                load(n)
            sp.wait_ge(mm, number[("nT", 3)] + 1)
            for t in range(TT):
                sp.dma_start(xn[:, t, :], mem[0, t * P:(t + 1) * P, :]).then_inc(mem_in, 16)
            for n in range(FW, len(order)):
                load(n)
            sp.wait_ge(merged_s, KD)
            expert_loads(sp, 0, 0, True)
            sp.dma_start(router, w_router[0].rearrange("(k p) e -> p k e", p=P)).then_inc(router_in, 16)
            sp.dma_start(bdn[0:E, :], b_dn[0]).then_inc(router_in, 16)
            sp.dma_start(brt[0:1, :], b_router).then_inc(router_in, 16)
            ready(sp, ("xo", TT - 1, 1))
            sp.dma_start(bias_row[0:1, :], b_gu[0, 0:1, :]).then_inc(bias_in, 16)
            sp.dma_start(gfin, g_final.partition_broadcast(P)).then_inc(gfin_in, 16)
            with sp.Fori(1, E) as e:
                expert_loads(sp, e, e, False)

            def again(r):
                with sp.Fori(0, E) as e:
                    expert_loads(sp, r * E + e, e, False)

            later_rounds(sp, again)
            sp.wait_ge(outd, 1)
            sp.dma_start(out[0, 0:P, :], h[:, 0, :]).then_inc(outn, 16)
            sp.wait_ge(outd, 2)
            sp.dma_start(out[0, P:S, :], h[:, 1, :]).then_inc(outn, 16)
            sp.wait_ge(outn, 32)

        @block.gpsimd
        def _(pool):
            gp = nc.gpsimd
            gp.memset(rows, 0.0)
            gp.memset(at(p_base, 1024), 0.0).then_inc(cleared, 1)
            gp.memset(ident, 0.0)
            gp.memset(ones, 1.0)
            gp.memset(mask, 0.0)
            gp.memset(at(ct_base, 3 * PAIRS * 32), 0.0)
            gp.memset(stat, 0.0)
            gp.iota(iota16, [[1, 16]], base=0, channel_multiplier=0, allow_small_or_imprecise_dtypes=True)
            gp.iota(slot_no, [[0, 2], [1, SLOTS]], base=0, channel_multiplier=0, allow_small_or_imprecise_dtypes=True)
            pool.drain()
            gp.memset(stat[:, 32:34], -0.5)
            gp.affine_select(out=ident, in_=ident, compare_op=ALU.not_equal, fill=1.0, base=0,
                             pattern=[[-1, P]], channel_multiplier=1)
            gp.affine_select(out=tri, in_=ones, compare_op=ALU.is_gt, fill=0.0, base=0,
                             pattern=[[1, P]], channel_multiplier=-1)
            for c in (0, 256):
                gp.affine_select(out=mask[:, c:c + P], in_=mask[:, c:c + P], compare_op=ALU.is_ge, fill=NEG, base=0,
                                 pattern=[[-1, P]], channel_multiplier=1)
            pool.drain()
            gp.memset(stat[:, 34:35], 0.0).then_inc(consts, 1)

            def root(n):
                pool.wait_ge(ms, n)
                gp.tensor_tensor(stat[:, 4:6], stat[:, 2:4], stat[:, 32:34], ALU.pow).then_inc(rstd_s, 1)

            root(1)
            pool.wait_ge(par_s, 3)
            for j in range(PAIRS):
                if j:
                    pool.wait_ge(ang_s, j)
                ph = phase.rearrange("p (c a b) -> p c a b", c=2, a=16)
                for c in range(2):
                    gp.tensor_tensor(ph[:, c], turn_a[:, j, c, :].unsqueeze(2).broadcast_to((P, 16, 16)),
                                     turn_b[:, j, :].unsqueeze(1).broadcast_to((P, 16, 16)), ALU.add)
                pool.drain()
                gp.tensor_scalar(whole, phase, ROUND, ROUND, ALU.add, ALU.subtract)
                pool.drain()
                gp.tensor_tensor(turns[:, j].rearrange("p c s -> p (c s)"), phase, whole, ALU.subtract).then_inc(ang_s, 1)
                if j == 6:
                    root(2)
            for j in range(PAIRS):
                pool.wait_ge(state_s, j + 1)
                pool.wait_ge(turn_s, PAIRS)
                if j >= 4:
                    pool.wait_ge(y_s, j // 4)
                else:
                    evacuated(pool, ("C", 1))
                for w in range(2):
                    last = gp.tensor_tensor(prod[:, j % 4, w], state[:, j % 2],
                                            turns[:, j, w, :].unsqueeze(1).broadcast_to((P, 2, S)), ALU.mult)
                last.then_inc(prod_s, 1)
            gp.iota(exp_no, [[1, E]], base=0, channel_multiplier=0, allow_small_or_imprecise_dtypes=True)
            root(3)
            root(4)
            pool.drain()
            gp.memset(stat[:, 35:36], 0.0).then_inc(consts, 1)
            root(5)

        @block.scalar
        def _(act):
            sa = nc.scalar
            act.wait_ge(cleared, 1)
            for r, src in ((R_ARE, a_re[0].rearrange("(j two) p -> j two p", two=2)),
                           (R_AIM, a_im[0].rearrange("(j two) p -> j two p", two=2))):
                act.dma_start(rows[r:r + PAIRS, :].rearrange("j (two p) -> j two p", two=2), src).then_inc(rows_in, 16)
            act.dma_start(ldt[R_LDT:R_LDT + PAIRS, :], log_dt[0].rearrange("(j two) -> j two", two=2)).then_inc(rows_in, 16)
            for i, g in enumerate((g_mix, g_xattn, g_mem, g_moe)):
                act.dma_start(rows[R_GAIN + i * KD:R_GAIN + (i + 1) * KD, :], g[0].rearrange("(k p) -> k p", p=P)).then_inc(rows_in, 16)
            act.dma_start(rows[R_DSK:R_DSK + QG, :].rearrange("q (g c) -> q g c", c=GC),
                          d_skip[0].rearrange("(q g) c -> q g c", q=QG)).then_inc(rows_in, 16)
            for w, b in enumerate((b_re, b_im)):
                for two in range(2):
                    act.dma_start(b_raw[two * NS:(two + 1) * NS, w, :, two * GC:(two + 1) * GC],
                                  b[0].rearrange("(j two) p c -> two p j c", two=2)[two]).then_inc(b_in, 16)
            for w, c in enumerate((c_re, c_im)):
                for dup in range(2):
                    act.dma_start(c_raw[:, w, :, dup * NS:(dup + 1) * NS],
                                  c[0].rearrange("(q g) c p -> (g c) q p", q=QG)).then_inc(c_in, 16)

            def squares(n, src, scratch):
                for t in range(TT):
                    last = sa.activation(scratch[:, t, :], src[:, t, :], ACT.Square, accum_out=stat[:, t:t + 1])
                last.then_inc(sq, 1)

            act.wait_ge(x_in, 32)
            act.wait_ge(consts, 1)
            squares(1, h, junk)

            def evacuate(u, dst, scale=1.0, func=ACT.Copy, part=slice(0, P)):
                ready(act, u)
                sa.activation(dst, psum[part, bank_of(u), 0:dst.free_size()], func, scale=scale).then_inc(unit_read["act"], 1)

            act.wait_ge(par_s, 1)
            sa.activation(par[:, 3], cols[:, R_LDT:R_LDT + 16], ACT.Tanh, scale=1.0 / 16).then_inc(apar_s, 1)
            act.wait_ge(par_s, 2)
            sa.activation(par[:, 5], par[:, 4], ACT.Tanh, scale=0.5).then_inc(apar_s, 1)
            act.wait_ge(par_s, 3)
            for w in range(2):
                last = sa.activation(par[:, 8 + w], par[:, 6 + w], ACT.Sin, scale=TWO_PI)
            sa.activation(par[:, 10], par[:, 13], ACT.Sin, scale=TWO_PI / 2).then_inc(apar_s, 1)
            for j in range(PAIRS):
                act.wait_ge(ang_s, j + 1)
                t = turns[:, j].rearrange("p c s -> p (c s)")
                sa.activation(t, t, ACT.Sin, scale=TWO_PI).then_inc(turn_s, 1)
                if j == 4:
                    act.wait_ge(mem_in, 32)
                    squares(2, xn, junk)
            for c in range(4):
                evacuate(("u", c), uT[:, c, :])
            for c in range(4):
                evacuate(("q", c), qT[:, c, :])
            for c in range(4):
                evacuate(("k", c), kT[:, c, :])
            for hf in range(2):
                for t in range(TT):
                    evacuate(("v", hf, t), v_sb[:, t, hf * 256:(hf + 1) * 256])

            def exps(hd):
                act.wait_ge(smax_s, hd + 1)
                b = sc[:, hd % 2]
                sa.activation(b[:, 0:P], b[:, 0:P], ACT.Exp, bias=stat[:, 12:13] if hd % 2 == 0 else stat[:, 14:15],
                              accum_out=stat[:, 16 + 2 * (hd % 2):17 + 2 * (hd % 2)])
                sa.activation(b[:, P:384], b[:, P:384], ACT.Exp, bias=stat[:, 13:14] if hd % 2 == 0 else stat[:, 15:16],
                              accum_out=stat[:, 17 + 2 * (hd % 2):18 + 2 * (hd % 2)]).then_inc(exp_s, 1)

            def gelu_act(q):
                act.wait_ge(gl1, q + 1)
                sa.activation(gtmp, yskip, ACT.Square).then_inc(gl2, 1)
                act.wait_ge(gl3, q + 1)
                sa.activation(gtmp, gtmp, ACT.Tanh, scale=0.7978845608028654).then_inc(gl2, 1)

            for j in range(STEPS):
                if j % 2 == 0 and j < PAIRS:
                    exps(j // 2)
                if j % 2 == 0 and 2 <= j <= PAIRS:
                    hd = j // 2 - 1
                    if hd:
                        ready(act, ("O", hd - 1))
                    evacuate(("T", hd), scT)
                if j % 2 == 1 and 3 <= j <= PAIRS + 1:
                    hd = (j - 3) // 2
                    part = slice(DH * (hd % 2), DH * (hd % 2) + DH)
                    evacuate(("O", hd), attnT[part, hd // 2, :], part=part)
                if j < PAIRS:
                    evacuate(("z", j), gates[:, j, :], scale=0.5, func=ACT.Tanh)
                if j % 4 == 3 and j >= 7:
                    gelu_act((j - 7) // 4)
            for c in range(KD):
                if c >= 2:
                    act.wait_ge(merged_s, c - 1)
                evacuate(("zg", c), sc[:, c % 2, 0:S], scale=0.25, func=ACT.Tanh)
            for c in range(4):
                evacuate(("xk", c), kxT[:, c, :])
            for hf in range(2):
                for t in range(TT):
                    evacuate(("xv", hf, t), vx[:, t, hf * 256:(hf + 1) * 256])
            evacuated(act, ("out", 1, 1))
            squares(3, h, xn)
            for c in range(4):
                evacuate(("xq", c), attnT[:, c, :])

            def xexps(hd):
                u = ("XS", hd)
                act.wait_ge(xmax_s, hd + 1)
                if hd >= 2:
                    act.wait_ge(mm, number[("XT", hd - 2)] + 1)
                for t in range(TT):
                    last = sa.activation(xp[:, hd % 2, t, :], psum[:, bank_of(u), t * 256:(t + 1) * 256], ACT.Exp,
                                  scale=XDH ** -0.5, bias=stat[:, 20 + 2 * (hd % 2) + t:21 + 2 * (hd % 2) + t],
                                  accum_out=stat[:, 24 + 2 * (hd % 2) + t:25 + 2 * (hd % 2) + t])
                last.then_inc(unit_read["act"], 1)

            xexps(0)
            xexps(1)
            for hd in range(XH):
                if hd >= 2:
                    act.wait_ge(mm, number[("XO", hd - 2)] + 1)
                evacuate(("XT", hd), xpT[:, hd % 2].rearrange("p m s -> p (m s)"))
                evacuate(("XO", hd), attnT[:, hd, :])
                if hd + 2 < XH:
                    xexps(hd + 2)
            evacuated(act, ("xo", 1, 1))
            squares(4, h, xn)
            act.wait_ge(rt1, 1)
            for t in range(TT):
                last = sa.activation(gate_w[:, t, 0:E], logit[:, t, :], ACT.Exp, bias=stat[:, 36 + t:37 + t])
            last.then_inc(rt2, 1)
            act.wait_ge(y_zero, 1)
            sa.activation(stat[:, 40:41], stat[:, 34:35], ACT.Copy).then_inc(y_ready, 1)

            def expert(i, b):
                act.wait_ge(gate_cs, i + 1)
                sa.activation(gate_t, gate_c, ACT.Tanh, scale=ALPHA / 2).then_inc(tanh_s, 1)
                act.wait_ge(hidT_ps, i + 1)
                sa.activation(hidT.rearrange("p b s -> p (b s)"), psum[:, DN, :], ACT.Copy, scale=0.5).then_inc(hidT_s, 1)
                act.wait_ge(spT_ps, i + 1)
                sa.activation(spreadT[b].rearrange("p t s -> p (t s)"), psum[:, 6, 0:TT * P], ACT.Copy).then_inc(spT_s, 1)
                act.wait_ge(dn_used, (i + 1) * KD)
                sa.activation(y_sb[b], psum[:, DN, :], ACT.Copy).then_inc(y_ready, 1)

            def sweep(r):
                with act.Fori(0, E // 2) as e2:
                    for b in range(2):
                        expert(r * E + e2 * 2 + b, b)

            sweep(0)
            later_rounds(act, sweep)
            act.wait_ge(h_s, 1)
            squares(5, h, xn)

        @block.vector
        def _(dve):
            ve = nc.vector
            fence = dve.drain

            read = unit_read["dve"]

            def mean_square(n):
                dve.wait_ge(sq, n)
                ve.tensor_scalar(stat[:, 2:4], stat[:, 0:2], 1.0 / D, EPS, ALU.mult, ALU.add).then_inc(ms, 1)

            def normalise(n, src):
                dve.wait_ge(rstd_s, n)
                for t in range(TT):
                    ve.tensor_scalar(xn[:, t, :], src[:, t, :], stat[:, 4 + t:5 + t], None, ALU.mult).then_inc(xn_s, 1)

            def transposed(name, g):
                for kp in range(4):
                    u = (name, kp)
                    ready(dve, u)
                    gain = cols[:, R_GAIN + g * KD + 2 * kp:R_GAIN + g * KD + 2 * kp + 2].unsqueeze(2).broadcast_to((P, 2, S))
                    ve.tensor_tensor(nT[:, 2 * kp:2 * kp + 2, :], psum[:, bank_of(u), :].rearrange("p (k s) -> p k s", k=2),
                                     gain, ALU.mult).then_inc(read, 1)

            dve.wait_ge(cleared, 1)
            dve.wait_ge(rows_in, 8 * 16)
            dve.wait_ge(consts, 1)
            ve.tensor_copy(rows[R_LDT:R_LDT + PAIRS, :].rearrange("j (two p) -> j two p", two=2),
                           ldt[R_LDT:R_LDT + PAIRS, :].unsqueeze(2).broadcast_to((PAIRS, 2, NS))).then_inc(ldt_rows, 1)
            mean_square(1)
            normalise(1, h)
            ready(dve, ("rows",))
            ve.tensor_copy(cols, psum[:, bank_of(("rows",)), 0:N_ROWS]).then_inc(read, 1)
            fence()
            are, dt, lre, frac, step_f = par[:, 0], par[:, 1], par[:, 4], par[:, 2], par[:, 11]
            ve.tensor_scalar(are, cols[:, R_ARE:R_ARE + 16], -1e-4, None, ALU.min).then_inc(par_s, 1)
            transposed("nT", 0)
            dve.wait_ge(apar_s, 1)

            def one_over_ratio(dst, t, tmp):
                ve.tensor_scalar(tmp, t, -1.0, 1.0, ALU.mult, ALU.add)
                fence()
                ve.reciprocal(tmp, tmp)
                fence()
                ve.scalar_tensor_tensor(dst, t, 1.0, tmp, ALU.add, ALU.mult)
                fence()

            one_over_ratio(dt, par[:, 3], par[:, 12])
            for _ in range(3):
                ve.tensor_tensor(dt, dt, dt, ALU.mult)
                fence()
            ve.tensor_tensor(lre, are, dt, ALU.mult)
            fence()
            ve.tensor_tensor(frac, cols[:, R_AIM:R_AIM + 16], dt, ALU.mult).then_inc(par_s, 1)
            fence()
            ve.tensor_scalar(frac, frac, 1.0 / 6.283185307179586, None, ALU.mult)
            fence()

            def reduce(dst, src, tmp, add=0.0):
                ve.tensor_scalar(dst, src, 1.0, add, ALU.mult, ALU.add)
                fence()
                ve.tensor_scalar(tmp, dst, ROUND, ROUND, ALU.add, ALU.subtract)
                fence()
                ve.tensor_tensor(dst, dst, tmp, ALU.subtract)
                fence()

            reduce(par[:, 13], frac, par[:, 12])
            reduce(par[:, 6], par[:, 13], par[:, 12], 0.25)
            ve.tensor_copy(par[:, 7], par[:, 13])
            ve.tensor_scalar(step_f, par[:, 13], 16.0, None, ALU.mult)
            fence()
            reduce(step_f, step_f, par[:, 12])
            big = whole[:, 0:256].rearrange("p (j a) -> p j a", j=PAIRS)
            it = iota16.unsqueeze(1).broadcast_to((P, PAIRS, 16))
            ta = phase[:, 0:256].rearrange("p (j a) -> p j a", j=PAIRS)
            ve.tensor_tensor(ta, step_f.unsqueeze(2).broadcast_to((P, PAIRS, 16)), it, ALU.mult)
            ve.tensor_tensor(turn_b, par[:, 13].unsqueeze(2).broadcast_to((P, PAIRS, 16)), it, ALU.mult)
            fence()
            reduce(turn_b, turn_b, big)
            for c, add in ((0, 0.25), (1, 0.0)):
                reduce(turn_a[:, :, c, :], ta, big, add)
            ve.tensor_copy(par[:, 12], par[:, 13]).then_inc(par_s, 1)
            dve.wait_ge(apar_s, 3)
            t_ = par[:, 5]
            ve.tensor_scalar(par[:, 12], t_, -1.0, 1.0, ALU.mult, ALU.add)
            fence()
            ve.reciprocal(par[:, 12], par[:, 12])
            fence()
            decay, rm1 = par[:, 3], par[:, 4]
            ve.scalar_tensor_tensor(decay, t_, 1.0, par[:, 12], ALU.add, ALU.mult)
            ve.scalar_tensor_tensor(rm1, t_, 2.0, par[:, 12], ALU.mult, ALU.mult)
            fence()
            lb_re, lb_im, tmp1, tmp2 = par[:, 5], par[:, 2], par[:, 12], par[:, 11]
            ve.tensor_tensor(lb_re, rm1, par[:, 8], ALU.mult)
            ve.tensor_tensor(tmp1, par[:, 10], par[:, 10], ALU.mult)
            ve.tensor_tensor(lb_im, decay, par[:, 9], ALU.mult)
            fence()
            ve.scalar_tensor_tensor(lb_re, tmp1, -2.0, lb_re, ALU.mult, ALU.add)
            ve.tensor_tensor(tmp2, are, are, ALU.mult)
            ve.tensor_tensor(par[:, 13], cols[:, R_AIM:R_AIM + 16], cols[:, R_AIM:R_AIM + 16], ALU.mult)
            fence()
            ve.tensor_tensor(tmp2, tmp2, par[:, 13], ALU.add)
            fence()
            ve.reciprocal(tmp2, tmp2)
            kre, kim = par[:, 6], par[:, 7]
            aim = cols[:, R_AIM:R_AIM + 16]
            ve.tensor_tensor(kre, lb_re, are, ALU.mult)
            ve.tensor_tensor(tmp1, lb_im, aim, ALU.mult)
            ve.tensor_tensor(kim, lb_im, are, ALU.mult)
            ve.tensor_tensor(par[:, 13], lb_re, aim, ALU.mult)
            fence()
            ve.tensor_tensor(kre, kre, tmp1, ALU.add)
            ve.tensor_tensor(kim, kim, par[:, 13], ALU.subtract)
            fence()
            ve.tensor_tensor(kre, kre, tmp2, ALU.mult)
            ve.tensor_tensor(kim, kim, tmp2, ALU.mult)
            fence()
            dve.wait_ge(b_in, 64)
            kre_b, kim_b = (k.unsqueeze(2).broadcast_to((P, PAIRS, 32)) for k in (kre, kim))
            ve.tensor_tensor(b_bar[:, 0], b_raw[:, 0], kre_b, ALU.mult)
            ve.tensor_tensor(b_tmp[:, 0], b_raw[:, 1], kim_b, ALU.mult)
            ve.tensor_tensor(b_bar[:, 1], b_raw[:, 1], kre_b, ALU.mult)
            ve.tensor_tensor(b_tmp[:, 1], b_raw[:, 0], kim_b, ALU.mult)
            fence()
            ve.tensor_tensor(b_bar[:, 0], b_bar[:, 0], b_tmp[:, 0], ALU.subtract)
            ve.tensor_tensor(b_bar[:, 1], b_bar[:, 1], b_tmp[:, 1], ALU.add).then_inc(bbar_s, 1)
            for w in range(2):
                u = ("Bd", w)
                ready(dve, u)
                ve.tensor_copy(Bd[:, w], psum[:, bank_of(u), :].rearrange("p (q m) -> p q m", q=QG)).then_inc(read, 1)
            for w in range(2):
                u = ("C", w)
                ready(dve, u)
                for two in range(2):
                    sl = slice(two * NS, (two + 1) * NS)
                    src = psum[sl, bank_of(u), :].rearrange("p (j m) -> p j m", j=PAIRS)[:, :, two * GC:(two + 1) * GC]
                    dst = Ct[sl, :, :, two * GC:(two + 1) * GC]
                    if w == 0:
                        ve.tensor_copy(dst[:, 0], src)
                        last = ve.tensor_scalar(dst[:, 1], src, -1.0, None, ALU.mult)
                    else:
                        last = ve.tensor_scalar(dst[:, 2], src, -1.0, None, ALU.mult)
                last.then_inc(read, 1)
            mean_square(2)
            normalise(2, xn)

            def scan(j):
                bank = BU + j % 2
                dve.wait_ge(bu_s, j + 1)
                dve.wait_ge(turn_s, j + 1)
                bu = psum[:, bank, :].rearrange("p (c s) -> p c s", c=2)
                ve.tensor_tensor(m_cos, bu, turns[:, j, 0, :].unsqueeze(1).broadcast_to((P, 2, S)), ALU.mult)
                ve.tensor_tensor(m_sin, bu, turns[:, j, 1, :].unsqueeze(1).broadcast_to((P, 2, S)), ALU.mult).then_inc(bu_read, 1)
                fence()
                ve.tensor_tensor(drive[:, 0], m_cos[:, 0], m_sin[:, 1], ALU.add)
                ve.tensor_tensor(drive[:, 1], m_cos[:, 1], m_sin[:, 0], ALU.subtract)
                fence()
                if j >= 2:
                    dve.wait_ge(prod_s, j - 1)
                for c in range(2):
                    last = ve.tensor_tensor_scan(state[:, j % 2, c], decay[:, j:j + 1].broadcast_to((P, S)), drive[:, c],
                                                 0.0, ALU.mult, ALU.add)
                last.then_inc(state_s, 1)

            def softmax_head(hd):
                u = ("S", hd)
                ready(dve, u)
                b = sc[:, hd % 2]
                if hd >= 2:
                    dve.wait_ge(mm, number[("T", hd - 2)] + 1)
                ve.scalar_tensor_tensor(b, psum[:, bank_of(u), 0:384], DH ** -0.5, mask, ALU.mult, ALU.add).then_inc(read, 1)
                fence()
                o = 12 + 2 * (hd % 2)
                ve.reduce_max(stat[:, 8:9], b[:, 0:P], AX)
                ve.reduce_max(stat[:, 9:10], b[:, P:384], AX)
                fence()
                ve.tensor_scalar(stat[:, o:o + 2], stat[:, 8:10], -1.0, None, ALU.mult).then_inc(smax_s, 1)

            def normalise_head(hd):
                dve.wait_ge(exp_s, hd + 1)
                b = sc[:, hd % 2]
                o = 16 + 2 * (hd % 2)
                ve.reciprocal(stat[:, 10:12], stat[:, o:o + 2])
                fence()
                ve.tensor_scalar(b[:, 0:P], b[:, 0:P], stat[:, 10:11], None, ALU.mult)
                ve.tensor_scalar(b[:, P:384], b[:, P:384], stat[:, 11:12], None, ALU.mult).then_inc(prob_s, 1)

            def gelu_dve(q):
                dve.wait_ge(y_s, q + 1)
                if q:
                    fence()
                ve.scalar_tensor_tensor(yskip, uT[:, q, :], cols[:, R_DSK + q:R_DSK + q + 1], psum[:, Y, 0:S],
                                        ALU.mult, ALU.add).then_inc(gl1, 1)
                dve.wait_ge(gl2, 2 * q + 1)
                ve.tensor_scalar(gtmp, gtmp, 0.044715, 1.0, ALU.mult, ALU.add)
                fence()
                ve.tensor_tensor(gtmp, gtmp, yskip, ALU.mult).then_inc(gl3, 1)
                dve.wait_ge(gl2, 2 * q + 2)
                ve.scalar_tensor_tensor(geluT[:, q, :], gtmp, 1.0, yskip, ALU.add, ALU.mult).then_inc(gelu_s, 1)

            for j in range(STEPS):
                if j < PAIRS:
                    scan(j)
                if j % 2 == 0 and j < PAIRS:
                    softmax_head(j // 2)
                if j % 2 == 1 and j < PAIRS:
                    normalise_head(j // 2)
                if j % 4 == 3 and j >= 7:
                    gelu_dve((j - 7) // 4)
            for c in range(KD):
                u = ("ya", c)
                ready(dve, u)
                evacuated(dve, ("z", PAIRS - 1))
                ve.scalar_tensor_tensor(gates[:, c, :], gates[:, c, :], 1.0, psum[:, bank_of(u), 0:S],
                                        ALU.add, ALU.mult).then_inc(read, 1)
            for c in range(KD):
                u = ("zb", c)
                evacuated(dve, ("zg", c))
                fence()
                ve.scalar_tensor_tensor(yskip, sc[:, c % 2, 0:S], 1.0, psum[:, bank_of(u), 0:S],
                                        ALU.add, ALU.mult).then_inc(read, 1)
                fence()
                ve.scalar_tensor_tensor(gtmp, gates[:, KD + c, :], 1.0, yskip, ALU.add, ALU.mult)
                fence()
                ve.tensor_scalar(gtmp, gtmp, 0.125, None, ALU.mult)
                fence()
                ve.scalar_tensor_tensor(mergedT[:, c, :], gates[:, c, :], 0.5, gtmp, ALU.mult, ALU.add).then_inc(merged_s, 1)

            transposed("memT", 2)

            def add_residual(name):
                for t in range(TT):
                    for hf in range(2):
                        u = (name, t, hf)
                        ready(dve, u)
                        cs = slice(hf * HALF, (hf + 1) * HALF)
                        ve.tensor_tensor(h[:, t, cs], h[:, t, cs], psum[:, bank_of(u), :], ALU.add).then_inc(read, 1)

            add_residual("out")
            mean_square(3)
            normalise(3, h)
            transposed("n2T", 1)

            def xsoftmax(hd):
                u = ("XS", hd)
                ready(dve, u)
                fence()
                o = 20 + 2 * (hd % 2)
                ve.tensor_reduce(stat[:, 8:10], psum[:, bank_of(u), :].rearrange("p (t s) -> p t s", t=TT), AX, ALU.max)
                fence()
                ve.tensor_scalar(stat[:, o:o + 2], stat[:, 8:10], -XDH ** -0.5, None, ALU.mult).then_inc(xmax_s, 1)

            def xnormalise(hd):
                evacuated(dve, ("XS", hd))
                o = 24 + 2 * (hd % 2)
                ve.reciprocal(stat[:, 10:12], stat[:, o:o + 2])
                fence()
                for t in range(TT):
                    last = ve.tensor_scalar(xp[:, hd % 2, t, :], xp[:, hd % 2, t, :], stat[:, 10 + t:11 + t], None, ALU.mult)
                last.then_inc(xprob_s, 1)
                fence()

            xsoftmax(0)
            xsoftmax(1)
            for hd in range(XH):
                xnormalise(hd)
                if hd + 2 < XH:
                    xsoftmax(hd + 2)
            add_residual("xo")
            mean_square(4)
            normalise(4, h)
            transposed("n3T", 3)

            u = ("logits",)
            ready(dve, u)
            dve.wait_ge(consts, 2)
            ve.tensor_copy(logit, psum[:, bank_of(u), 0:2 * E].rearrange("p (t e) -> p t e", t=TT)).then_inc(read, 1)
            fence()
            for t in range(TT):
                ve.max(top8[:, t, :], logit[:, t, :])
            fence()
            ve.tensor_scalar(stat[:, 36:38], top8[:, :, 0], -1.0, None, ALU.mult).then_inc(rt1, 1)
            for t in range(TT):
                ve.max_index(topi[:, t, :], top8[:, t, :], logit[:, t, :])
            fence()
            ve.tensor_copy(topf, topi[:, :, :])
            fence()
            for n in range(TOPK):
                for t in range(TT):
                    if n == 0:
                        last = ve.tensor_scalar(chosen[:, t, :], exp_no, topf[:, t, 0:1], None, ALU.is_equal)
                    else:
                        last = ve.scalar_tensor_tensor(chosen[:, t, :], exp_no, topf[:, t, n:n + 1], chosen[:, t, :],
                                                       ALU.is_equal, ALU.add)
                if n == TOPK - 1:
                    last.then_inc(chosen_s, 1)
                fence()
            dve.wait_ge(rt2, 1)
            ve.tensor_tensor(gate_w[:, :, 0:E], gate_w[:, :, 0:E], chosen, ALU.mult)
            fence()
            ve.tensor_reduce(stat[:, 46:48], gate_w[:, :, 0:E], AX, ALU.add)
            fence()
            ve.reciprocal(stat[:, 46:48], stat[:, 46:48])
            fence()
            for t in range(TT):
                ve.tensor_scalar(gate_w[:, t, 0:E], gate_w[:, t, 0:E], stat[:, 46 + t:47 + t], None, ALU.mult)
            fence()
            ve.tensor_copy(gate_w[:, :, E:E + 1], gate_w[:, :, 0:1]).then_inc(rt1, 1)
            u = ("pos",)
            ready(dve, u)
            pp = psum[:, bank_of(u), 0:3 * E].rearrange("p (t e) -> p t e", t=3)
            ve.scalar_tensor_tensor(pos[:, :, 0:E], pp[:, 0:2, :], OFF, chosen, ALU.add, ALU.mult)
            ve.reduce_max(stat[:, 48:49], pp[:, 2, :], AX).then_inc(read, 1)
            fence()
            ve.tensor_scalar(pos[:, :, 0:E], pos[:, :, 0:E], OFF, None, ALU.subtract)
            ve.tensor_scalar(stat[:, 49:50], stat[:, 48:49], float(SLOTS), 1.0, ALU.is_gt, ALU.add)
            fence()
            for r in range(2, ROUNDS):
                ve.scalar_tensor_tensor(stat[:, 49:50], stat[:, 48:49], float(r * SLOTS), stat[:, 49:50], ALU.is_gt, ALU.add)
                fence()
            ve.tensor_scalar(pos[:, :, E:E + 1], pos[:, :, 0:1], float(SLOTS), None, ALU.subtract)
            ve.tensor_copy(rounds_i[:, :], stat[:, 49:50]).then_inc(rounds_s, 1)
            u = ("GT",)
            ready(dve, u)
            ve.tensor_copy(GT[0:E, :], psum[0:E, bank_of(u), 0:S]).then_inc(GT_s, 1)
            ve.memset(y_sb[0], 0.0).then_inc(gu_read, 1)
            ve.memset(y_sb[1], 0.0)
            ve.memset(spreadT[0], 0.0)
            ve.memset(spreadT[1], 0.0).then_inc(y_zero, 1)
            fence()
            gain_e = cols[:, R_GAIN + 3 * KD:R_GAIN + 4 * KD].unsqueeze(2).broadcast_to((P, KD, SLOTS))

            def one_hots(col, b):
                for t in range(TT):
                    ve.tensor_scalar(pick[b][:, t, :], slot_no[:, 0:SLOTS], pos[:, t, col], None, ALU.is_equal)
                for t in range(TT):
                    last = ve.tensor_scalar(spread[b][:, t, :], slot_no, pos[:, t, col], gate_w[:, t, col],
                                            ALU.is_equal, ALU.mult)
                last.then_inc(pick_s, 1)

            def gathered(i, b):
                dve.wait_ge(gather_s, i + 1)
                ve.tensor_tensor(xeT[b], psum[:, 6, :].rearrange("p (k s) -> p k s", k=KD), gain_e, ALU.mult).then_inc(xe_s, 1)

            one_hots(slice(0, 1), 0)
            gathered(0, 0)

            def expert(i, e, b):
                dve.wait_ge(gu_used, i * KD + 1)
                one_hots(bass.ds(e + 1, 1), 1 - b)
                dve.wait_ge(gu_used, (i + 1) * KD)
                ve.tensor_scalar(gate_c, psum[:, 4, :], LIMIT, None, ALU.min).then_inc(gate_cs, 1)
                ve.tensor_scalar(up_c, psum[:, 5, :], LIMIT, -LIMIT, ALU.min, ALU.max).then_inc(gu_read, 1)
                fence()
                ve.scalar_tensor_tensor(gated, up_c, 1.0, gate_c, ALU.add, ALU.mult)
                fence()
                dve.wait_ge(tanh_s, i + 1)
                ve.scalar_tensor_tensor(hid, gate_t, 1.0, gated, ALU.add, ALU.mult).then_inc(hid_s, 1)
                gathered(i + 1, 1 - b)

            def sweep(r):
                with dve.Fori(0, E // 2) as e2:
                    for b in range(2):
                        expert(r * E + e2 * 2 + b, e2 * 2 + b, b)

            def later(r):
                fence()
                ve.tensor_scalar(pos, pos, float(SLOTS), None, ALU.subtract)
                fence()
                sweep(r)

            sweep(0)
            later_rounds(dve, later)
            dve.wait_ge(acc_s, 1)
            for t in range(TT):
                for hf in range(2):
                    cs = slice(hf * HALF, (hf + 1) * HALF)
                    ve.tensor_tensor(h[:, t, cs], h[:, t, cs], psum[:, 2 * t + hf, :], ALU.add)
            fence()
            ve.tensor_copy(stat[:, 44:45], stat[:, 34:35]).then_inc(h_s, 1)
            mean_square(5)
            dve.wait_ge(rstd_s, 5)
            dve.wait_ge(gfin_in, 16)
            for t in range(TT):
                ve.scalar_tensor_tensor(h[:, t, :], h[:, t, :], stat[:, 4 + t:5 + t], gfin, ALU.mult, ALU.mult).then_inc(outd, 1)

        @block.tensor
        def _(pe):
            te = nc.tensor
            done_blocks = [0]

            def open_unit(u):
                if number[u] >= MM:
                    evacuated(pe, plan[number[u] - MM][0])
                return psum[:, bank_of(u), :]

            def transposes(name, n_norm):
                for kp in range(4):
                    u = (name, kp)
                    ps = open_unit(u)
                    if kp == 0:
                        pe.wait_ge(xn_s, TT * n_norm)
                    for k in range(2):
                        for t in range(TT):
                            last = te.transpose(ps[:, k * S + t * P:k * S + (t + 1) * P],
                                                xn[:, t, (2 * kp + k) * P:(2 * kp + k + 1) * P], ident)
                    last.then_inc(mm, 1)

            def next_block():
                n = done_blocks[0]
                done_blocks[0] += 1
                arrived(pe, n)
                return front[n % FW]

            def column_unit(u, w, c, rhs, kn):
                ps = open_unit(u)
                for k in range(kn):
                    last = te.matmul(ps[:, 0:S], w[:, k, c * P:(c + 1) * P], rhs[:, k, :], start=(k == 0), stop=(k == kn - 1))
                last.then_inc(mm, 1)

            pe.wait_ge(consts, 1)
            ps = open_unit(("rows",))
            pe.wait_ge(ldt_rows, 1)
            te.transpose(ps[:, 0:N_ROWS], rows[0:N_ROWS, :], ident[0:N_ROWS, 0:N_ROWS]).then_inc(mm, 1)
            transposes("nT", 1)
            for w in range(2):
                ps = open_unit(("Bd", w))
                pe.wait_ge(bbar_s, 1)
                for q in range(QG):
                    last = te.transpose(ps[:, q * P:(q + 1) * P], b_bar[:, w, 4 * q:4 * q + 4, :].rearrange("p j c -> p (j c)"), ident)
                last.then_inc(mm, 1)
            for w in range(2):
                ps = open_unit(("C", w))
                pe.wait_ge(c_in, 64)
                for q in range(QG):
                    last = te.transpose(ps[:, q * P:(q + 1) * P], c_raw[:, w, q, :], ident)
                last.then_inc(mm, 1)
            evacuated(pe, ("nT", 3))
            for name in ("u", "q", "k"):
                for hf in range(2):
                    w = next_block().rearrange("p (k n) -> p k n", k=KD)
                    for c in range(2):
                        column_unit((name, 2 * hf + c), w, c, nT, KD)
            for hf in range(2):
                w = next_block().rearrange("p (k n) -> p k n", k=KD)
                for t in range(TT):
                    u = ("v", hf, t)
                    ps = open_unit(u)
                    for k in range(KD):
                        last = te.matmul(ps[:, 0:256], nT[:, k, t * P:(t + 1) * P], w[:, k, :], start=(k == 0), stop=(k == KD - 1))
                    last.then_inc(mm, 1)
            evacuated(pe, ("Bd", 1))

            def drive_in(j):
                if j >= 2:
                    pe.wait_ge(bu_read, j - 1)
                if j % 4 == 0:
                    evacuated(pe, ("u", j // 4))
                o = 32 * (j % 4)
                for w in range(2):
                    last = te.matmul(psum[:, BU + j % 2, w * S:(w + 1) * S], Bd[o:o + 32, w, j // 4, :],
                                     uT[o:o + 32, j // 4, :], start=True, stop=True)
                last.then_inc(bu_s, 1)

            def y_out(q):
                pe.wait_ge(prod_s, 4 * (q + 1))
                if q == 0:
                    evacuated(pe, ("C", 1))
                else:
                    pe.wait_ge(gl1, q)
                for n, (w, m, c) in enumerate(((0, 0, 0), (2, 0, 1), (1, 1, 1), (2, 1, 0))):
                    for jj in range(4):
                        last = te.matmul(psum[32 * jj:32 * jj + 32, Y, 0:S], Ct[:, w, 4 * q + jj, :], prod[:, jj, m, c, :],
                                         start=(n == 0), stop=(n == 3))
                last.then_inc(y_s, 1)

            def scores(hd):
                ps = open_unit(("S", hd))
                o, c = DH * (hd % 2), hd // 2
                if hd % 2 == 0:
                    evacuated(pe, ("k", c))
                te.matmul(ps[:, 0:P], qT[o:o + DH, c, 0:P], kT[o:o + DH, c, 0:P], start=True, stop=True)
                te.matmul(ps[:, P:384], qT[o:o + DH, c, P:S], kT[o:o + DH, c, :], start=True, stop=True).then_inc(mm, 1)

            def probs_T(hd):
                ps = open_unit(("T", hd))
                pe.wait_ge(prob_s, hd + 1)
                b = sc[:, hd % 2]
                for n in range(3):
                    last = te.transpose(ps[:, n * P:(n + 1) * P], b[:, n * P:(n + 1) * P], ident)
                last.then_inc(mm, 1)

            def weighted(hd):
                open_unit(("O", hd))
                evacuated(pe, ("T", hd))
                evacuated(pe, ("v", 1, 1))
                o = DH * (hd % 2)
                ps = psum[o:o + DH, bank_of(("O", hd)), :]
                te.matmul(ps[:, 0:S], v_sb[:, 0, hd * DH:(hd + 1) * DH], scT[:, 0:S], start=True, stop=False)
                te.matmul(ps[:, P:S], v_sb[:, 1, hd * DH:(hd + 1) * DH], scT[:, S:384], start=False, stop=True).then_inc(mm, 1)

            for j in range(STEPS):
                if j < PAIRS:
                    drive_in(j)
                if j % 2 == 0 and j < PAIRS:
                    scores(j // 2)
                if j % 2 == 0 and 2 <= j <= PAIRS:
                    probs_T(j // 2 - 1)
                if j % 2 == 1 and 3 <= j <= PAIRS + 1:
                    weighted((j - 3) // 2)
                if j < PAIRS:
                    if j % 2 == 0:
                        w = next_block().rearrange("p (k n) -> p k n", k=KD)
                    column_unit(("z", j), w, j % 2, nT, KD)
                if j % 4 == 2 and j >= 6:
                    y_out((j - 6) // 4)
            evacuated(pe, ("O", HEADS - 1))
            for hf in range(2):
                w = next_block().rearrange("p (k n) -> p k n", k=4)
                for c in range(4):
                    column_unit(("ya", 4 * hf + c), w, c, attnT, 4)
            pe.wait_ge(gelu_s, 4)
            for hf in range(2):
                wa = next_block().rearrange("p (k n) -> p k n", k=4)
                wb = next_block().rearrange("p (k n) -> p k n", k=4)
                for c in range(4):
                    column_unit(("zb", 4 * hf + c), wa, c, geluT, 4)
                    column_unit(("zg", 4 * hf + c), wb, c, geluT, 4)

            def rows_out(name, src, blocks, source_ready):
                us = [(name, t, hf) for t in range(TT) for hf in range(2)]
                for u in us:
                    open_unit(u)
                for bl in range(blocks):
                    w = next_block().rearrange("p (k n) -> p k n", k=2)
                    for k in range(2):
                        source_ready(2 * bl + k)
                        for u in us:
                            last = te.matmul(psum[:, bank_of(u), :], src[:, 2 * bl + k, u[1] * P:(u[1] + 1) * P],
                                             w[:, k, u[2] * HALF:(u[2] + 1) * HALF],
                                             start=(bl + k == 0), stop=(bl == blocks - 1 and k == 1))
                            if bl == blocks - 1 and k == 1:
                                last.then_inc(mm, 1)
                    if bl < blocks - 1:
                        last.then_inc(rows_used, 1)
    
            transposes("memT", 2)
            evacuated(pe, ("memT", 3))
            for hf in range(2):
                w = next_block().rearrange("p (k n) -> p k n", k=KD)
                for c in range(2):
                    column_unit(("xk", 2 * hf + c), w, c, nT, KD)
            for hf in range(2):
                w = next_block().rearrange("p (k n) -> p k n", k=KD)
                for t in range(TT):
                    ps = open_unit(("xv", hf, t))
                    for k in range(KD):
                        last = te.matmul(ps[:, 0:256], nT[:, k, t * P:(t + 1) * P], w[:, k, :], start=(k == 0), stop=(k == KD - 1))
                    last.then_inc(mm, 1)
            rows_out("out", mergedT, 4, lambda k: pe.wait_ge(merged_s, k + 1))
            transposes("n2T", 3)
            evacuated(pe, ("n2T", 3))
            for hf in range(2):
                w = next_block().rearrange("p (k n) -> p k n", k=KD)
                for c in range(2):
                    column_unit(("xq", 2 * hf + c), w, c, nT, KD)

            def xscores(hd):
                ps = open_unit(("XS", hd))
                evacuated(pe, ("xq", hd))
                for t in range(TT):
                    last = te.matmul(ps[:, t * S:(t + 1) * S], attnT[:, hd, t * P:(t + 1) * P], kxT[:, hd, :], start=True, stop=True)
                last.then_inc(mm, 1)

            xscores(0)
            xscores(1)
            for hd in range(XH):
                ps = open_unit(("XT", hd))
                pe.wait_ge(xprob_s, hd + 1)
                for m in range(TT):
                    for t in range(TT):
                        last = te.transpose(ps[:, m * S + t * P:m * S + (t + 1) * P], xp[:, hd % 2, t, m * P:(m + 1) * P], ident)
                last.then_inc(mm, 1)
                ps = open_unit(("XO", hd))
                evacuated(pe, ("XT", hd))
                for m in range(TT):
                    last = te.matmul(ps[:, 0:S], vx[:, m, hd * XDH:(hd + 1) * XDH], xpT[:, hd % 2, m, :], start=(m == 0), stop=(m == 1))
                last.then_inc(mm, 1)
                if hd + 2 < XH:
                    xscores(hd + 2)
            rows_out("xo", attnT, 2, lambda k: evacuated(pe, ("XO", k)))
            transposes("n3T", 4)
            ps = open_unit(("logits",))
            pe.wait_ge(router_in, 48)
            evacuated(pe, ("n3T", 3))
            for t in range(TT):
                for k in range(KD):
                    te.matmul(ps[:, t * E:(t + 1) * E], nT[:, k, t * P:(t + 1) * P], router[:, k, :], start=(k == 0), stop=False)
                last = te.matmul(ps[:, t * E:(t + 1) * E], ones[0:1, 0:P], brt[0:1, :], start=False, stop=True)
            last.then_inc(mm, 1)
            ps = open_unit(("pos",))
            pe.wait_ge(chosen_s, 1)
            te.matmul(ps[:, 0:E], tri, chosen[:, 0, :], start=True, stop=True)
            te.matmul(ps[:, E:2 * E], ones, chosen[:, 0, :], start=True, stop=False)
            te.matmul(ps[:, E:2 * E], tri, chosen[:, 1, :], start=False, stop=True)
            te.matmul(ps[:, 2 * E:3 * E], ones, chosen[:, 0, :], start=True, stop=False)
            te.matmul(ps[:, 2 * E:3 * E], ones, chosen[:, 1, :], start=False, stop=True).then_inc(mm, 1)
            ps = open_unit(("GT",))
            pe.wait_ge(rt1, 2)
            for t in range(TT):
                last = te.transpose(ps[0:E, t * P:(t + 1) * P], gate_w[:, t, 0:E], ident)
            last.then_inc(mm, 1)

            def gather(i, b):
                pe.wait_ge(pick_s, i + 1)
                for k in range(KD):
                    for t in range(TT):
                        last = te.matmul(psum[:, 6, k * SLOTS:(k + 1) * SLOTS], xn[:, t, k * P:(k + 1) * P], pick[b][:, t, :],
                                         start=(t == 0), stop=(t == TT - 1))
                last.then_inc(gather_s, 1)

            gather(0, 0)
            pe.wait_ge(GT_s, 1)
            for t in range(TT):
                for hf in range(2):
                    te.matmul(psum[:, 2 * t + hf, :], GT[0:E, t * P:(t + 1) * P], bdn[0:E, hf * HALF:(hf + 1) * HALF],
                              start=True, stop=False)

            def combine(b, stop=False):
                for t in range(TT):
                    for hf in range(2):
                        last = te.matmul(psum[:, 2 * t + hf, :], spreadT[b][hf * SLOTS:(hf + 1) * SLOTS, t, :],
                                         y_sb[b][hf * SLOTS:(hf + 1) * SLOTS, :], start=False, stop=stop, skip_group_check=not stop)
                return last

            def expert(i, b):
                pe.wait_ge(gu_read, i + 1)
                pe.wait_ge(xe_s, i + 1)
                pe.wait_ge(bias_in, 16 * (i + 1))
                for gu in range(2):
                    for hf in range(2):
                        last = te.matmul(psum[hf * SLOTS:(hf + 1) * SLOTS, 4 + gu, :], ones[0:1, 0:SLOTS],
                                         bias_row[0:1, gu * FF + hf * HALF:gu * FF + (hf + 1) * HALF], start=True, stop=False)
                last.then_inc(bias_used, 1)
                for k in range(KD):
                    pe.wait_ge(gu_in[k], 16 * (i + 1))
                    for gu in range(2):
                        for hf in range(2):
                            last = te.matmul(psum[hf * SLOTS:(hf + 1) * SLOTS, 4 + gu, :], xeT[b][:, k, :],
                                             gu_ring[k][:, gu * FF + hf * HALF:gu * FF + (hf + 1) * HALF],
                                             start=False, stop=(k == KD - 1))
                    last.then_inc(gu_used, 1)
                pe.wait_ge(y_ready, i + 1)
                combine(1 - b)
                gather(i + 1, 1 - b)
                pe.wait_ge(hid_s, i + 1)
                for n in range(4):
                    last = te.transpose(psum[:, DN, n * P:(n + 1) * P], hid[:, n * P:(n + 1) * P], ident)
                last.then_inc(hidT_ps, 1)
                pe.wait_ge(xe_s, i + 2)
                for t in range(TT):
                    last = te.transpose(psum[:, 6, t * P:(t + 1) * P], spread[b][:, t, :], ident)
                last.then_inc(spT_ps, 1)
                pe.wait_ge(hidT_s, i + 1)
                for k in range(FF // P):
                    pe.wait_ge(dn_in[k], 16 * (i + 1))
                    n, c = k % 4, k // 4
                    for hf in range(2):
                        last = te.matmul(psum[hf * SLOTS:(hf + 1) * SLOTS, DN, :], hidT[:, n, c * SLOTS:(c + 1) * SLOTS],
                                         dn_ring[k][:, hf * HALF:(hf + 1) * HALF], start=(k == 0), stop=(k == FF // P - 1))
                    last.then_inc(dn_used, 1)

            def sweep(r):
                with pe.Fori(0, E // 2) as e2:
                    for b in range(2):
                        expert(r * E + e2 * 2 + b, b)

            sweep(0)
            n = later_rounds(pe, sweep)
            pe.wait_ge(y_ready, n * E + 1)
            combine(1, True).then_inc(acc_s, 1)


_INS = ["x", "mem", "g_mix", "w_in", "a_re", "a_im", "log_dt", "b_re", "b_im", "c_re", "c_im", "d_skip", "w_glu",
        "w_proj_a", "w_out", "g_xattn", "g_mem", "w_xq", "w_xkv", "w_xo", "g_moe", "w_router", "b_router", "w_gu",
        "b_gu", "w_dn", "b_dn", "g_final"]


def kernel(**inputs):
    import numpy as _np
    import concourse.bacc as _bacc
    from concourse import mybir as _mybir
    from concourse.bass_utils import run_bass_kernel_spmd as _run

    nc = _bacc.Bacc("TRN2", target_bir_lowering=False, num_devices=1)
    arrays, args = {}, []
    for name in _INS:
        a = _np.ascontiguousarray(inputs[name])
        arrays[f"in_{name}"] = a
        args.append(nc.dram_tensor(f"in_{name}", a.shape, _mybir.dt.from_np(a.dtype), kind="ExternalInput").ap())
    out = nc.dram_tensor("out_dram", (1, S, D), F32, kind="ExternalOutput").ap()
    build_layer(nc, *args, out)
    r = _run(nc, [arrays], core_ids=[0])
    return r.results[0]["out_dram"]
```

```python
from contextlib import ExitStack

import concourse.bass as bass
from concourse import mybir

F32 = mybir.dt.float32
I32 = mybir.dt.int32
U32 = mybir.dt.uint32
ALU = mybir.AluOpType
ACT = mybir.ActivationFunctionType
AX = mybir.AxisListType.X

P = 128
D = 1024
S = 256
TT = S // P
KD = D // P
HEADS, DH = 8, 64
XH, XDH = 4, 128
G, NS, GC = 32, 64, 16
PAIRS = G // 2
QG = 4
E, TOPK, FF = 32, 4, 1024
SLOTS = 64
ROUNDS = S // SLOTS
HALF = 512
EPS = 1e-6
NEG = -1e30
LIMIT, ALPHA = 7.0, 1.702
ROUND = 12582912.0
TWO_PI = 6.2831850
OFF = 16384.0
FW = 6
SLOT = 2048
STEPS = PAIRS + 2
MM = 4

R_ARE, R_LDT, R_DSK, R_AIM, R_GAIN = 0, 32, 48, 64, 80
N_ROWS = R_GAIN + 4 * KD


def dense_weights():
    order = [("w_in", "cols", 1536 + 256 * i) for i in range(2)]
    order += [("w_in", "cols", 256 * i) for i in range(6)]
    order += [("w_in", "cols", 2048 + 256 * i) for i in range(8)]
    order += [("w_proj_a", "wide", 512 * i) for i in range(2)]
    order += [("w_glu", "wide", c) for c in (0, 1024, 512, 1536)]
    order += [("w_out", "rows", 2 * i) for i in range(4)]
    order += [("w_xkv", "cols", 256 * i) for i in range(2)]
    order += [("w_xq", "cols", 256 * i) for i in range(2)]
    order += [("w_xkv", "cols", 512 + 256 * i) for i in range(2)]
    order += [("w_xo", "rows", 2 * i) for i in range(2)]
    return order


def last_units():
    out = [("u", 1), ("u", 3), ("q", 1), ("q", 3), ("k", 1), ("k", 3), ("v", 0, 1), ("v", 1, 1)]
    out += [("z", c) for c in range(1, PAIRS, 2)]
    out += [("ya", 3), ("ya", 7), ("zb", 3), ("zg", 3), ("zb", 7), ("zg", 7)]
    out += [None, None, None, ("out", 1, 1), ("xk", 1), ("xk", 3), ("xq", 1), ("xq", 3), ("xv", 0, 1), ("xv", 1, 1)]
    return out + [None, ("xo", 1, 1)]


def units():
    def tiles(name, t):
        return [((name, t, kq), "dve") for kq in range(2)]

    out = [(("rows",), "dve")] + tiles("nT", 0) + tiles("nT", 1)
    out += [(("u", c), "act") for c in range(4)] + [(("q", c), "act") for c in range(4)]
    out += [(("Bd", 0), "dve"), (("Bd", 1), "dve"), (("C", 0), "dve"), (("C", 1), "dve")]
    out += [(("k", c), "act") for c in range(4)] + [(("v", hf, t), "act") for hf in range(2) for t in range(TT)]
    for j in range(STEPS):
        if j % 2 == 0 and j < PAIRS:
            out.append((("S", j // 2), "dve"))
        if j % 2 == 0 and j >= 2:
            out.append((("T", j // 2 - 1), "act"))
        if j % 2 == 1 and j >= 3:
            out.append((("O", (j - 3) // 2), "act"))
        if j < PAIRS:
            out.append((("z", j), "act"))
        if j == PAIRS:
            out += tiles("memT", 0) + tiles("memT", 1)
    out += [(("ya", c), "dve") for c in range(KD)]
    out += [((w, c), e) for c in range(KD) for w, e in (("zb", "dve"), ("zg", "act"))]
    out += [(("out", t, hf), "dve") for t in range(TT) for hf in range(2)]
    out += tiles("n2T", 0) + [(("xk", c), "act") for c in range(4)] + tiles("n2T", 1)
    out += [(("xq", c), "act") for c in range(4)] + [(("XS", hd), "act") for hd in range(XH)]
    out += [(("xv", hf, t), "act") for hf in range(2) for t in range(TT)]
    out.append((("XT", 0), "act"))
    for hd in range(XH):
        if hd + 1 < XH:
            out.append((("XT", hd + 1), "act"))
        out.append((("XO", hd), "act"))
    out += [(("xo", t, hf), "dve") for t in range(TT) for hf in range(2)]
    out += tiles("n3T", 0) + [(("logits", 0), "dve")] + tiles("n3T", 1) + [(("logits", 1), "dve")]
    out += [(("pos",), "dve"), (("GT",), "dve")]
    return out


def build_layer(nc, x, mem, g_mix, w_in, a_re, a_im, log_dt, b_re, b_im, c_re, c_im, d_skip, w_glu, w_proj_a,
                w_out, g_xattn, g_mem, w_xq, w_xkv, w_xo, g_moe, w_router, b_router, w_gu, b_gu, w_dn, b_dn,
                g_final, out):
    weights = dict(w_in=w_in[0], w_xkv=w_xkv[0], w_proj_a=w_proj_a[0], w_glu=w_glu[0], w_out=w_out[0],
                   w_xq=w_xq[0], w_xo=w_xo[0])
    order = dense_weights()
    plan = units()
    number = {u: n for n, (u, _) in enumerate(plan)}
    reader = dict(plan)
    rank = {u: sum(e == reader[u] for _, e in plan[:number[u]]) for u, _ in plan}
    last_user = last_units()

    with ExitStack() as ctx:
        sem_names = {}

        def sem(name):
            sem_names[name] = ctx.enter_context(nc.semaphore(name))
            return sem_names[name]

        words = {}
        top = [0]
        total = 53184
        arena = ctx.enter_context(nc.sbuf_tensor("arena", [P, total], F32))

        def at(start, n):
            return arena[:, start:start + n]

        def take(n):
            top[0] += n
            assert top[0] <= total, top[0]
            return top[0] - n

        ring0 = take(KD * 2 * FF + (FF // P) * D)
        gu_ring = [at(ring0 + k * 2 * FF, 2 * FF) for k in range(KD)]
        dn_ring = [at(ring0 + KD * 2 * FF + k * D, D) for k in range(FF // P)]
        a0 = ring0
        turns = at(a0, PAIRS * 512).rearrange("p (j c s) -> p j c s", j=PAIRS, c=2)
        a0 += PAIRS * 512
        p_base = a0
        prod = at(a0, 4096).rearrange("p (b w c s) -> p b w c s", b=4, w=2, c=2)
        a0 += 4096
        gate_base = a0
        gates = at(a0, 4096).rearrange("p (c s) -> p c s", c=16)
        a0 += 4096
        qT = at(a0, 1024).rearrange("p (c s) -> p c s", c=4)
        kT = at(a0 + 1024, 1024).rearrange("p (c s) -> p c s", c=4)
        v_sb = at(a0 + 2048, 1024).rearrange("p (t n) -> p t n", t=TT)
        uT = at(a0 + 3072, 1024).rearrange("p (c s) -> p c s", c=4)
        a0 += 4096
        m_cos = at(a0, 512).rearrange("p (c s) -> p c s", c=2)
        m_sin = at(a0 + 512, 512).rearrange("p (c s) -> p c s", c=2)
        drive = at(a0 + 1024, 512).rearrange("p (c s) -> p c s", c=2)
        state = at(a0 + 1536, 1024).rearrange("p (b c s) -> p b c s", b=2, c=2)
        a0 += 3072
        Bd = at(a0, 1024).rearrange("p (w q m) -> p w q m", w=2, q=QG)
        a0 += 1024
        assert a0 <= ring0 + 24576
        b_raw = at(p_base, 1024).rearrange("p (w j c) -> p w j c", w=2, j=PAIRS)
        b_bar = at(p_base + 1024, 1024).rearrange("p (w j c) -> p w j c", w=2, j=PAIRS)
        c_raw = at(p_base + 2048, 1024).rearrange("p (w q m) -> p w q m", w=2, q=QG)
        b_tmp = at(p_base + 3072, 1024).rearrange("p (w j c) -> p w j c", w=2, j=PAIRS)
        g1 = gate_base + 4 * 256
        turn_a = at(g1, 512).rearrange("p (j c a) -> p j c a", j=PAIRS, c=2)
        turn_b = at(g1 + 512, 256).rearrange("p (j b) -> p j b", j=PAIRS)
        whole = at(g1 + 768, 2048)

        front0 = take(FW * SLOT)
        front = [at(front0 + s * SLOT, SLOT) for s in range(FW)]
        h_base = take(TT * D)
        h = at(h_base, TT * D).rearrange("p (t n) -> p t n", t=TT)
        xn_base = take(TT * D)
        xn = at(xn_base, TT * D).rearrange("p (t n) -> p t n", t=TT)
        xpT = at(xn_base, 2048).rearrange("p (b m s) -> p b m s", b=4, m=TT)
        nT_base = take(KD * S)
        nT = at(nT_base, KD * S).rearrange("p (k s) -> p k s", k=KD)
        attnT = at(take(4 * S), 4 * S).rearrange("p (c s) -> p c s", c=4)
        kx_base = take(4 * S)
        kxT = at(kx_base, 4 * S).rearrange("p (c s) -> p c s", c=4)
        geluT = at(kx_base, 4 * S).rearrange("p (c s) -> p c s", c=4)
        vx = at(take(TT * 512), TT * 512).rearrange("p (t n) -> p t n", t=TT)
        merged_base = take(KD * S)
        mergedT = at(merged_base, KD * S).rearrange("p (k s) -> p k s", k=KD)
        junk = at(merged_base, TT * D).rearrange("p (t n) -> p t n", t=TT)
        n2T = at(merged_base, KD * S).rearrange("p (k s) -> p k s", k=KD)
        xp = at(merged_base, 2048).rearrange("p (b t s) -> p b t s", b=4, t=TT)
        gfin = at(merged_base, D)
        ct_base = take(3 * PAIRS * 32)
        Ct = at(ct_base, 3 * PAIRS * 32).rearrange("p (w j m) -> p w j m", w=3, j=PAIRS)
        router = at(ct_base, KD * E).rearrange("p (k e) -> p k e", k=KD)
        bdn = at(ct_base + 256, D)
        ident = at(take(P), P)
        ones = at(take(P), P)
        tri = at(take(P), P)
        mask = at(take(384), 384)
        sc = at(take(768), 768).rearrange("p (b n) -> p b n", b=2)
        scT = at(take(384), 384)
        yskip = at(take(S), S)
        gtmp = at(take(S), S)
        cols = at(take(N_ROWS), N_ROWS)
        rows_base = take(P)
        rows = at(rows_base, P)
        ldt = at(take(2), 2)
        par = at(take(14 * 16), 14 * 16).rearrange("p (n j) -> p n j", n=14)
        iota16 = at(take(16), 16)
        slot_no = at(take(2 * SLOTS), 2 * SLOTS)
        exp_no = at(rows_base, E)
        stat = at(take(64), 64)
        xstat = at(take(32), 32)
        logit = at(take(2 * E), 2 * E).rearrange("p (t e) -> p t e", t=TT)
        chosen = at(take(2 * E), 2 * E).rearrange("p (t e) -> p t e", t=TT)
        gate_w = at(take(2 * 33), 2 * 33).rearrange("p (t e) -> p t e", t=TT)
        pos = at(take(2 * 33), 2 * 33).rearrange("p (t e) -> p t e", t=TT)
        top8 = at(take(16), 16).rearrange("p (t e) -> p t e", t=TT)
        topi = ctx.enter_context(nc.sbuf_tensor("topi", [P, TT, 8], U32))
        topf = at(take(16), 16).rearrange("p (t e) -> p t e", t=TT)
        brt = at(take(E), E)
        rounds_i = ctx.enter_context(nc.sbuf_tensor("rounds_i", [P, 1], I32))
        f0 = [front0]

        def moe(n):
            f0[0] += n
            assert f0[0] <= front0 + FW * SLOT
            return at(f0[0] - n, n)

        xeT = [moe(KD * SLOTS).rearrange("p (k s) -> p k s", k=KD) for _ in range(2)]
        pick = [moe(TT * SLOTS).rearrange("p (t s) -> p t s", t=TT) for _ in range(2)]
        spread = [moe(TT * 2 * SLOTS).rearrange("p (t s) -> p t s", t=TT) for _ in range(2)]
        spreadT = [moe(TT * P).rearrange("p (t s) -> p t s", t=TT) for _ in range(2)]
        gate_c, up_c, gate_t, gated, hid = [moe(HALF) for _ in range(5)]
        hidT = moe(HALF).rearrange("p (b s) -> p b s", b=4)
        y_sb = [moe(HALF) for _ in range(2)]
        bias_row = moe(2 * FF)
        GT = moe(S)

        psum = ctx.enter_context(nc.psum_tensor("psum", [P, 8, HALF], F32))
        BU, Y, DN = 4, 6, 7
        own_bank = {("logits", 0): BU, ("logits", 1): BU + 1, ("pos",): DN, ("GT",): BU}

        x_in = [sem(f"x_in{t}") for t in range(TT)]
        mem_in, rows_in, b_in, c_in = sem("mem_in"), sem("rows_in"), sem("b_in"), sem("c_in")
        w_in_s = [sem(f"weights_in{s}") for s in range(FW)]
        router_in, gfin_in = sem("router_in"), sem("gfin_in")
        consts = sem("consts")
        ldt_rows = sem("ldt_rows")
        cleared = sem("cleared")
        rows_used = sem("rows_used")
        mm = sem("mm")
        unit_read = {"dve": sem("dve_read"), "act": sem("act_read")}
        sq = sem("sq")
        ms = sem("ms")
        rstd_s = sem("rstd_s")
        xn_s = sem("xn_s")
        par_s = sem("par_s")
        apar_s = sem("apar_s")
        bbar_s = sem("bbar_s")
        ang_s = sem("ang_s")
        turn_s = sem("turn_s")
        bu_s, bu_read = sem("bu_s"), sem("bu_read")
        state_s, prod_s = sem("state_s"), sem("prod_s")
        y_s = sem("y_s")
        gl1, gl2, gl3, gelu_s = sem("gl1"), sem("gl2"), sem("gl3"), sem("gelu_s")
        smax_s, exp_s, prob_s = sem("smax_s"), sem("exp_s"), sem("prob_s")
        merged_s = sem("merged_s")
        xmax_s, xprob_s = sem("xmax_s"), sem("xprob_s")
        rt1, rt2, chosen_s, rounds_s, GT_s = sem("rt1"), sem("rt2"), sem("chosen_s"), sem("rounds_s"), sem("GT_s")
        gu_in = [sem(f"gu_in{k}") for k in range(KD)]
        dn_in = [sem(f"dn_in{k}") for k in range(FF // P)]
        bias_in = sem("bias_in")
        bias_used, gu_used, dn_used = sem("bias_used"), sem("gu_used"), sem("dn_used")
        pick_s, gather_s, xe_s = sem("pick_s"), sem("gather_s"), sem("xe_s")
        gu_read, gate_cs, tanh_s, hid_s = sem("gu_read"), sem("gate_cs"), sem("tanh_s"), sem("hid_s")
        hidT_ps, hidT_s, spT_ps, spT_s, y_ready = sem("hidT_ps"), sem("hidT_s"), sem("spT_ps"), sem("spT_s"), sem("y_ready")
        acc_s, outd, outn = sem("acc_s"), sem("outd"), sem("outn")
        y_zero = sem("y_zero")

        block = ctx.enter_context(nc.Block())

        def bank_of(u):
            return own_bank.get(u, number[u] % MM)

        def arrived(eng, n):
            eng.wait_ge(w_in_s[n % FW], 16 * (n // FW + 1))

        def ready(eng, u):
            eng.wait_ge(mm, number[u] + 1)

        def evacuated(eng, u):
            eng.wait_ge(unit_read[reader[u]], rank[u] + 1)

        def later_rounds(eng, body):
            eng.wait_ge(rounds_s, 1)
            n = eng.value_load(rounds_i[0:1, 0:1], min_val=1, max_val=ROUNDS)
            with eng.Fori(1, ROUNDS) as r:
                with eng.If(n > r):
                    body(r)
            return n

        def expert_loads(sp, i, e, first):
            gu = w_gu[0].rearrange("e (k p) n -> (e k) p n", p=P)
            dn = w_dn[0].rearrange("e (k p) n -> (e k) p n", p=P)
            if not first:
                sp.wait_ge(bias_used, i)
                sp.dma_start(bias_row[0:1, :], b_gu[0, bass.ds(e, 1), :]).then_inc(bias_in, 16)
            for k in range(KD):
                if first:
                    sp.dma_start(gu_ring[k], gu[k]).then_inc(gu_in[k], 16)
                else:
                    sp.wait_ge(gu_used, (i - 1) * KD + k + 1)
                    sp.dma_start(gu_ring[k], gu[bass.ds(e * KD + k, 1)].rearrange("a p n -> p (a n)")).then_inc(gu_in[k], 16)
            for k in range(FF // P):
                if first:
                    sp.dma_start(dn_ring[k], dn[k]).then_inc(dn_in[k], 16)
                else:
                    sp.wait_ge(dn_used, (i - 1) * (FF // P) + k + 1)
                    sp.dma_start(dn_ring[k], dn[bass.ds(e * (FF // P) + k, 1)].rearrange("a p n -> p (a n)")).then_inc(dn_in[k], 16)

        @block.sync
        def _(sp):
            for t in range(TT):
                sp.dma_start(h[:, t, :], x[0, t * P:(t + 1) * P, :]).then_inc(x_in[t], 16)

            def load(n):
                name, cut, c = order[n]
                if n >= FW:
                    if last_user[n - FW] is None:
                        sp.wait_ge(rows_used, last_user[:n - FW + 1].count(None))
                    else:
                        ready(sp, last_user[n - FW])
                w, dst = weights[name], front[n % FW]
                if cut == "rows":
                    sp.dma_start(dst.rearrange("p (k n) -> p k n", k=2),
                                 w.rearrange("(k p) n -> p k n", p=P)[:, c:c + 2, :]).then_inc(w_in_s[n % FW], 16)
                else:
                    k = 8 if cut == "cols" else 4
                    sp.dma_start(dst.rearrange("p (k n) -> p k n", k=k),
                                 w.rearrange("(k p) n -> p k n", p=P)[:, :, c:c + SLOT // k]).then_inc(w_in_s[n % FW], 16)

            load(0)
            sp.wait_ge(cleared, 1)
            for r, src in ((R_ARE, a_re[0].rearrange("(j two) p -> j two p", two=2)),
                           (R_AIM, a_im[0].rearrange("(j two) p -> j two p", two=2))):
                sp.dma_start(rows[r:r + PAIRS, :].rearrange("j (two p) -> j two p", two=2), src).then_inc(rows_in, 16)
            sp.dma_start(ldt[R_LDT:R_LDT + PAIRS, :], log_dt[0].rearrange("(j two) -> j two", two=2)).then_inc(rows_in, 16)
            for i, g in enumerate((g_mix, g_xattn, g_mem, g_moe)):
                sp.dma_start(rows[R_GAIN + i * KD:R_GAIN + (i + 1) * KD, :], g[0].rearrange("(k p) -> k p", p=P)).then_inc(rows_in, 16)
            sp.dma_start(rows[R_DSK:R_DSK + QG, :].rearrange("q (g c) -> q g c", c=GC),
                          d_skip[0].rearrange("(q g) c -> q g c", q=QG)).then_inc(rows_in, 16)
            load(1)
            sp.wait_ge(cleared, 3)
            for w, b in enumerate((b_re, b_im)):
                for two in range(2):
                    sp.dma_start(b_raw[two * NS:(two + 1) * NS, w, :, two * GC:(two + 1) * GC],
                                 b[0].rearrange("(j two) p c -> two p j c", two=2)[two]).then_inc(b_in, 16)
            for w, c in enumerate((c_re, c_im)):
                for dup in range(2):
                    sp.dma_start(c_raw[:, w, :, dup * NS:(dup + 1) * NS],
                                 c[0].rearrange("(q g) c p -> (g c) q p", q=QG)).then_inc(c_in, 16)
            for n in range(2, FW):
                load(n)
            ready(sp, ("nT", 1, 1))
            for t in range(TT):
                sp.dma_start(xn[:, t, :], mem[0, t * P:(t + 1) * P, :]).then_inc(mem_in, 16)
            for n in range(FW, len(order)):
                load(n)
            sp.wait_ge(merged_s, KD)
            expert_loads(sp, 0, 0, True)
            sp.dma_start(router, w_router[0].rearrange("(k p) e -> p k e", p=P)).then_inc(router_in, 16)
            sp.dma_start(bdn[0:E, :], b_dn[0]).then_inc(router_in, 16)
            sp.dma_start(brt[0:1, :], b_router).then_inc(router_in, 16)
            ready(sp, ("xo", TT - 1, 1))
            sp.dma_start(bias_row[0:1, :], b_gu[0, 0:1, :]).then_inc(bias_in, 16)
            sp.dma_start(gfin, g_final.partition_broadcast(P)).then_inc(gfin_in, 16)
            with sp.Fori(1, E) as e:
                expert_loads(sp, e, e, False)

            def again(r):
                with sp.Fori(0, E) as e:
                    expert_loads(sp, r * E + e, e, False)

            later_rounds(sp, again)
            for t in range(TT):
                for hf in range(2):
                    cs = slice(hf * HALF, (hf + 1) * HALF)
                    sp.wait_ge(outd, 2 * t + hf + 1)
                    sp.dma_start(out[0, t * P:(t + 1) * P, cs], h[:, t, cs]).then_inc(outn, 16)
            sp.wait_ge(outn, 16 * TT * 2)

        @block.gpsimd
        def _(pool):
            gp = nc.gpsimd
            gp.memset(rows, 0.0).then_inc(cleared, 1)
            gp.memset(stat, 0.0).then_inc(cleared, 1)
            gp.memset(at(p_base, 1024), 0.0).then_inc(cleared, 1)
            gp.memset(ident, 0.0)
            gp.memset(ones, 1.0)
            gp.memset(mask, 0.0)
            gp.memset(at(ct_base, 3 * PAIRS * 32), 0.0)
            gp.iota(iota16, [[1, 16]], base=0, channel_multiplier=0, allow_small_or_imprecise_dtypes=True)
            gp.iota(slot_no, [[0, 2], [1, SLOTS]], base=0, channel_multiplier=0, allow_small_or_imprecise_dtypes=True)
            pool.drain()
            gp.memset(stat[:, 32:34], -0.5)
            gp.affine_select(out=ident, in_=ident, compare_op=ALU.not_equal, fill=1.0, base=0,
                             pattern=[[-1, P]], channel_multiplier=1)
            gp.affine_select(out=tri, in_=ones, compare_op=ALU.is_gt, fill=0.0, base=0,
                             pattern=[[1, P]], channel_multiplier=-1)
            for c in (0, 256):
                gp.affine_select(out=mask[:, c:c + P], in_=mask[:, c:c + P], compare_op=ALU.is_ge, fill=NEG, base=0,
                                 pattern=[[-1, P]], channel_multiplier=1)
            pool.drain()
            gp.memset(stat[:, 34:35], 0.0).then_inc(consts, 1)

            def root(n):
                for t in range(TT):
                    pool.wait_ge(ms, 2 * n + t - 1)
                    gp.tensor_tensor(stat[:, 4 + t:5 + t], stat[:, 2 + t:3 + t], stat[:, 32:33], ALU.pow).then_inc(rstd_s, 1)

            root(1)
            root(2)
            for j in range(PAIRS):
                pool.wait_ge(state_s, j + 1)
                pool.wait_ge(turn_s, j // 4 + 1)
                if j >= 4:
                    pool.wait_ge(y_s, j // 4)
                else:
                    evacuated(pool, ("C", 1))
                for w in range(2):
                    last = gp.tensor_tensor(prod[:, j % 4, w], state[:, j % 2],
                                            turns[:, j, w, :].unsqueeze(1).broadcast_to((P, 2, S)), ALU.mult)
                last.then_inc(prod_s, 1)
            gp.iota(exp_no, [[1, E]], base=0, channel_multiplier=0, allow_small_or_imprecise_dtypes=True)
            root(3)
            root(4)
            pool.drain()
            gp.memset(stat[:, 35:36], 0.0).then_inc(consts, 1)
            root(5)

        @block.scalar
        def _(act):
            sa = nc.scalar
            def squares(t, src, scratch):
                sa.activation(scratch, src, ACT.Square, accum_out=stat[:, t:t + 1]).then_inc(sq, 1)

            act.wait_ge(cleared, 2)
            sa.activation(stat[:, 42:43], stat[:, 43:44], ACT.Square)
            for t in range(TT):
                act.wait_ge(x_in[t], 16)
                squares(t, h[:, t, :], junk[:, t, :])

            def evacuate(u, dst, scale=1.0, func=ACT.Copy, part=slice(0, P)):
                ready(act, u)
                sa.activation(dst, psum[part, bank_of(u), 0:dst.free_size()], func, scale=scale).then_inc(unit_read["act"], 1)

            act.wait_ge(par_s, 1)
            sa.activation(par[:, 3], cols[:, R_LDT:R_LDT + 16], ACT.Tanh, scale=1.0 / 16).then_inc(apar_s, 1)
            act.wait_ge(par_s, 2)
            sa.activation(par[:, 5], par[:, 4], ACT.Tanh, scale=0.5).then_inc(apar_s, 1)
            act.wait_ge(par_s, 3)
            for w in range(2):
                last = sa.activation(par[:, 8 + w], par[:, 6 + w], ACT.Sin, scale=TWO_PI)
            sa.activation(par[:, 10], par[:, 13], ACT.Sin, scale=TWO_PI / 2).then_inc(apar_s, 1)

            def turn(g):
                act.wait_ge(ang_s, g + 1)
                t = turns[:, 4 * g:4 * g + 4].rearrange("p j c s -> p (j c s)")
                sa.activation(t, t, ACT.Sin, scale=TWO_PI).then_inc(turn_s, 1)

            for c in range(4):
                evacuate(("u", c), uT[:, c, :])
            for c in range(4):
                evacuate(("q", c), qT[:, c, :])
            for c in range(4):
                evacuate(("k", c), kT[:, c, :])
            for hf in range(2):
                for t in range(TT):
                    evacuate(("v", hf, t), v_sb[:, t, hf * 256:(hf + 1) * 256])
                turn(hf)
            act.wait_ge(mem_in, 32)
            for t in range(TT):
                squares(t, xn[:, t, :], junk[:, t, :])
            turn(2)
            turn(3)

            def exps(hd):
                act.wait_ge(smax_s, hd + 1)
                b = sc[:, hd % 2]
                sa.activation(b[:, 0:P], b[:, 0:P], ACT.Exp, bias=stat[:, 12:13] if hd % 2 == 0 else stat[:, 14:15],
                              accum_out=stat[:, 16 + 2 * (hd % 2):17 + 2 * (hd % 2)])
                sa.activation(b[:, P:384], b[:, P:384], ACT.Exp, bias=stat[:, 13:14] if hd % 2 == 0 else stat[:, 15:16],
                              accum_out=stat[:, 17 + 2 * (hd % 2):18 + 2 * (hd % 2)]).then_inc(exp_s, 1)

            def gelu_act(q):
                act.wait_ge(gl1, q + 1)
                sa.activation(gtmp, yskip, ACT.Square).then_inc(gl2, 1)
                act.wait_ge(gl3, q + 1)
                sa.activation(gtmp, gtmp, ACT.Tanh, scale=0.7978845608028654).then_inc(gl2, 1)

            for j in range(STEPS):
                if j % 2 == 0 and j < PAIRS:
                    exps(j // 2)
                if j % 2 == 0 and j >= 2:
                    hd = j // 2 - 1
                    if hd:
                        ready(act, ("O", hd - 1))
                    evacuate(("T", hd), scT)
                if j % 2 == 1 and j >= 3:
                    hd = (j - 3) // 2
                    part = slice(DH * (hd % 2), DH * (hd % 2) + DH)
                    evacuate(("O", hd), attnT[part, hd // 2, :], part=part)
                if j < PAIRS:
                    evacuate(("z", j), gates[:, j, :], scale=0.5, func=ACT.Tanh)
                if j % 4 == 1 and 5 <= j < PAIRS:
                    gelu_act((j - 5) // 4)
            gelu_act(3)
            for c in range(KD):
                if c >= 2:
                    act.wait_ge(merged_s, c - 1)
                evacuate(("zg", c), sc[:, c % 2, 0:S], scale=0.25, func=ACT.Tanh)
            for t in range(TT):
                evacuated(act, ("out", t, 1))
                squares(t, h[:, t, :], xn[:, t, :])
            for c in range(4):
                evacuate(("xk", c), kxT[:, c, :])
            for c in range(4):
                evacuate(("xq", c), attnT[:, c, :])
            for hd in range(XH):
                u = ("XS", hd)
                act.wait_ge(xmax_s, hd + 1)
                for t in range(TT):
                    o = 2 * hd + t
                    last = sa.activation(xp[:, hd, t, :], psum[:, bank_of(u), t * 256:(t + 1) * 256], ACT.Exp,
                                         scale=XDH ** -0.5, bias=xstat[:, 8 + o:9 + o], accum_out=xstat[:, 16 + o:17 + o])
                last.then_inc(unit_read["act"], 1)
            for hf in range(2):
                for t in range(TT):
                    evacuate(("xv", hf, t), vx[:, t, hf * 256:(hf + 1) * 256])

            def xT(hd):
                evacuate(("XT", hd), xpT[:, hd].rearrange("p m s -> p (m s)"))

            xT(0)
            for hd in range(XH):
                if hd + 1 < XH:
                    xT(hd + 1)
                evacuate(("XO", hd), attnT[:, hd, :])
            for t in range(TT):
                evacuated(act, ("xo", t, 1))
                squares(t, h[:, t, :], xn[:, t, :])
            for t in range(TT):
                act.wait_ge(rt1, t + 1)
                last = sa.activation(gate_w[:, t, 0:E], logit[:, t, :], ACT.Exp, bias=stat[:, 36 + t:37 + t])
            last.then_inc(rt2, 1)
            act.wait_ge(y_zero, 1)
            sa.activation(stat[:, 40:41], stat[:, 34:35], ACT.Copy).then_inc(y_ready, 1)

            def expert(i, b):
                act.wait_ge(gate_cs, i + 1)
                sa.activation(gate_t, gate_c, ACT.Tanh, scale=ALPHA / 2).then_inc(tanh_s, 1)
                act.wait_ge(hidT_ps, i + 1)
                sa.activation(hidT.rearrange("p b s -> p (b s)"), psum[:, DN, :], ACT.Copy, scale=0.5).then_inc(hidT_s, 1)
                act.wait_ge(spT_ps, i + 1)
                sa.activation(spreadT[b].rearrange("p t s -> p (t s)"), psum[:, 6, 0:TT * P], ACT.Copy).then_inc(spT_s, 1)
                act.wait_ge(dn_used, (i + 1) * KD)
                sa.activation(y_sb[b], psum[:, DN, :], ACT.Copy).then_inc(y_ready, 1)

            def sweep(r):
                with act.Fori(0, E // 2) as e2:
                    for b in range(2):
                        expert(r * E + e2 * 2 + b, b)

            sweep(0)
            later_rounds(act, sweep)
            for t in range(TT):
                act.wait_ge(acc_s, t + 1)
                squares(t, psum[:, 2 * t:2 * t + 2, :].rearrange("p b n -> p (b n)"), xn[:, t, :])

        @block.vector
        def _(dve):
            ve = nc.vector
            fence = dve.drain

            read = unit_read["dve"]

            def mean_square(n, t):
                dve.wait_ge(sq, 2 * n + t - 1)
                ve.tensor_scalar(stat[:, 2 + t:3 + t], stat[:, t:t + 1], 1.0 / D, EPS, ALU.mult, ALU.add).then_inc(ms, 1)

            def normalise(n, t, src):
                dve.wait_ge(rstd_s, 2 * n + t - 1)
                ve.tensor_scalar(xn[:, t, :], src[:, t, :], stat[:, 4 + t:5 + t], None, ALU.mult).then_inc(xn_s, 1)

            def transposed(name, g, t, dst):
                for kq in range(2):
                    u = (name, t, kq)
                    ready(dve, u)
                    o = R_GAIN + g * KD + 4 * kq
                    ve.tensor_tensor(dst[:, 4 * kq:4 * kq + 4, t * P:(t + 1) * P],
                                     psum[:, bank_of(u), :].rearrange("p (k s) -> p k s", k=4),
                                     cols[:, o:o + 4].unsqueeze(2).broadcast_to((P, 4, P)), ALU.mult).then_inc(read, 1)

            dve.wait_ge(rows_in, 8 * 16)
            dve.wait_ge(consts, 1)
            ve.tensor_copy(rows[R_LDT:R_LDT + PAIRS, :].rearrange("j (two p) -> j two p", two=2),
                           ldt[R_LDT:R_LDT + PAIRS, :].unsqueeze(2).broadcast_to((PAIRS, 2, NS))).then_inc(ldt_rows, 1)
            for t in range(TT):
                mean_square(1, t)
            for t in range(TT):
                normalise(1, t, h)
            ready(dve, ("rows",))
            ve.tensor_copy(cols, psum[:, bank_of(("rows",)), 0:N_ROWS]).then_inc(read, 1)
            fence()
            are, dt, lre, frac = par[:, 0], par[:, 1], par[:, 4], par[:, 2]
            ve.tensor_scalar(are, cols[:, R_ARE:R_ARE + 16], -1e-4, None, ALU.min).then_inc(par_s, 1)
            for t in range(TT):
                transposed("nT", 0, t, nT)
            dve.wait_ge(apar_s, 1)

            def one_over_ratio(dst, t, tmp):
                ve.tensor_scalar(tmp, t, -1.0, 1.0, ALU.mult, ALU.add)
                fence()
                ve.reciprocal(tmp, tmp)
                fence()
                ve.scalar_tensor_tensor(dst, t, 1.0, tmp, ALU.add, ALU.mult)
                fence()

            one_over_ratio(dt, par[:, 3], par[:, 12])
            for _ in range(3):
                ve.tensor_tensor(dt, dt, dt, ALU.mult)
                fence()
            ve.tensor_tensor(lre, are, dt, ALU.mult)
            fence()
            ve.tensor_tensor(frac, cols[:, R_AIM:R_AIM + 16], dt, ALU.mult).then_inc(par_s, 1)
            fence()
            ve.tensor_scalar(frac, frac, 1.0 / 6.283185307179586, None, ALU.mult)
            fence()

            def reduce(dst, src, tmp, add=0.0):
                ve.tensor_scalar(dst, src, 1.0, add, ALU.mult, ALU.add)
                fence()
                ve.tensor_scalar(tmp, dst, ROUND, ROUND, ALU.add, ALU.subtract)
                fence()
                ve.tensor_tensor(dst, dst, tmp, ALU.subtract)
                fence()

            reduce(par[:, 13], frac, par[:, 12])
            reduce(par[:, 6], par[:, 13], par[:, 12], 0.25)
            ve.tensor_copy(par[:, 7], par[:, 13])
            ve.tensor_copy(par[:, 1], par[:, 13]).then_inc(par_s, 1)
            dve.wait_ge(apar_s, 3)
            t_ = par[:, 5]
            ve.tensor_scalar(par[:, 12], t_, -1.0, 1.0, ALU.mult, ALU.add)
            fence()
            ve.reciprocal(par[:, 12], par[:, 12])
            fence()
            decay, rm1 = par[:, 3], par[:, 4]
            ve.scalar_tensor_tensor(decay, t_, 1.0, par[:, 12], ALU.add, ALU.mult)
            ve.scalar_tensor_tensor(rm1, t_, 2.0, par[:, 12], ALU.mult, ALU.mult)
            fence()
            lb_re, lb_im, tmp1, tmp2 = par[:, 5], par[:, 2], par[:, 12], par[:, 11]
            ve.tensor_tensor(lb_re, rm1, par[:, 8], ALU.mult)
            ve.tensor_tensor(tmp1, par[:, 10], par[:, 10], ALU.mult)
            ve.tensor_tensor(lb_im, decay, par[:, 9], ALU.mult)
            fence()
            ve.scalar_tensor_tensor(lb_re, tmp1, -2.0, lb_re, ALU.mult, ALU.add)
            ve.tensor_tensor(tmp2, are, are, ALU.mult)
            ve.tensor_tensor(par[:, 13], cols[:, R_AIM:R_AIM + 16], cols[:, R_AIM:R_AIM + 16], ALU.mult)
            fence()
            ve.tensor_tensor(tmp2, tmp2, par[:, 13], ALU.add)
            fence()
            ve.reciprocal(tmp2, tmp2)
            kre, kim = par[:, 6], par[:, 7]
            aim = cols[:, R_AIM:R_AIM + 16]
            ve.tensor_tensor(kre, lb_re, are, ALU.mult)
            ve.tensor_tensor(tmp1, lb_im, aim, ALU.mult)
            ve.tensor_tensor(kim, lb_im, are, ALU.mult)
            ve.tensor_tensor(par[:, 13], lb_re, aim, ALU.mult)
            fence()
            ve.tensor_tensor(kre, kre, tmp1, ALU.add)
            ve.tensor_tensor(kim, kim, par[:, 13], ALU.subtract)
            fence()
            ve.tensor_tensor(kre, kre, tmp2, ALU.mult)
            ve.tensor_tensor(kim, kim, tmp2, ALU.mult)
            fence()
            dve.wait_ge(b_in, 64)
            kre_b, kim_b = (k.unsqueeze(2).broadcast_to((P, PAIRS, 32)) for k in (kre, kim))
            ve.tensor_tensor(b_bar[:, 0], b_raw[:, 0], kre_b, ALU.mult)
            ve.tensor_tensor(b_tmp[:, 0], b_raw[:, 1], kim_b, ALU.mult)
            ve.tensor_tensor(b_bar[:, 1], b_raw[:, 1], kre_b, ALU.mult)
            ve.tensor_tensor(b_tmp[:, 1], b_raw[:, 0], kim_b, ALU.mult)
            fence()
            ve.tensor_tensor(b_bar[:, 0], b_bar[:, 0], b_tmp[:, 0], ALU.subtract)
            ve.tensor_tensor(b_bar[:, 1], b_bar[:, 1], b_tmp[:, 1], ALU.add).then_inc(bbar_s, 1)
            for w in range(2):
                u = ("Bd", w)
                ready(dve, u)
                ve.tensor_copy(Bd[:, w], psum[:, bank_of(u), :].rearrange("p (q m) -> p q m", q=QG)).then_inc(read, 1)
            for w in range(2):
                u = ("C", w)
                ready(dve, u)
                for two in range(2):
                    sl = slice(two * NS, (two + 1) * NS)
                    src = psum[sl, bank_of(u), :].rearrange("p (j m) -> p j m", j=PAIRS)[:, :, two * GC:(two + 1) * GC]
                    dst = Ct[sl, :, :, two * GC:(two + 1) * GC]
                    if w == 0:
                        ve.tensor_copy(dst[:, 0], src)
                        last = ve.tensor_scalar(dst[:, 1], src, -1.0, None, ALU.mult)
                    else:
                        last = ve.tensor_scalar(dst[:, 2], src, -1.0, None, ALU.mult)
                last.then_inc(read, 1)
            fence()
            ve.tensor_scalar(par[:, 0], par[:, 1], 16.0, None, ALU.mult)
            fence()
            reduce(par[:, 0], par[:, 0], par[:, 12])
            big = whole[:, 0:256].rearrange("p (j a) -> p j a", j=PAIRS)
            it = iota16.unsqueeze(1).broadcast_to((P, PAIRS, 16))
            ta = whole[:, 256:512].rearrange("p (j a) -> p j a", j=PAIRS)
            ve.tensor_tensor(ta, par[:, 0].unsqueeze(2).broadcast_to((P, PAIRS, 16)), it, ALU.mult)
            ve.tensor_tensor(turn_b, par[:, 1].unsqueeze(2).broadcast_to((P, PAIRS, 16)), it, ALU.mult)
            fence()
            reduce(turn_b, turn_b, big)
            for c, add in ((0, 0.25), (1, 0.0)):
                reduce(turn_a[:, :, c, :], ta, big, add)
            fence()
            for g in range(4):
                js = slice(4 * g, 4 * g + 4)
                four = turns[:, js].rearrange("p j c s -> p (j c s)")
                for c in range(2):
                    ve.tensor_tensor(turns[:, js, c, :].rearrange("p j (a b) -> p j a b", a=16),
                                     turn_a[:, js, c, :].unsqueeze(3).broadcast_to((P, 4, 16, 16)),
                                     turn_b[:, js, :].unsqueeze(2).broadcast_to((P, 4, 16, 16)), ALU.add)
                fence()
                ve.tensor_scalar(whole, four, ROUND, ROUND, ALU.add, ALU.subtract)
                fence()
                ve.tensor_tensor(four, four, whole, ALU.subtract).then_inc(ang_s, 1)
            for t in range(TT):
                mean_square(2, t)
            for t in range(TT):
                normalise(2, t, xn)

            def scan(j):
                bank = BU + j % 2
                dve.wait_ge(bu_s, j + 1)
                dve.wait_ge(turn_s, j // 4 + 1)
                bu = psum[:, bank, :].rearrange("p (c s) -> p c s", c=2)
                ve.tensor_tensor(m_cos, bu, turns[:, j, 0, :].unsqueeze(1).broadcast_to((P, 2, S)), ALU.mult)
                ve.tensor_tensor(m_sin, bu, turns[:, j, 1, :].unsqueeze(1).broadcast_to((P, 2, S)), ALU.mult).then_inc(bu_read, 1)
                fence()
                ve.tensor_tensor(drive[:, 0], m_cos[:, 0], m_sin[:, 1], ALU.add)
                ve.tensor_tensor(drive[:, 1], m_cos[:, 1], m_sin[:, 0], ALU.subtract)
                fence()
                if j >= 2:
                    dve.wait_ge(prod_s, j - 1)
                for c in range(2):
                    last = ve.tensor_tensor_scan(state[:, j % 2, c], decay[:, j:j + 1].broadcast_to((P, S)), drive[:, c],
                                                 0.0, ALU.mult, ALU.add)
                last.then_inc(state_s, 1)

            def softmax_head(hd):
                u = ("S", hd)
                ready(dve, u)
                b = sc[:, hd % 2]
                if hd >= 2:
                    dve.wait_ge(mm, number[("T", hd - 2)] + 1)
                ve.scalar_tensor_tensor(b, psum[:, bank_of(u), 0:384], DH ** -0.5, mask, ALU.mult, ALU.add).then_inc(read, 1)
                fence()
                o = 12 + 2 * (hd % 2)
                ve.reduce_max(stat[:, 8:9], b[:, 0:P], AX)
                ve.reduce_max(stat[:, 9:10], b[:, P:384], AX)
                fence()
                ve.tensor_scalar(stat[:, o:o + 2], stat[:, 8:10], -1.0, None, ALU.mult).then_inc(smax_s, 1)

            def normalise_head(hd):
                dve.wait_ge(exp_s, hd + 1)
                b = sc[:, hd % 2]
                o = 16 + 2 * (hd % 2)
                ve.reciprocal(stat[:, 10:12], stat[:, o:o + 2])
                fence()
                ve.tensor_scalar(b[:, 0:P], b[:, 0:P], stat[:, 10:11], None, ALU.mult)
                ve.tensor_scalar(b[:, P:384], b[:, P:384], stat[:, 11:12], None, ALU.mult).then_inc(prob_s, 1)

            def gelu_dve(q):
                dve.wait_ge(y_s, q + 1)
                if q:
                    fence()
                ve.scalar_tensor_tensor(yskip, uT[:, q, :], cols[:, R_DSK + q:R_DSK + q + 1], psum[:, Y, 0:S],
                                        ALU.mult, ALU.add).then_inc(gl1, 1)
                dve.wait_ge(gl2, 2 * q + 1)
                ve.tensor_scalar(gtmp, gtmp, 0.044715, 1.0, ALU.mult, ALU.add)
                fence()
                ve.tensor_tensor(gtmp, gtmp, yskip, ALU.mult).then_inc(gl3, 1)
                dve.wait_ge(gl2, 2 * q + 2)
                ve.scalar_tensor_tensor(geluT[:, q, :], gtmp, 1.0, yskip, ALU.add, ALU.mult).then_inc(gelu_s, 1)

            for j in range(STEPS):
                if j < PAIRS:
                    scan(j)
                if j % 2 == 0 and j < PAIRS:
                    softmax_head(j // 2)
                if j % 2 == 1 and j < PAIRS:
                    normalise_head(j // 2)
                if j % 4 == 1 and 5 <= j < PAIRS:
                    gelu_dve((j - 5) // 4)
                if j == PAIRS:
                    for t in range(TT):
                        transposed("memT", 2, t, nT)
            for c in range(KD):
                if c == 4:
                    gelu_dve(3)
                u = ("ya", c)
                ready(dve, u)
                evacuated(dve, ("z", PAIRS - 1))
                ve.scalar_tensor_tensor(gates[:, c, :], gates[:, c, :], 1.0, psum[:, bank_of(u), 0:S],
                                        ALU.add, ALU.mult).then_inc(read, 1)
            for c in range(KD):
                u = ("zb", c)
                evacuated(dve, ("zg", c))
                fence()
                ve.scalar_tensor_tensor(yskip, sc[:, c % 2, 0:S], 1.0, psum[:, bank_of(u), 0:S],
                                        ALU.add, ALU.mult).then_inc(read, 1)
                fence()
                ve.scalar_tensor_tensor(gtmp, gates[:, KD + c, :], 1.0, yskip, ALU.add, ALU.mult)
                fence()
                ve.tensor_scalar(gtmp, gtmp, 0.125, None, ALU.mult)
                fence()
                ve.scalar_tensor_tensor(mergedT[:, c, :], gates[:, c, :], 0.5, gtmp, ALU.mult, ALU.add).then_inc(merged_s, 1)

            def residual_norm(name, n, first_tile):
                for t in range(TT):
                    for hf in range(2):
                        u = (name, t, hf)
                        ready(dve, u)
                        cs = slice(hf * HALF, (hf + 1) * HALF)
                        ve.tensor_tensor(h[:, t, cs], h[:, t, cs], psum[:, bank_of(u), :], ALU.add).then_inc(read, 1)
                    if t:
                        transposed(*first_tile)
                    mean_square(n, t)
                    normalise(n, t, h)

            residual_norm("out", 3, ("n2T", 1, 0, n2T))
            transposed("n2T", 1, 1, n2T)
            for hd in range(XH):
                u = ("XS", hd)
                ready(dve, u)
                ve.tensor_reduce(xstat[:, 2 * hd:2 * hd + 2], psum[:, bank_of(u), :].rearrange("p (t s) -> p t s", t=TT), AX, ALU.max)
                fence()
                ve.tensor_scalar(xstat[:, 8 + 2 * hd:10 + 2 * hd], xstat[:, 2 * hd:2 * hd + 2], -XDH ** -0.5, None, ALU.mult).then_inc(xmax_s, 1)
            for hd in range(XH):
                evacuated(dve, ("XS", hd))
                ve.reciprocal(xstat[:, 24 + 2 * hd:26 + 2 * hd], xstat[:, 16 + 2 * hd:18 + 2 * hd])
                fence()
                for t in range(TT):
                    last = ve.tensor_scalar(xp[:, hd, t, :], xp[:, hd, t, :], xstat[:, 24 + 2 * hd + t:25 + 2 * hd + t], None, ALU.mult)
                last.then_inc(xprob_s, 1)
            residual_norm("xo", 4, ("n3T", 3, 0, nT))
            ve.memset(y_sb[0], 0.0).then_inc(gu_read, 1)
            ve.memset(y_sb[1], 0.0)
            transposed("n3T", 3, 1, nT)
            ve.memset(spreadT[0], 0.0)
            ve.memset(spreadT[1], 0.0).then_inc(y_zero, 1)

            dve.wait_ge(consts, 2)
            for t in range(TT):
                u = ("logits", t)
                ready(dve, u)
                ve.tensor_copy(logit[:, t, :], psum[:, bank_of(u), 0:E]).then_inc(read, 1)
                fence()
                ve.max(top8[:, t, :], logit[:, t, :])
                fence()
                ve.tensor_scalar(stat[:, 36 + t:37 + t], top8[:, t, 0:1], -1.0, None, ALU.mult).then_inc(rt1, 1)
                ve.max_index(topi[:, t, :], top8[:, t, :], logit[:, t, :])
                fence()
                ve.tensor_copy(topf[:, t, :], topi[:, t, :])
                fence()
                ve.tensor_scalar(chosen[:, t, :], exp_no, topf[:, t, 0:1], None, ALU.is_equal)
                for n in range(1, TOPK):
                    fence()
                    last = ve.scalar_tensor_tensor(chosen[:, t, :], exp_no, topf[:, t, n:n + 1], chosen[:, t, :],
                                                   ALU.is_equal, ALU.add)
                last.then_inc(chosen_s, 1)
            fence()
            dve.wait_ge(rt2, 1)
            ve.tensor_tensor(gate_w[:, :, 0:E], gate_w[:, :, 0:E], chosen, ALU.mult)
            fence()
            ve.tensor_reduce(stat[:, 46:48], gate_w[:, :, 0:E], AX, ALU.add)
            fence()
            ve.reciprocal(stat[:, 46:48], stat[:, 46:48])
            fence()
            for t in range(TT):
                ve.tensor_scalar(gate_w[:, t, 0:E], gate_w[:, t, 0:E], stat[:, 46 + t:47 + t], None, ALU.mult)
            fence()
            ve.tensor_copy(gate_w[:, :, E:E + 1], gate_w[:, :, 0:1]).then_inc(rt1, 1)
            u = ("pos",)
            ready(dve, u)
            pp = psum[:, bank_of(u), 0:3 * E].rearrange("p (t e) -> p t e", t=3)
            ve.scalar_tensor_tensor(pos[:, :, 0:E], pp[:, 0:2, :], OFF, chosen, ALU.add, ALU.mult)
            ve.reduce_max(stat[:, 48:49], pp[:, 2, :], AX).then_inc(read, 1)
            fence()
            ve.tensor_scalar(pos[:, :, 0:E], pos[:, :, 0:E], OFF, None, ALU.subtract)
            ve.tensor_scalar(stat[:, 49:50], stat[:, 48:49], float(SLOTS), 1.0, ALU.is_gt, ALU.add)
            fence()
            for r in range(2, ROUNDS):
                ve.scalar_tensor_tensor(stat[:, 49:50], stat[:, 48:49], float(r * SLOTS), stat[:, 49:50], ALU.is_gt, ALU.add)
                fence()
            ve.tensor_scalar(pos[:, :, E:E + 1], pos[:, :, 0:1], float(SLOTS), None, ALU.subtract)
            ve.tensor_copy(rounds_i[:, :], stat[:, 49:50]).then_inc(rounds_s, 1)
            u = ("GT",)
            ready(dve, u)
            ve.tensor_copy(GT[0:E, :], psum[0:E, bank_of(u), 0:S]).then_inc(GT_s, 1)
            fence()
            gain_e = cols[:, R_GAIN + 3 * KD:R_GAIN + 4 * KD].unsqueeze(2).broadcast_to((P, KD, SLOTS))

            def one_hots(col, b):
                for t in range(TT):
                    ve.tensor_scalar(pick[b][:, t, :], slot_no[:, 0:SLOTS], pos[:, t, col], None, ALU.is_equal)
                for t in range(TT):
                    last = ve.tensor_scalar(spread[b][:, t, :], slot_no, pos[:, t, col], gate_w[:, t, col],
                                            ALU.is_equal, ALU.mult)
                last.then_inc(pick_s, 1)

            def gathered(i, b):
                dve.wait_ge(gather_s, i + 1)
                ve.tensor_tensor(xeT[b], psum[:, 6, :].rearrange("p (k s) -> p k s", k=KD), gain_e, ALU.mult).then_inc(xe_s, 1)

            one_hots(slice(0, 1), 0)
            gathered(0, 0)

            def expert(i, e, b):
                dve.wait_ge(gu_used, i * KD + 1)
                one_hots(bass.ds(e + 1, 1), 1 - b)
                gathered(i + 1, 1 - b)
                dve.wait_ge(gu_used, (i + 1) * KD)
                ve.tensor_scalar(gate_c, psum[:, 4, :], LIMIT, None, ALU.min).then_inc(gate_cs, 1)
                ve.tensor_scalar(up_c, psum[:, 5, :], LIMIT, -LIMIT, ALU.min, ALU.max).then_inc(gu_read, 1)
                fence()
                ve.scalar_tensor_tensor(gated, up_c, 1.0, gate_c, ALU.add, ALU.mult)
                fence()
                dve.wait_ge(tanh_s, i + 1)
                ve.scalar_tensor_tensor(hid, gate_t, 1.0, gated, ALU.add, ALU.mult).then_inc(hid_s, 1)

            def sweep(r):
                with dve.Fori(0, E // 2) as e2:
                    for b in range(2):
                        expert(r * E + e2 * 2 + b, e2 * 2 + b, b)

            def later(r):
                fence()
                ve.tensor_scalar(pos, pos, float(SLOTS), None, ALU.subtract)
                fence()
                sweep(r)

            sweep(0)
            later_rounds(dve, later)
            for t in range(TT):
                mean_square(5, t)
            dve.wait_ge(gfin_in, 16)
            for t in range(TT):
                dve.wait_ge(rstd_s, 9 + t)
                for hf in range(2):
                    cs = slice(hf * HALF, (hf + 1) * HALF)
                    ve.scalar_tensor_tensor(h[:, t, cs], psum[:, 2 * t + hf, :], stat[:, 4 + t:5 + t], gfin[:, cs],
                                            ALU.mult, ALU.mult).then_inc(outd, 1)

        @block.tensor
        def _(pe):
            te = nc.tensor
            done_blocks = [0]

            def open_unit(u):
                if number[u] >= MM:
                    evacuated(pe, plan[number[u] - MM][0])
                return psum[:, bank_of(u), :]

            def transposes(name, n_norm, t):
                for kq in range(2):
                    ps = open_unit((name, t, kq))
                    pe.wait_ge(xn_s, 2 * n_norm + t - 1)
                    for k in range(4):
                        last = te.transpose(ps[:, k * P:(k + 1) * P], xn[:, t, (4 * kq + k) * P:(4 * kq + k + 1) * P], ident)
                    last.then_inc(mm, 1)

            def next_block():
                n = done_blocks[0]
                done_blocks[0] += 1
                arrived(pe, n)
                return front[n % FW]

            def column_unit(u, w, c, rhs, kn):
                ps = open_unit(u)
                for k in range(kn):
                    last = te.matmul(ps[:, 0:S], w[:, k, c * P:(c + 1) * P], rhs[:, k, :], start=(k == 0), stop=(k == kn - 1))
                last.then_inc(mm, 1)

            pe.wait_ge(consts, 1)
            ps = open_unit(("rows",))
            pe.wait_ge(ldt_rows, 1)
            te.transpose(ps[:, 0:N_ROWS], rows[0:N_ROWS, :], ident[0:N_ROWS, 0:N_ROWS]).then_inc(mm, 1)
            for t in range(TT):
                transposes("nT", 1, t)
            def parameters():
                for w in range(2):
                    ps = open_unit(("Bd", w))
                    pe.wait_ge(bbar_s, 1)
                    for q in range(QG):
                        last = te.transpose(ps[:, q * P:(q + 1) * P], b_bar[:, w, 4 * q:4 * q + 4, :].rearrange("p j c -> p (j c)"), ident)
                    last.then_inc(mm, 1)
                for w in range(2):
                    ps = open_unit(("C", w))
                    pe.wait_ge(c_in, 64)
                    for q in range(QG):
                        last = te.transpose(ps[:, q * P:(q + 1) * P], c_raw[:, w, q, :], ident)
                    last.then_inc(mm, 1)

            evacuated(pe, ("nT", 1, 1))
            for name in ("u", "q", "k"):
                for hf in range(2):
                    w = next_block().rearrange("p (k n) -> p k n", k=KD)
                    for c in range(2):
                        column_unit((name, 2 * hf + c), w, c, nT, KD)
                if name == "q":
                    parameters()
            for hf in range(2):
                w = next_block().rearrange("p (k n) -> p k n", k=KD)
                for t in range(TT):
                    u = ("v", hf, t)
                    ps = open_unit(u)
                    for k in range(KD):
                        last = te.matmul(ps[:, 0:256], nT[:, k, t * P:(t + 1) * P], w[:, k, :], start=(k == 0), stop=(k == KD - 1))
                    last.then_inc(mm, 1)
            evacuated(pe, ("Bd", 1))

            def drive_in(j):
                if j >= 2:
                    pe.wait_ge(bu_read, j - 1)
                if j % 4 == 0:
                    evacuated(pe, ("u", j // 4))
                o = 32 * (j % 4)
                for w in range(2):
                    last = te.matmul(psum[:, BU + j % 2, w * S:(w + 1) * S], Bd[o:o + 32, w, j // 4, :],
                                     uT[o:o + 32, j // 4, :], start=True, stop=True)
                last.then_inc(bu_s, 1)

            def y_out(q):
                pe.wait_ge(prod_s, 4 * (q + 1))
                if q == 0:
                    evacuated(pe, ("C", 1))
                else:
                    pe.wait_ge(gl1, q)
                for n, (w, m, c) in enumerate(((0, 0, 0), (2, 0, 1), (1, 1, 1), (2, 1, 0))):
                    for jj in range(4):
                        last = te.matmul(psum[32 * jj:32 * jj + 32, Y, 0:S], Ct[:, w, 4 * q + jj, :], prod[:, jj, m, c, :],
                                         start=(n == 0), stop=(n == 3))
                last.then_inc(y_s, 1)

            def scores(hd):
                ps = open_unit(("S", hd))
                o, c = DH * (hd % 2), hd // 2
                if hd % 2 == 0:
                    evacuated(pe, ("k", c))
                te.matmul(ps[:, 0:P], qT[o:o + DH, c, 0:P], kT[o:o + DH, c, 0:P], start=True, stop=True)
                te.matmul(ps[:, P:384], qT[o:o + DH, c, P:S], kT[o:o + DH, c, :], start=True, stop=True).then_inc(mm, 1)

            def probs_T(hd):
                ps = open_unit(("T", hd))
                pe.wait_ge(prob_s, hd + 1)
                b = sc[:, hd % 2]
                for n in range(3):
                    last = te.transpose(ps[:, n * P:(n + 1) * P], b[:, n * P:(n + 1) * P], ident)
                last.then_inc(mm, 1)

            def weighted(hd):
                open_unit(("O", hd))
                evacuated(pe, ("T", hd))
                evacuated(pe, ("v", 1, 1))
                o = DH * (hd % 2)
                ps = psum[o:o + DH, bank_of(("O", hd)), :]
                te.matmul(ps[:, 0:S], v_sb[:, 0, hd * DH:(hd + 1) * DH], scT[:, 0:S], start=True, stop=False)
                te.matmul(ps[:, P:S], v_sb[:, 1, hd * DH:(hd + 1) * DH], scT[:, S:384], start=False, stop=True).then_inc(mm, 1)

            for j in range(STEPS):
                if j < PAIRS:
                    drive_in(j)
                if j % 2 == 0 and j < PAIRS:
                    scores(j // 2)
                if j % 2 == 0 and j >= 2:
                    probs_T(j // 2 - 1)
                if j % 2 == 1 and j >= 3:
                    weighted((j - 3) // 2)
                if j < PAIRS:
                    if j % 2 == 0:
                        w = next_block().rearrange("p (k n) -> p k n", k=KD)
                    column_unit(("z", j), w, j % 2, nT, KD)
                if j == PAIRS:
                    for t in range(TT):
                        transposes("memT", 2, t)
                if j % 4 == 0 and 4 <= j < PAIRS:
                    y_out((j - 4) // 4)
            evacuated(pe, ("O", HEADS - 1))
            for hf in range(2):
                w = next_block().rearrange("p (k n) -> p k n", k=4)
                for c in range(4):
                    column_unit(("ya", 4 * hf + c), w, c, attnT, 4)
                if hf == 0:
                    y_out(3)
            pe.wait_ge(gelu_s, 4)
            for hf in range(2):
                wa = next_block().rearrange("p (k n) -> p k n", k=4)
                wb = next_block().rearrange("p (k n) -> p k n", k=4)
                for c in range(4):
                    column_unit(("zb", 4 * hf + c), wa, c, geluT, 4)
                    column_unit(("zg", 4 * hf + c), wb, c, geluT, 4)

            def rows_out(name, src, blocks, source_ready):
                ws = [next_block().rearrange("p (k n) -> p k n", k=2) for _ in range(blocks)]
                for t in range(TT):
                    for hf in range(2):
                        open_unit((name, t, hf))
                    for k in range(2 * blocks):
                        source_ready(k)
                        for hf in range(2):
                            last = te.matmul(psum[:, bank_of((name, t, hf)), :], src[:, k, t * P:(t + 1) * P],
                                             ws[k // 2][:, k % 2, hf * HALF:(hf + 1) * HALF],
                                             start=(k == 0), stop=(k == 2 * blocks - 1))
                            if k == 2 * blocks - 1:
                                last.then_inc(mm, 1)
                        if t == TT - 1 and k % 2 == 1 and k < 2 * blocks - 1:
                            last.then_inc(rows_used, 1)

            rows_out("out", mergedT, 4, lambda k: pe.wait_ge(merged_s, k + 1))
            transposes("n2T", 3, 0)
            for hf in range(2):
                w = next_block().rearrange("p (k n) -> p k n", k=KD)
                for c in range(2):
                    if hf == c == 0:
                        evacuated(pe, ("memT", 1, 1))
                    column_unit(("xk", 2 * hf + c), w, c, nT, KD)
            transposes("n2T", 3, 1)
            evacuated(pe, ("n2T", 1, 1))
            for hf in range(2):
                w = next_block().rearrange("p (k n) -> p k n", k=KD)
                for c in range(2):
                    column_unit(("xq", 2 * hf + c), w, c, n2T, KD)
            for hd in range(XH):
                ps = open_unit(("XS", hd))
                evacuated(pe, ("xq", hd))
                for t in range(TT):
                    last = te.matmul(ps[:, t * S:(t + 1) * S], attnT[:, hd, t * P:(t + 1) * P], kxT[:, hd, :], start=True, stop=True)
                last.then_inc(mm, 1)
            for hf in range(2):
                w = next_block().rearrange("p (k n) -> p k n", k=KD)
                for t in range(TT):
                    ps = open_unit(("xv", hf, t))
                    for k in range(KD):
                        last = te.matmul(ps[:, 0:256], nT[:, k, t * P:(t + 1) * P], w[:, k, :], start=(k == 0), stop=(k == KD - 1))
                    last.then_inc(mm, 1)

            def xprobs_T(hd):
                ps = open_unit(("XT", hd))
                pe.wait_ge(xprob_s, hd + 1)
                for m in range(TT):
                    for t in range(TT):
                        last = te.transpose(ps[:, m * S + t * P:m * S + (t + 1) * P], xp[:, hd, t, m * P:(m + 1) * P], ident)
                last.then_inc(mm, 1)

            xprobs_T(0)
            for hd in range(XH):
                if hd + 1 < XH:
                    xprobs_T(hd + 1)
                ps = open_unit(("XO", hd))
                evacuated(pe, ("XT", hd))
                for m in range(TT):
                    last = te.matmul(ps[:, 0:S], vx[:, m, hd * XDH:(hd + 1) * XDH], xpT[:, hd, m, :], start=(m == 0), stop=(m == 1))
                last.then_inc(mm, 1)
            rows_out("xo", attnT, 2, lambda k: evacuated(pe, ("XO", k)))
            for t in range(TT):
                transposes("n3T", 4, t)
                ps = open_unit(("logits", t))
                pe.wait_ge(router_in, 48)
                evacuated(pe, ("n3T", t, 1))
                for k in range(KD):
                    te.matmul(ps[:, 0:E], nT[:, k, t * P:(t + 1) * P], router[:, k, :], start=(k == 0), stop=False)
                te.matmul(ps[:, 0:E], ones[0:1, 0:P], brt[0:1, :], start=False, stop=True).then_inc(mm, 1)
            for t in range(TT):
                for hf in range(2):
                    te.matmul(psum[:, 2 * t + hf, :], ident, h[:, t, hf * HALF:(hf + 1) * HALF], start=True, stop=False)
            ps = open_unit(("pos",))
            pe.wait_ge(chosen_s, TT)
            te.matmul(ps[:, 0:E], tri, chosen[:, 0, :], start=True, stop=True)
            te.matmul(ps[:, E:2 * E], ones, chosen[:, 0, :], start=True, stop=False)
            te.matmul(ps[:, E:2 * E], tri, chosen[:, 1, :], start=False, stop=True)
            te.matmul(ps[:, 2 * E:3 * E], ones, chosen[:, 0, :], start=True, stop=False)
            te.matmul(ps[:, 2 * E:3 * E], ones, chosen[:, 1, :], start=False, stop=True).then_inc(mm, 1)
            ps = open_unit(("GT",))
            pe.wait_ge(rt1, TT + 1)
            for t in range(TT):
                last = te.transpose(ps[0:E, t * P:(t + 1) * P], gate_w[:, t, 0:E], ident)
            last.then_inc(mm, 1)

            def gather(i, b):
                pe.wait_ge(pick_s, i + 1)
                for k in range(KD):
                    for t in range(TT):
                        last = te.matmul(psum[:, 6, k * SLOTS:(k + 1) * SLOTS], xn[:, t, k * P:(k + 1) * P], pick[b][:, t, :],
                                         start=(t == 0), stop=(t == TT - 1))
                last.then_inc(gather_s, 1)

            gather(0, 0)
            pe.wait_ge(GT_s, 1)
            for t in range(TT):
                for hf in range(2):
                    cs = slice(hf * HALF, (hf + 1) * HALF)
                    te.matmul(psum[:, 2 * t + hf, :], GT[0:E, t * P:(t + 1) * P], bdn[0:E, cs], start=False, stop=False,
                              skip_group_check=True)

            def combine(b, tile, stop=False):
                for hf in range(2):
                    last = te.matmul(psum[:, 2 * tile + hf, :], spreadT[b][hf * SLOTS:(hf + 1) * SLOTS, tile, :],
                                     y_sb[b][hf * SLOTS:(hf + 1) * SLOTS, :], start=False, stop=stop, skip_group_check=not stop)
                return last

            def expert(i, b):
                pe.wait_ge(gu_read, i + 1)
                pe.wait_ge(xe_s, i + 1)
                pe.wait_ge(bias_in, 16 * (i + 1))
                for gu in range(2):
                    for hf in range(2):
                        last = te.matmul(psum[hf * SLOTS:(hf + 1) * SLOTS, 4 + gu, :], ones[0:1, 0:SLOTS],
                                         bias_row[0:1, gu * FF + hf * HALF:gu * FF + (hf + 1) * HALF], start=True, stop=False)
                last.then_inc(bias_used, 1)
                for k in range(KD):
                    pe.wait_ge(gu_in[k], 16 * (i + 1))
                    for gu in range(2):
                        for hf in range(2):
                            last = te.matmul(psum[hf * SLOTS:(hf + 1) * SLOTS, 4 + gu, :], xeT[b][:, k, :],
                                             gu_ring[k][:, gu * FF + hf * HALF:gu * FF + (hf + 1) * HALF],
                                             start=False, stop=(k == KD - 1))
                    last.then_inc(gu_used, 1)
                    if k == 4:
                        pe.wait_ge(y_ready, i + 1)
                        gather(i + 1, 1 - b)
                for t in range(TT):
                    combine(1 - b, t)
                pe.wait_ge(xe_s, i + 2)
                for t in range(TT):
                    last = te.transpose(psum[:, 6, t * P:(t + 1) * P], spread[b][:, t, :], ident)
                last.then_inc(spT_ps, 1)
                pe.wait_ge(hid_s, i + 1)
                for n in range(4):
                    last = te.transpose(psum[:, DN, n * P:(n + 1) * P], hid[:, n * P:(n + 1) * P], ident)
                last.then_inc(hidT_ps, 1)
                pe.wait_ge(hidT_s, i + 1)
                for k in range(FF // P):
                    pe.wait_ge(dn_in[k], 16 * (i + 1))
                    n, c = k % 4, k // 4
                    for hf in range(2):
                        last = te.matmul(psum[hf * SLOTS:(hf + 1) * SLOTS, DN, :], hidT[:, n, c * SLOTS:(c + 1) * SLOTS],
                                         dn_ring[k][:, hf * HALF:(hf + 1) * HALF], start=(k == 0), stop=(k == FF // P - 1))
                    last.then_inc(dn_used, 1)

            def sweep(r):
                with pe.Fori(0, E // 2) as e2:
                    for b in range(2):
                        expert(r * E + e2 * 2 + b, b)

            sweep(0)
            n = later_rounds(pe, sweep)
            pe.wait_ge(y_ready, n * E + 1)
            for t in range(TT):
                combine(1, t, True).then_inc(acc_s, 1)


_INS = ["x", "mem", "g_mix", "w_in", "a_re", "a_im", "log_dt", "b_re", "b_im", "c_re", "c_im", "d_skip", "w_glu",
        "w_proj_a", "w_out", "g_xattn", "g_mem", "w_xq", "w_xkv", "w_xo", "g_moe", "w_router", "b_router", "w_gu",
        "b_gu", "w_dn", "b_dn", "g_final"]


def kernel(**inputs):
    import numpy as _np
    import concourse.bacc as _bacc
    from concourse import mybir as _mybir
    from concourse.bass_utils import run_bass_kernel_spmd as _run

    nc = _bacc.Bacc("TRN2", target_bir_lowering=False, num_devices=1)
    arrays, args = {}, []
    for name in _INS:
        a = _np.ascontiguousarray(inputs[name])
        arrays[f"in_{name}"] = a
        args.append(nc.dram_tensor(f"in_{name}", a.shape, _mybir.dt.from_np(a.dtype), kind="ExternalInput").ap())
    out = nc.dram_tensor("out_dram", (1, S, D), F32, kind="ExternalOutput").ap()
    build_layer(nc, *args, out)
    r = _run(nc, [arrays], core_ids=[0])
    return r.results[0]["out_dram"]
```

```python
from contextlib import ExitStack

import concourse.bass as bass
from concourse import mybir

F32 = mybir.dt.float32
BF16 = mybir.dt.bfloat16
I32 = mybir.dt.int32
U32 = mybir.dt.uint32
ALU = mybir.AluOpType
ACT = mybir.ActivationFunctionType
AX = mybir.AxisListType.X

P = 128
D = 1024
S = 256
TT = S // P
KD = D // P
HEADS, DH = 8, 64
XH, XDH = 4, 128
G, NS, GC = 32, 64, 16
PAIRS = G // 2
QG = 4
E, TOPK, FF = 32, 4, 1024
SLOTS = 64
ROUNDS = S // SLOTS
AHEAD = 16
HALF = 512
EPS = 1e-6
NEG = -1e30
LIMIT, ALPHA = 7.0, 1.702
ROUND = 12582912.0
TWO_PI = 6.2831850
OFF = 16384.0
FW = 6
SLOT = 2048
STEPS = PAIRS + 2
MM = 4

R_ARE, R_LDT, R_DSK, R_AIM, R_GAIN = 0, 32, 48, 64, 80
N_ROWS = R_GAIN + 4 * KD


def dense_weights():
    order = [("w_in", "cols", 1536 + 256 * i) for i in range(2)]
    order += [("w_in", "cols", 256 * i) for i in range(6)]
    order += [("w_in", "cols", 2048 + 256 * i) for i in range(8)]
    order += [("w_proj_a", "wide", 512 * i) for i in range(2)]
    order += [("w_glu", "wide", c) for c in (0, 1024, 512, 1536)]
    order += [("w_out", "rows", 2 * i) for i in range(4)]
    order += [("w_xkv", "cols", 256 * i) for i in range(2)]
    order += [("w_xq", "cols", 256 * i) for i in range(2)]
    order += [("w_xkv", "cols", 512 + 256 * i) for i in range(2)]
    order += [("w_xo", "rows", 2 * i) for i in range(2)]
    return order


def last_units():
    out = [("u", 1), ("u", 3), ("q", 1), ("q", 3), ("k", 1), ("k", 3), ("v", 0, 1), ("v", 1, 1)]
    out += [("z", c) for c in range(1, PAIRS, 2)]
    out += [("ya", 3), ("ya", 7), ("zb", 3), ("zg", 3), ("zb", 7), ("zg", 7)]
    out += [None, None, None, ("out", 1, 1), ("xk", 1), ("xk", 3), ("xq", 1), ("xq", 3), ("xv", 0, 1), ("xv", 1, 1)]
    return out + [None, ("xo", 1, 1)]


def units():
    def tiles(name, t):
        return [((name, t, kq), "dve") for kq in range(2)]

    out = tiles("nT", 0) + [(("rows",), "dve")] + tiles("nT", 1)
    out += [(("u", c), "act") for c in range(4)] + [(("q", c), "act") for c in range(4)]
    out += [(("Bd", 0), "dve"), (("Bd", 1), "dve"), (("C", 0), "dve"), (("C", 1), "dve")]
    out += [(("k", c), "act") for c in range(4)] + [(("v", hf, t), "act") for hf in range(2) for t in range(TT)]
    for j in range(STEPS):
        if j % 2 == 0 and j < PAIRS:
            out.append((("S", j // 2), "dve"))
        if j % 2 == 0 and j >= 2:
            out.append((("T", j // 2 - 1), "act"))
        if j % 2 == 1 and j >= 3:
            out.append((("O", (j - 3) // 2), "act"))
        if j < PAIRS:
            out.append((("z", j), "act"))
        if j == PAIRS:
            out += tiles("memT", 0) + tiles("memT", 1)
    out += [(("ya", c), "dve") for c in range(KD)]
    out += [((w, c), e) for c in range(KD) for w, e in (("zb", "dve"), ("zg", "act"))]
    out += [(("out", t, hf), "dve") for t in range(TT) for hf in range(2)]
    out += tiles("n2T", 0) + [(("xk", c), "act") for c in range(4)] + tiles("n2T", 1)
    out += [(("xq", c), "act") for c in range(4)] + [(("XS", hd), "act") for hd in range(XH)]
    out += [(("xv", hf, t), "act") for hf in range(2) for t in range(TT)]
    out.append((("XT", 0), "act"))
    for hd in range(XH):
        if hd + 1 < XH:
            out.append((("XT", hd + 1), "act"))
        out.append((("XO", hd), "act"))
    out += [(("xo", t, hf), "dve") for t in range(TT) for hf in range(2)]
    out += tiles("n3T", 0) + [(("logits", 0), "dve")] + tiles("n3T", 1) + [(("logits", 1), "dve")]
    out += [(("pos",), "dve"), (("GT",), "dve")]
    return out


def build_layer(nc, x, mem, g_mix, w_in, a_re, a_im, log_dt, b_re, b_im, c_re, c_im, d_skip, w_glu, w_proj_a,
                w_out, g_xattn, g_mem, w_xq, w_xkv, w_xo, g_moe, w_router, b_router, w_gu, b_gu, w_dn, b_dn,
                g_final, out):
    weights = dict(w_in=w_in[0], w_xkv=w_xkv[0], w_proj_a=w_proj_a[0], w_glu=w_glu[0], w_out=w_out[0],
                   w_xq=w_xq[0], w_xo=w_xo[0])
    order = dense_weights()
    plan = units()
    number = {u: n for n, (u, _) in enumerate(plan)}
    reader = dict(plan)
    rank = {u: sum(e == reader[u] for _, e in plan[:number[u]]) for u, _ in plan}
    last_user = last_units()

    with ExitStack() as ctx:
        def sem(name):
            return ctx.enter_context(nc.semaphore(name))

        top = [0]
        total = 53184
        arena = ctx.enter_context(nc.sbuf_tensor("arena", [P, total], F32))

        def at(start, n):
            return arena[:, start:start + n]

        def take(n):
            top[0] += n
            assert top[0] <= total, top[0]
            return top[0] - n

        ring0 = take(KD * 2 * FF + (FF // P) * D)
        gu_even = [at(ring0 + k * 2 * FF, 2 * FF) for k in range(KD)]
        dn_ring = [at(ring0 + KD * 2 * FF + k * D, D) for k in range(FF // P)]
        a0 = ring0
        turns = at(a0, PAIRS * 512).rearrange("p (j c s) -> p j c s", j=PAIRS, c=2)
        a0 += PAIRS * 512
        p_base = a0
        prod = at(a0, 4096).rearrange("p (b w c s) -> p b w c s", b=4, w=2, c=2)
        a0 += 4096
        gate_base = a0
        gates = at(a0, 4096).rearrange("p (c s) -> p c s", c=16)
        a0 += 4096
        qT = at(a0, 1024).rearrange("p (c s) -> p c s", c=4)
        kT = at(a0 + 1024, 1024).rearrange("p (c s) -> p c s", c=4)
        v_sb = at(a0 + 2048, 1024).rearrange("p (t n) -> p t n", t=TT)
        uT = at(a0 + 3072, 1024).rearrange("p (c s) -> p c s", c=4)
        a0 += 4096
        m_cos = at(a0, 512).rearrange("p (c s) -> p c s", c=2)
        m_sin = at(a0 + 512, 512).rearrange("p (c s) -> p c s", c=2)
        drive = at(a0 + 1024, 512).rearrange("p (c s) -> p c s", c=2)
        state = at(a0 + 1536, 1024).rearrange("p (b c s) -> p b c s", b=2, c=2)
        a0 += 3072
        Bd = at(a0, 1024).rearrange("p (w q m) -> p w q m", w=2, q=QG)
        a0 += 1024
        assert a0 <= ring0 + 24576
        b_raw = at(p_base, 1024).rearrange("p (w j c) -> p w j c", w=2, j=PAIRS)
        b_bar = at(p_base + 1024, 1024).rearrange("p (w j c) -> p w j c", w=2, j=PAIRS)
        c_raw = at(p_base + 2048, 1024).rearrange("p (w q m) -> p w q m", w=2, q=QG)
        b_tmp = at(p_base + 3072, 1024).rearrange("p (w j c) -> p w j c", w=2, j=PAIRS)
        g1 = gate_base + 4 * 256
        turn_a = at(g1, 512).rearrange("p (j c a) -> p j c a", j=PAIRS, c=2)
        turn_b = at(g1 + 512, 256).rearrange("p (j b) -> p j b", j=PAIRS)
        whole = at(g1 + 768, 2048)

        front0 = take(FW * SLOT)
        front = [at(front0 + s * SLOT, SLOT) for s in range(FW)]
        h_base = take(TT * D)
        h = at(h_base, TT * D).rearrange("p (t n) -> p t n", t=TT)
        xn_base = take(TT * D)
        xn = at(xn_base, TT * D).rearrange("p (t n) -> p t n", t=TT)
        xpT = at(xn_base, 2048).rearrange("p (b m s) -> p b m s", b=4, m=TT)
        nT_base = take(KD * S)
        nT = at(nT_base, KD * S).rearrange("p (k s) -> p k s", k=KD)
        attnT = at(take(4 * S), 4 * S).rearrange("p (c s) -> p c s", c=4)
        kx_base = take(4 * S)
        kxT = at(kx_base, 4 * S).rearrange("p (c s) -> p c s", c=4)
        geluT = at(kx_base, 4 * S).rearrange("p (c s) -> p c s", c=4)
        vx = at(take(TT * 512), TT * 512).rearrange("p (t n) -> p t n", t=TT)
        merged_base = take(KD * S)
        mergedT = at(merged_base, KD * S).rearrange("p (k s) -> p k s", k=KD)
        junk = at(merged_base, TT * D).rearrange("p (t n) -> p t n", t=TT)
        n2T = at(merged_base, KD * S).rearrange("p (k s) -> p k s", k=KD)
        xp = at(merged_base, 2048).rearrange("p (b t s) -> p b t s", b=4, t=TT)
        ct_base = take(3 * PAIRS * 32)
        Ct = at(ct_base, 3 * PAIRS * 32).rearrange("p (w j m) -> p w j m", w=3, j=PAIRS)
        router = at(ct_base, KD * E).rearrange("p (k e) -> p k e", k=KD)
        bdn = at(ct_base + 256, D)
        gfin = bdn
        ident = at(take(P), P)
        ones = at(take(P), P)
        tri = at(take(P), P)
        mask_base = take(384)
        mask = at(mask_base, 384)
        sc = at(take(768), 768).rearrange("p (b n) -> p b n", b=2)
        scT = at(take(384), 384)
        yskip = at(take(S), S)
        gtmp = at(take(S), S)
        bgu_raw = at(mask_base, 2 * FF)
        cols = at(take(N_ROWS), N_ROWS)
        rows_base = take(P)
        rows = at(rows_base, P)
        ldt = at(take(2), 2)
        par = at(take(14 * 16), 14 * 16).rearrange("p (n j) -> p n j", n=14)
        iota16 = at(take(16), 16)
        slot_no = at(take(2 * SLOTS), 2 * SLOTS)
        exp_no = at(rows_base, E)
        stat = at(take(64), 64)
        xstat = at(take(32), 32)
        logit = at(take(2 * E), 2 * E).rearrange("p (t e) -> p t e", t=TT)
        chosen = at(take(2 * E), 2 * E).rearrange("p (t e) -> p t e", t=TT)
        gate_w = at(take(2 * 33), 2 * 33).rearrange("p (t e) -> p t e", t=TT)
        pos = at(take(2 * 33), 2 * 33).rearrange("p (t e) -> p t e", t=TT)
        top8 = at(take(16), 16).rearrange("p (t e) -> p t e", t=TT)
        topi = ctx.enter_context(nc.sbuf_tensor("topi", [P, TT, 8], U32))
        topf = at(take(16), 16).rearrange("p (t e) -> p t e", t=TT)
        brt = at(take(E), E)
        rounds_i = ctx.enter_context(nc.sbuf_tensor("rounds_i", [P, 1], I32))
        f0 = [front0 + FF]

        def moe(n):
            f0[0] += n
            assert f0[0] <= front0 + 3 * SLOT
            return at(f0[0] - n, n)

        xeT = [moe(KD * SLOTS).rearrange("p (k s) -> p k s", k=KD) for _ in range(2)]
        pick = [moe(TT * SLOTS).rearrange("p (t s) -> p t s", t=TT) for _ in range(2)]
        spread = moe(TT * 2 * SLOTS).rearrange("p (t s) -> p t s", t=TT)
        spreadT = moe(TT * P).rearrange("p (t s) -> p t s", t=TT)
        gate_c, up_c, gate_t = [moe(HALF) for _ in range(3)]
        gated, hid = up_c, gate_t
        hidT = moe(HALF).rearrange("p (b s) -> p b s", b=4)
        y_sb = moe(HALF)
        GT = moe(S)
        pick_bias = [moe(SLOTS // 2).bitcast(BF16) for _ in range(2)]
        expert_rows = moe(E + 1)
        bgu = at(front0, FF).bitcast(BF16)
        gu_odd = [at(front0 + 4 * SLOT, SLOT), at(front0 + 5 * SLOT, SLOT), bgu_raw, at(front0 + 3 * SLOT, SLOT),
                  at(nT_base + KD * S, SLOT), at(nT_base + KD * S + SLOT, SLOT), at(nT_base, SLOT), at(h_base, SLOT)]
        gu_slots = [gu_even, gu_odd]

        psum = ctx.enter_context(nc.psum_tensor("psum", [P, 8, HALF], F32))
        BU, Y, DN = 4, 6, 7
        own_bank = {("n3T", 0, 0): BU, ("n3T", 0, 1): BU + 1, ("n3T", 1, 0): Y, ("n3T", 1, 1): DN, ("logits", 0): BU, ("logits", 1): BU + 1, ("pos",): DN, ("GT",): BU}

        x_in = [sem(f"x_in{t}") for t in range(TT)]
        mem_in, rows_in, b_in, c_in = sem("mem_in"), sem("rows_in"), sem("b_in"), sem("c_in")
        w_in_s = [sem(f"weights_in{s}") for s in range(FW)]
        router_in, gfin_in, bgu_in = sem("router_in"), sem("gfin_in"), sem("bgu_in")
        gu_in = [[sem(f"gu_in{k}_{b}") for k in range(KD)] for b in ("even", "odd")]
        dn_in = [sem(f"dn_in{k}") for k in range(FF // P)]
        out_in_dram = sem("out_in_dram")
        cleared = sem("cleared")
        consts = sem("consts")
        ldt_rows = sem("ldt_rows")
        par_s = sem("par_s")
        apar_s = sem("apar_s")
        bbar_s = sem("bbar_s")
        ang_s = sem("ang_s")
        turn_s = sem("turn_s")
        mm = sem("mm")
        unit_read = {"dve": sem("dve_read"), "act": sem("act_read")}
        rows_used = sem("rows_used")
        sq = sem("sq")
        ms = sem("ms")
        rstd_s = sem("rstd_s")
        xn_s = sem("xn_s")
        bu_s, bu_read = sem("bu_s"), sem("bu_read")
        state_s = sem("state_s")
        prod_s = sem("prod_s")
        y_s = sem("y_s")
        skip_s = sem("skip_s")
        gelu_act = sem("gelu_act")
        gelu_arg = sem("gelu_arg")
        gelu_s = sem("gelu_s")
        smax_s, exp_s, prob_s = sem("smax_s"), sem("exp_s"), sem("prob_s")
        merged_s = sem("merged_s")
        xmax_s, xprob_s = sem("xmax_s"), sem("xprob_s")
        shift_s = sem("shift_s")
        gate_exp = sem("gate_exp")
        chosen_s = sem("chosen_s")
        gates_s = sem("gates_s")
        GT_s, rounds_s = sem("GT_s"), sem("rounds_s")
        bgu_s = sem("bgu_s")
        opened = sem("opened")
        gu_used, dn_used = sem("gu_used"), sem("dn_used")
        pick_s, spread_s = sem("pick_s"), sem("spread_s")
        gather_s, xe_s = sem("gather_s"), sem("xe_s")
        gate_cs, gu_read = sem("gate_cs"), sem("gu_read")
        tanh_s, hid_s = sem("tanh_s"), sem("hid_s")
        hidT_ps, hidT_s = sem("hidT_ps"), sem("hidT_s")
        spT_ps, spT_s = sem("spT_ps"), sem("spT_s")
        y_ready = sem("y_ready")
        acc_s, outd = sem("acc_s"), sem("outd")

        block = ctx.enter_context(nc.Block())

        def bank_of(u):
            return own_bank.get(u, number[u] % MM)

        def arrived(eng, n):
            eng.wait_ge(w_in_s[n % FW], 16 * (n // FW + 1))

        def ready(eng, u):
            eng.wait_ge(mm, number[u] + 1)

        def evacuated(eng, u):
            eng.wait_ge(unit_read[reader[u]], rank[u] + 1)

        def later_rounds(eng, body):
            eng.wait_ge(rounds_s, 1)
            n = eng.value_load(rounds_i[0:1, 0:1], min_val=1, max_val=ROUNDS)
            with eng.Fori(1, ROUNDS) as r:
                with eng.If(n > r):
                    body(r)
            return n

        def gu_loads(sp, i, e, b):
            for k in range(KD):
                sp.wait_ge(gu_used, (i - 2) * KD + k + 1)
                sp.dma_start(gu_slots[b][k], w_gu[0].rearrange("e (k p) n -> (e k) p n", p=P)
                             [bass.ds(e * KD + k, 1)].rearrange("a p n -> p (a n)")).then_inc(gu_in[b][k], 16)

        def dn_loads(sp, i, e):
            for k in range(FF // P):
                sp.wait_ge(dn_used, (i - 1) * (FF // P) + k + 1)
                sp.dma_start(dn_ring[k], w_dn[0].rearrange("e (k p) n -> (e k) p n", p=P)
                             [bass.ds(e * (FF // P) + k, 1)].rearrange("a p n -> p (a n)")).then_inc(dn_in[k], 16)

        def rest_of_loads(sp, first):
            with sp.Fori(0, E // 2 - 1) as e2:
                for b in range(2):
                    e = e2 * 2 + b
                    gu_loads(sp, first + e + 2, e + 2, b)
                    dn_loads(sp, first + e + 1, e + 1)
            dn_loads(sp, first + E - 1, E - 1)

        @block.sync
        def _(sp):
            for t in range(TT):
                sp.dma_start(h[:, t, :], x[0, t * P:(t + 1) * P, :]).then_inc(x_in[t], 16)

            def load(n):
                name, cut, c = order[n]
                if n >= FW:
                    if last_user[n - FW] is None:
                        sp.wait_ge(rows_used, last_user[:n - FW + 1].count(None))
                    else:
                        ready(sp, last_user[n - FW])
                w, dst = weights[name], front[n % FW]
                if cut == "rows":
                    sp.dma_start(dst.rearrange("p (k n) -> p k n", k=2),
                                 w.rearrange("(k p) n -> p k n", p=P)[:, c:c + 2, :]).then_inc(w_in_s[n % FW], 16)
                else:
                    k = 8 if cut == "cols" else 4
                    sp.dma_start(dst.rearrange("p (k n) -> p k n", k=k),
                                 w.rearrange("(k p) n -> p k n", p=P)[:, :, c:c + SLOT // k]).then_inc(w_in_s[n % FW], 16)

            sp.wait_ge(cleared, 1)
            for r, src in ((R_ARE, a_re[0].rearrange("(j two) p -> j two p", two=2)),
                           (R_AIM, a_im[0].rearrange("(j two) p -> j two p", two=2))):
                sp.dma_start(rows[r:r + PAIRS, :].rearrange("j (two p) -> j two p", two=2), src).then_inc(rows_in, 16)
            sp.dma_start(ldt[R_LDT:R_LDT + PAIRS, :], log_dt[0].rearrange("(j two) -> j two", two=2)).then_inc(rows_in, 16)
            for i, g in enumerate((g_mix, g_xattn, g_mem, g_moe)):
                sp.dma_start(rows[R_GAIN + i * KD:R_GAIN + (i + 1) * KD, :], g[0].rearrange("(k p) -> k p", p=P)).then_inc(rows_in, 16)
            sp.dma_start(rows[R_DSK:R_DSK + QG, :].rearrange("q (g c) -> q g c", c=GC),
                          d_skip[0].rearrange("(q g) c -> q g c", q=QG)).then_inc(rows_in, 16)
            load(0)
            load(1)
            sp.wait_ge(cleared, 3)
            for w, b in enumerate((b_re, b_im)):
                for two in range(2):
                    sp.dma_start(b_raw[two * NS:(two + 1) * NS, w, :, two * GC:(two + 1) * GC],
                                 b[0].rearrange("(j two) p c -> two p j c", two=2)[two]).then_inc(b_in, 16)
            for w, c in enumerate((c_re, c_im)):
                for dup in range(2):
                    sp.dma_start(c_raw[:, w, :, dup * NS:(dup + 1) * NS],
                                 c[0].rearrange("(q g) c p -> (g c) q p", q=QG)).then_inc(c_in, 16)
            for n in range(2, FW):
                load(n)
            ready(sp, ("nT", 1, 1))
            for t in range(TT):
                sp.dma_start(xn[:, t, :], mem[0, t * P:(t + 1) * P, :]).then_inc(mem_in, 16)
            for n in range(FW, len(order)):
                load(n)
            sp.wait_ge(merged_s, KD)
            for part in range(3):
                sp.dma_start(bgu_raw[part * E:(part + 1) * E, :], b_gu[0]).then_inc(bgu_in, 16)
            for k in range(KD):
                sp.dma_start(gu_even[k], w_gu[0, 0, k * P:(k + 1) * P, :]).then_inc(gu_in[0][k], 16)
            for k in range(FF // P):
                sp.dma_start(dn_ring[k], w_dn[0, 0, k * P:(k + 1) * P, :]).then_inc(dn_in[k], 16)
            sp.dma_start(router, w_router[0].rearrange("(k p) e -> p k e", p=P)).then_inc(router_in, 16)
            sp.dma_start(bdn[0:E, :], b_dn[0]).then_inc(router_in, 16)
            sp.dma_start(brt[0:1, :], b_router).then_inc(router_in, 16)
            for k, place in enumerate(gu_odd):
                if k == 0:
                    ready(sp, ("xq", 3))
                elif k == 2:
                    sp.wait_ge(bgu_s, 1)
                elif k == 3:
                    ready(sp, ("xo", TT - 1, 1))
                elif k == 6:
                    ready(sp, ("logits", TT - 1))
                elif k == 7:
                    sp.wait_ge(opened, TT)
                sp.dma_start(place, w_gu[0, 1, k * P:(k + 1) * P, :]).then_inc(gu_in[1][k], 16)
            rest_of_loads(sp, 0)

            def again(r):
                gu_loads(sp, r * E, 0, 0)
                gu_loads(sp, r * E + 1, 1, 1)
                dn_loads(sp, r * E, 0)
                rest_of_loads(sp, r * E)

            later_rounds(sp, again)
            for t in range(TT):
                for hf in range(2):
                    cs = slice(hf * HALF, (hf + 1) * HALF)
                    sp.wait_ge(outd, 2 * t + hf + 1)
                    sp.dma_start(out[0, t * P:(t + 1) * P, cs], h[:, t, cs]).then_inc(out_in_dram, 16)
            sp.wait_ge(out_in_dram, 16 * TT * 2)

        @block.gpsimd
        def _(pool):
            gp = nc.gpsimd
            gp.memset(rows, 0.0).then_inc(cleared, 1)
            gp.memset(stat, 0.0).then_inc(cleared, 1)
            gp.memset(at(p_base, 1024), 0.0).then_inc(cleared, 1)
            gp.memset(ident, 0.0)
            gp.memset(ones, 1.0)
            gp.memset(mask, 0.0)
            gp.memset(at(ct_base, 3 * PAIRS * 32), 0.0)
            gp.iota(iota16, [[1, 16]], base=0, channel_multiplier=0, allow_small_or_imprecise_dtypes=True)
            gp.iota(slot_no, [[0, 2], [1, SLOTS]], base=0, channel_multiplier=0, allow_small_or_imprecise_dtypes=True)
            pool.drain()
            gp.memset(stat[:, 32:34], -0.5)
            gp.affine_select(out=ident, in_=ident, compare_op=ALU.not_equal, fill=1.0, base=0,
                             pattern=[[-1, P]], channel_multiplier=1)
            gp.affine_select(out=tri, in_=ones, compare_op=ALU.is_gt, fill=0.0, base=0,
                             pattern=[[1, P]], channel_multiplier=-1)
            for c in (0, 256):
                gp.affine_select(out=mask[:, c:c + P], in_=mask[:, c:c + P], compare_op=ALU.is_ge, fill=NEG, base=0,
                                 pattern=[[-1, P]], channel_multiplier=1)
            pool.drain()
            gp.memset(stat[:, 34:35], 0.0).then_inc(consts, 1)

            def root(n):
                for t in range(TT):
                    pool.wait_ge(ms, 2 * n + t - 1)
                    gp.tensor_tensor(stat[:, 4 + t:5 + t], stat[:, 2 + t:3 + t], stat[:, 32:33], ALU.pow).then_inc(rstd_s, 1)

            root(1)
            root(2)
            for j in range(PAIRS):
                pool.wait_ge(state_s, j + 1)
                pool.wait_ge(turn_s, j // 4 + 1)
                if j >= 4:
                    pool.wait_ge(y_s, j // 4)
                else:
                    evacuated(pool, ("C", 1))
                for w in range(2):
                    last = gp.tensor_tensor(prod[:, j % 4, w], state[:, j % 2],
                                            turns[:, j, w, :].unsqueeze(1).broadcast_to((P, 2, S)), ALU.mult)
                last.then_inc(prod_s, 1)
            gp.iota(exp_no, [[1, E]], base=0, channel_multiplier=0, allow_small_or_imprecise_dtypes=True)
            root(3)
            root(4)
            pool.drain()
            gp.memset(stat[:, 35:36], 0.0).then_inc(consts, 1)
            pool.wait_ge(gu_used, KD + 1)
            pool.dma_start(gfin, g_final.partition_broadcast(P)).then_inc(gfin_in, 16)
            root(5)

        @block.scalar
        def _(act):
            sa = nc.scalar
            def squares(t, src, scratch):
                sa.activation(scratch, src, ACT.Square, accum_out=stat[:, t:t + 1]).then_inc(sq, 1)

            act.wait_ge(cleared, 2)
            sa.activation(stat[:, 42:43], stat[:, 43:44], ACT.Square)
            for t in range(TT):
                act.wait_ge(x_in[t], 16)
                squares(t, h[:, t, :], junk[:, t, :])

            def evacuate(u, dst, scale=1.0, func=ACT.Copy, part=slice(0, P)):
                ready(act, u)
                sa.activation(dst, psum[part, bank_of(u), 0:dst.free_size()], func, scale=scale).then_inc(unit_read["act"], 1)

            act.wait_ge(par_s, 1)
            sa.activation(par[:, 3], cols[:, R_LDT:R_LDT + 16], ACT.Tanh, scale=1.0 / 16).then_inc(apar_s, 1)
            act.wait_ge(par_s, 2)
            sa.activation(par[:, 5], par[:, 4], ACT.Tanh, scale=0.5).then_inc(apar_s, 1)
            act.wait_ge(par_s, 3)
            for w in range(2):
                last = sa.activation(par[:, 8 + w], par[:, 6 + w], ACT.Sin, scale=TWO_PI)
            sa.activation(par[:, 10], par[:, 13], ACT.Sin, scale=TWO_PI / 2).then_inc(apar_s, 1)

            def turn(g):
                act.wait_ge(ang_s, g + 1)
                t = turns[:, 4 * g:4 * g + 4].rearrange("p j c s -> p (j c s)")
                sa.activation(t, t, ACT.Sin, scale=TWO_PI).then_inc(turn_s, 1)

            for c in range(4):
                evacuate(("u", c), uT[:, c, :])
            for c in range(4):
                evacuate(("q", c), qT[:, c, :])
            for c in range(4):
                evacuate(("k", c), kT[:, c, :])
            act.wait_ge(mem_in, 32)
            for t in range(TT):
                squares(t, xn[:, t, :], junk[:, t, :])
            turn(0)
            for hf in range(2):
                for t in range(TT):
                    evacuate(("v", hf, t), v_sb[:, t, hf * 256:(hf + 1) * 256])
                turn(1 + hf)
            turn(3)

            def exps(hd):
                act.wait_ge(smax_s, hd + 1)
                b = sc[:, hd % 2]
                sa.activation(b[:, 0:P], b[:, 0:P], ACT.Exp, bias=stat[:, 12:13] if hd % 2 == 0 else stat[:, 14:15],
                              accum_out=stat[:, 16 + 2 * (hd % 2):17 + 2 * (hd % 2)])
                sa.activation(b[:, P:384], b[:, P:384], ACT.Exp, bias=stat[:, 13:14] if hd % 2 == 0 else stat[:, 15:16],
                              accum_out=stat[:, 17 + 2 * (hd % 2):18 + 2 * (hd % 2)]).then_inc(exp_s, 1)

            def gelu_square(q):
                act.wait_ge(skip_s, q + 1)
                sa.activation(gtmp, yskip, ACT.Square).then_inc(gelu_act, 1)

            def gelu_tanh(q):
                act.wait_ge(gelu_arg, q + 1)
                sa.activation(gtmp, gtmp, ACT.Tanh, scale=0.7978845608028654).then_inc(gelu_act, 1)

            for j in range(STEPS):
                if j % 2 == 0 and j < PAIRS:
                    exps(j // 2)
                if j % 2 == 0 and j >= 2:
                    hd = j // 2 - 1
                    if hd:
                        ready(act, ("O", hd - 1))
                    evacuate(("T", hd), scT)
                if j % 2 == 1 and j >= 3:
                    hd = (j - 3) // 2
                    part = slice(DH * (hd % 2), DH * (hd % 2) + DH)
                    evacuate(("O", hd), attnT[part, hd // 2, :], part=part)
                if j < PAIRS:
                    evacuate(("z", j), gates[:, j, :], scale=0.5, func=ACT.Tanh)
                if j % 4 == 1 and 5 <= j < PAIRS:
                    gelu_square((j - 5) // 4)
                if j % 4 == 2 and 5 <= j < PAIRS:
                    gelu_tanh((j - 6) // 4)
            gelu_square(3)
            gelu_tanh(3)
            for c in range(KD):
                if c >= 2:
                    act.wait_ge(merged_s, c - 1)
                evacuate(("zg", c), sc[:, c % 2, 0:S], scale=0.25, func=ACT.Tanh)
            for t in range(TT):
                evacuated(act, ("out", t, 1))
                squares(t, h[:, t, :], xn[:, t, :])
            for c in range(4):
                evacuate(("xk", c), kxT[:, c, :])
            for c in range(4):
                evacuate(("xq", c), attnT[:, c, :])
            for hd in range(XH):
                u = ("XS", hd)
                act.wait_ge(xmax_s, hd + 1)
                for t in range(TT):
                    o = 2 * hd + t
                    last = sa.activation(xp[:, hd, t, :], psum[:, bank_of(u), t * 256:(t + 1) * 256], ACT.Exp,
                                         scale=XDH ** -0.5, bias=xstat[:, 8 + o:9 + o], accum_out=xstat[:, 16 + o:17 + o])
                last.then_inc(unit_read["act"], 1)
            for hf in range(2):
                for t in range(TT):
                    evacuate(("xv", hf, t), vx[:, t, hf * 256:(hf + 1) * 256])

            def xT(hd):
                evacuate(("XT", hd), xpT[:, hd].rearrange("p m s -> p (m s)"))

            xT(0)
            for hd in range(XH):
                if hd + 1 < XH:
                    xT(hd + 1)
                evacuate(("XO", hd), attnT[:, hd, :])
            for t in range(TT):
                evacuated(act, ("xo", t, 1))
                squares(t, h[:, t, :], xn[:, t, :])
            for t in range(TT):
                act.wait_ge(shift_s, t + 1)
                last = sa.activation(gate_w[:, t, 0:E], logit[:, t, :], ACT.Exp, bias=stat[:, 36 + t:37 + t])
            last.then_inc(gate_exp, 1)

            def tanh_of_gate(i):
                act.wait_ge(gate_cs, i + 1)
                sa.activation(gate_t, gate_c, ACT.Tanh, scale=ALPHA / 2).then_inc(tanh_s, 1)

            def keep_hidT(i):
                act.wait_ge(hidT_ps, i + 1)
                sa.activation(hidT.rearrange("p b s -> p (b s)"), psum[:, 6, :], ACT.Copy, scale=0.5).then_inc(hidT_s, 1)

            def keep_spreadT(i):
                act.wait_ge(spT_ps, i + 1)
                sa.activation(spreadT.rearrange("p t s -> p (t s)"), psum[:, 6, 0:TT * P], ACT.Copy).then_inc(spT_s, 1)

            def keep_y(i):
                act.wait_ge(dn_used, (i + 1) * KD)
                sa.activation(y_sb, psum[:, DN, :], ACT.Copy).then_inc(y_ready, 1)

            def step(i):
                tanh_of_gate(i)
                keep_hidT(i)
                keep_spreadT(i)
                keep_y(i)

            def step_ahead(i):
                keep_spreadT(i - 1)
                tanh_of_gate(i)
                keep_y(i - 1)
                keep_hidT(i)

            step(0)
            step(1)
            with act.Fori(1, AHEAD // 2) as e2:
                for b in range(2):
                    step(e2 * 2 + b)
            tanh_of_gate(AHEAD)
            keep_hidT(AHEAD)
            step_ahead(AHEAD + 1)
            with act.Fori(AHEAD // 2 + 1, E // 2) as e2:
                for b in range(2):
                    step_ahead(e2 * 2 + b)

            def again(r):
                with act.Fori(0, E // 2) as e2:
                    for b in range(2):
                        step_ahead(r * E + e2 * 2 + b)

            n = later_rounds(act, again)
            keep_spreadT(n * E - 1)
            keep_y(n * E - 1)
            for t in range(TT):
                act.wait_ge(acc_s, t + 1)
                squares(t, psum[:, 2 * t:2 * t + 2, :].rearrange("p b n -> p (b n)"), xn[:, t, :])

        @block.vector
        def _(dve):
            ve = nc.vector
            fence = dve.drain

            read = unit_read["dve"]

            def mean_square(n, t):
                dve.wait_ge(sq, 2 * n + t - 1)
                ve.tensor_scalar(stat[:, 2 + t:3 + t], stat[:, t:t + 1], 1.0 / D, EPS, ALU.mult, ALU.add).then_inc(ms, 1)

            def normalise(n, t, src):
                dve.wait_ge(rstd_s, 2 * n + t - 1)
                ve.tensor_scalar(xn[:, t, :], src[:, t, :], stat[:, 4 + t:5 + t], None, ALU.mult).then_inc(xn_s, 1)

            def transposed(name, g, t, dst):
                for kq in range(2):
                    u = (name, t, kq)
                    ready(dve, u)
                    o = R_GAIN + g * KD + 4 * kq
                    ve.tensor_tensor(dst[:, 4 * kq:4 * kq + 4, t * P:(t + 1) * P],
                                     psum[:, bank_of(u), :].rearrange("p (k s) -> p k s", k=4),
                                     cols[:, o:o + 4].unsqueeze(2).broadcast_to((P, 4, P)), ALU.mult).then_inc(read, 1)

            for t in range(TT):
                mean_square(1, t)
                normalise(1, t, h)
                if t == 0:
                    dve.wait_ge(rows_in, 8 * 16)
                    ve.tensor_copy(rows[R_LDT:R_LDT + PAIRS, :].rearrange("j (two p) -> j two p", two=2),
                                   ldt[R_LDT:R_LDT + PAIRS, :].unsqueeze(2).broadcast_to((PAIRS, 2, NS))).then_inc(ldt_rows, 1)
            ready(dve, ("rows",))
            ve.tensor_copy(cols, psum[:, bank_of(("rows",)), 0:N_ROWS])
            fence()
            transposed("nT", 0, 0, nT)
            fence().then_inc(read, 1)
            are, dt, lre, frac = par[:, 0], par[:, 1], par[:, 4], par[:, 2]
            ve.tensor_scalar(are, cols[:, R_ARE:R_ARE + 16], -1e-4, None, ALU.min).then_inc(par_s, 1)
            transposed("nT", 0, 1, nT)
            dve.wait_ge(apar_s, 1)

            def one_over_ratio(dst, t, tmp):
                ve.tensor_scalar(tmp, t, -1.0, 1.0, ALU.mult, ALU.add)
                fence()
                ve.reciprocal(tmp, tmp)
                fence()
                ve.scalar_tensor_tensor(dst, t, 1.0, tmp, ALU.add, ALU.mult)
                fence()

            one_over_ratio(dt, par[:, 3], par[:, 12])
            for _ in range(3):
                ve.tensor_tensor(dt, dt, dt, ALU.mult)
                fence()
            ve.tensor_tensor(lre, are, dt, ALU.mult)
            fence()
            ve.tensor_tensor(frac, cols[:, R_AIM:R_AIM + 16], dt, ALU.mult).then_inc(par_s, 1)
            fence()
            ve.tensor_scalar(frac, frac, 1.0 / 6.283185307179586, None, ALU.mult)
            fence()

            def reduce(dst, src, tmp, add=0.0):
                ve.tensor_scalar(dst, src, 1.0, add, ALU.mult, ALU.add)
                fence()
                ve.tensor_scalar(tmp, dst, ROUND, ROUND, ALU.add, ALU.subtract)
                fence()
                ve.tensor_tensor(dst, dst, tmp, ALU.subtract)
                fence()

            reduce(par[:, 13], frac, par[:, 12])
            reduce(par[:, 6], par[:, 13], par[:, 12], 0.25)
            ve.tensor_copy(par[:, 7], par[:, 13])
            ve.tensor_copy(par[:, 1], par[:, 13]).then_inc(par_s, 1)
            dve.wait_ge(apar_s, 3)
            t_ = par[:, 5]
            ve.tensor_scalar(par[:, 12], t_, -1.0, 1.0, ALU.mult, ALU.add)
            fence()
            ve.reciprocal(par[:, 12], par[:, 12])
            fence()
            decay, rm1 = par[:, 3], par[:, 4]
            ve.scalar_tensor_tensor(decay, t_, 1.0, par[:, 12], ALU.add, ALU.mult)
            ve.scalar_tensor_tensor(rm1, t_, 2.0, par[:, 12], ALU.mult, ALU.mult)
            fence()
            lb_re, lb_im, tmp1, tmp2 = par[:, 5], par[:, 2], par[:, 12], par[:, 11]
            ve.tensor_tensor(lb_re, rm1, par[:, 8], ALU.mult)
            ve.tensor_tensor(tmp1, par[:, 10], par[:, 10], ALU.mult)
            ve.tensor_tensor(lb_im, decay, par[:, 9], ALU.mult)
            fence()
            ve.scalar_tensor_tensor(lb_re, tmp1, -2.0, lb_re, ALU.mult, ALU.add)
            ve.tensor_tensor(tmp2, are, are, ALU.mult)
            ve.tensor_tensor(par[:, 13], cols[:, R_AIM:R_AIM + 16], cols[:, R_AIM:R_AIM + 16], ALU.mult)
            fence()
            ve.tensor_tensor(tmp2, tmp2, par[:, 13], ALU.add)
            fence()
            ve.reciprocal(tmp2, tmp2)
            kre, kim = par[:, 6], par[:, 7]
            aim = cols[:, R_AIM:R_AIM + 16]
            ve.tensor_tensor(kre, lb_re, are, ALU.mult)
            ve.tensor_tensor(tmp1, lb_im, aim, ALU.mult)
            ve.tensor_tensor(kim, lb_im, are, ALU.mult)
            ve.tensor_tensor(par[:, 13], lb_re, aim, ALU.mult)
            fence()
            ve.tensor_tensor(kre, kre, tmp1, ALU.add)
            ve.tensor_tensor(kim, kim, par[:, 13], ALU.subtract)
            fence()
            ve.tensor_tensor(kre, kre, tmp2, ALU.mult)
            ve.tensor_tensor(kim, kim, tmp2, ALU.mult)
            fence()
            dve.wait_ge(b_in, 64)
            kre_b, kim_b = (k.unsqueeze(2).broadcast_to((P, PAIRS, 32)) for k in (kre, kim))
            ve.tensor_tensor(b_bar[:, 0], b_raw[:, 0], kre_b, ALU.mult)
            ve.tensor_tensor(b_tmp[:, 0], b_raw[:, 1], kim_b, ALU.mult)
            ve.tensor_tensor(b_bar[:, 1], b_raw[:, 1], kre_b, ALU.mult)
            ve.tensor_tensor(b_tmp[:, 1], b_raw[:, 0], kim_b, ALU.mult)
            fence()
            ve.tensor_tensor(b_bar[:, 0], b_bar[:, 0], b_tmp[:, 0], ALU.subtract)
            ve.tensor_tensor(b_bar[:, 1], b_bar[:, 1], b_tmp[:, 1], ALU.add).then_inc(bbar_s, 1)
            fence()
            ve.tensor_scalar(par[:, 0], par[:, 1], 16.0, None, ALU.mult)
            fence()
            reduce(par[:, 0], par[:, 0], par[:, 12])
            big = whole[:, 0:256].rearrange("p (j a) -> p j a", j=PAIRS)
            it = iota16.unsqueeze(1).broadcast_to((P, PAIRS, 16))
            ta = whole[:, 256:512].rearrange("p (j a) -> p j a", j=PAIRS)
            ve.tensor_tensor(ta, par[:, 0].unsqueeze(2).broadcast_to((P, PAIRS, 16)), it, ALU.mult)
            ve.tensor_tensor(turn_b, par[:, 1].unsqueeze(2).broadcast_to((P, PAIRS, 16)), it, ALU.mult)
            fence()
            reduce(turn_b, turn_b, big)
            for c, add in ((0, 0.25), (1, 0.0)):
                reduce(turn_a[:, :, c, :], ta, big, add)
            fence()
            def angles(g):
                js = slice(4 * g, 4 * g + 4)
                four = turns[:, js].rearrange("p j c s -> p (j c s)")
                for c in range(2):
                    ve.tensor_tensor(turns[:, js, c, :].rearrange("p j (a b) -> p j a b", a=16),
                                     turn_a[:, js, c, :].unsqueeze(3).broadcast_to((P, 4, 16, 16)),
                                     turn_b[:, js, :].unsqueeze(2).broadcast_to((P, 4, 16, 16)), ALU.add)
                fence()
                ve.tensor_scalar(whole, four, ROUND, ROUND, ALU.add, ALU.subtract)
                fence()
                ve.tensor_tensor(four, four, whole, ALU.subtract).then_inc(ang_s, 1)

            angles(0)
            for w in range(2):
                u = ("Bd", w)
                ready(dve, u)
                ve.tensor_copy(Bd[:, w], psum[:, bank_of(u), :].rearrange("p (q m) -> p q m", q=QG)).then_inc(read, 1)
            for w in range(2):
                u = ("C", w)
                ready(dve, u)
                for two in range(2):
                    sl = slice(two * NS, (two + 1) * NS)
                    src = psum[sl, bank_of(u), :].rearrange("p (j m) -> p j m", j=PAIRS)[:, :, two * GC:(two + 1) * GC]
                    dst = Ct[sl, :, :, two * GC:(two + 1) * GC]
                    if w == 0:
                        ve.tensor_copy(dst[:, 0], src)
                        last = ve.tensor_scalar(dst[:, 1], src, -1.0, None, ALU.mult)
                    else:
                        last = ve.tensor_scalar(dst[:, 2], src, -1.0, None, ALU.mult)
                last.then_inc(read, 1)
            angles(1)
            angles(2)
            for t in range(TT):
                mean_square(2, t)
            for t in range(TT):
                normalise(2, t, xn)
            angles(3)
            def scan(j):
                bank = BU + j % 2
                dve.wait_ge(bu_s, j + 1)
                dve.wait_ge(turn_s, j // 4 + 1)
                bu = psum[:, bank, :].rearrange("p (c s) -> p c s", c=2)
                ve.tensor_tensor(m_cos, bu, turns[:, j, 0, :].unsqueeze(1).broadcast_to((P, 2, S)), ALU.mult)
                ve.tensor_tensor(m_sin, bu, turns[:, j, 1, :].unsqueeze(1).broadcast_to((P, 2, S)), ALU.mult).then_inc(bu_read, 1)
                fence()
                ve.tensor_tensor(drive[:, 0], m_cos[:, 0], m_sin[:, 1], ALU.add)
                ve.tensor_tensor(drive[:, 1], m_cos[:, 1], m_sin[:, 0], ALU.subtract)
                fence()
                if j >= 2:
                    dve.wait_ge(prod_s, j - 1)
                for c in range(2):
                    last = ve.tensor_tensor_scan(state[:, j % 2, c], decay[:, j:j + 1].broadcast_to((P, S)), drive[:, c],
                                                 0.0, ALU.mult, ALU.add)
                last.then_inc(state_s, 1)

            def softmax_head(hd):
                u = ("S", hd)
                ready(dve, u)
                b = sc[:, hd % 2]
                if hd >= 2:
                    dve.wait_ge(mm, number[("T", hd - 2)] + 1)
                ve.scalar_tensor_tensor(b, psum[:, bank_of(u), 0:384], DH ** -0.5, mask, ALU.mult, ALU.add).then_inc(read, 1)
                fence()
                o = 12 + 2 * (hd % 2)
                ve.reduce_max(stat[:, 8:9], b[:, 0:P], AX)
                ve.reduce_max(stat[:, 9:10], b[:, P:384], AX)
                fence()
                ve.tensor_scalar(stat[:, o:o + 2], stat[:, 8:10], -1.0, None, ALU.mult).then_inc(smax_s, 1)

            def normalise_head(hd):
                dve.wait_ge(exp_s, hd + 1)
                b = sc[:, hd % 2]
                o = 16 + 2 * (hd % 2)
                ve.reciprocal(stat[:, 10:12], stat[:, o:o + 2])
                fence()
                ve.tensor_scalar(b[:, 0:P], b[:, 0:P], stat[:, 10:11], None, ALU.mult)
                ve.tensor_scalar(b[:, P:384], b[:, P:384], stat[:, 11:12], None, ALU.mult).then_inc(prob_s, 1)

            def gelu_start(q):
                dve.wait_ge(y_s, q + 1)
                if q:
                    fence()
                ve.scalar_tensor_tensor(yskip, uT[:, q, :], cols[:, R_DSK + q:R_DSK + q + 1], psum[:, Y, 0:S],
                                        ALU.mult, ALU.add).then_inc(skip_s, 1)

            def gelu_argument(q):
                dve.wait_ge(gelu_act, 2 * q + 1)
                ve.tensor_scalar(gtmp, gtmp, 0.044715, 1.0, ALU.mult, ALU.add)
                fence()
                ve.tensor_tensor(gtmp, gtmp, yskip, ALU.mult).then_inc(gelu_arg, 1)

            def gelu_end(q):
                dve.wait_ge(gelu_act, 2 * q + 2)
                ve.scalar_tensor_tensor(geluT[:, q, :], gtmp, 1.0, yskip, ALU.add, ALU.mult).then_inc(gelu_s, 1)

            for j in range(STEPS):
                if j < PAIRS:
                    scan(j)
                if j % 2 == 0 and j < PAIRS:
                    softmax_head(j // 2)
                if j % 2 == 1 and j < PAIRS:
                    normalise_head(j // 2)
                if 5 <= j < PAIRS:
                    if j % 4 == 1:
                        gelu_start((j - 5) // 4)
                    elif j % 4 == 2:
                        gelu_argument((j - 6) // 4)
                    elif j % 4 == 3:
                        gelu_end((j - 7) // 4)
                if j == PAIRS:
                    for t in range(TT):
                        transposed("memT", 2, t, nT)
            for c in range(KD):
                if c == 4:
                    gelu_start(3)
                    gelu_argument(3)
                    gelu_end(3)
                u = ("ya", c)
                ready(dve, u)
                evacuated(dve, ("z", PAIRS - 1))
                ve.scalar_tensor_tensor(gates[:, c, :], gates[:, c, :], 1.0, psum[:, bank_of(u), 0:S],
                                        ALU.add, ALU.mult).then_inc(read, 1)
            for c in range(KD):
                u = ("zb", c)
                evacuated(dve, ("zg", c))
                fence()
                ve.scalar_tensor_tensor(yskip, sc[:, c % 2, 0:S], 1.0, psum[:, bank_of(u), 0:S],
                                        ALU.add, ALU.mult).then_inc(read, 1)
                fence()
                ve.scalar_tensor_tensor(gtmp, gates[:, KD + c, :], 1.0, yskip, ALU.add, ALU.mult)
                fence()
                ve.tensor_scalar(gtmp, gtmp, 0.125, None, ALU.mult)
                fence()
                ve.scalar_tensor_tensor(mergedT[:, c, :], gates[:, c, :], 0.5, gtmp, ALU.mult, ALU.add).then_inc(merged_s, 1)

            def residual_norm(name, n, first_tile):
                for t in range(TT):
                    for hf in range(2):
                        u = (name, t, hf)
                        ready(dve, u)
                        cs = slice(hf * HALF, (hf + 1) * HALF)
                        ve.tensor_tensor(h[:, t, cs], h[:, t, cs], psum[:, bank_of(u), :], ALU.add).then_inc(read, 1)
                    if t:
                        transposed(*first_tile)
                    mean_square(n, t)
                    normalise(n, t, h)

            residual_norm("out", 3, ("n2T", 1, 0, n2T))
            transposed("n2T", 1, 1, n2T)
            for hd in range(XH):
                u = ("XS", hd)
                ready(dve, u)
                ve.tensor_reduce(xstat[:, 2 * hd:2 * hd + 2], psum[:, bank_of(u), :].rearrange("p (t s) -> p t s", t=TT), AX, ALU.max)
                fence()
                ve.tensor_scalar(xstat[:, 8 + 2 * hd:10 + 2 * hd], xstat[:, 2 * hd:2 * hd + 2], -XDH ** -0.5, None, ALU.mult).then_inc(xmax_s, 1)
            for hd in range(XH):
                evacuated(dve, ("XS", hd))
                ve.reciprocal(xstat[:, 24 + 2 * hd:26 + 2 * hd], xstat[:, 16 + 2 * hd:18 + 2 * hd])
                fence()
                for t in range(TT):
                    last = ve.tensor_scalar(xp[:, hd, t, :], xp[:, hd, t, :], xstat[:, 24 + 2 * hd + t:25 + 2 * hd + t], None, ALU.mult)
                last.then_inc(xprob_s, 1)
            dve.wait_ge(bgu_in, 48)
            ready(dve, ("xv", 0, 1))
            ve.tensor_copy(bgu[0:3 * E, :], bgu_raw[0:3 * E, :])
            for part in (1, 2):
                fence()
                for lo in range(part * E, 3 * E, E):
                    ve.tensor_tensor(bgu_raw[lo:lo + E, :], bgu_raw[lo:lo + E, :], bgu[lo:lo + E, :], ALU.subtract)
                fence()
                for lo in range(part * E, 3 * E, E):
                    last = ve.tensor_copy(bgu[lo:lo + E, :], bgu_raw[lo:lo + E, :])
            last.then_inc(bgu_s, 1)
            residual_norm("xo", 4, ("n3T", 3, 0, nT))
            transposed("n3T", 3, 1, nT)
            for part in range(3):
                rs = slice(part * E, (part + 1) * E)
                ve.tensor_copy(expert_rows[rs, 0:E], ident[rs, rs])
                ve.tensor_copy(expert_rows[rs, E:E + 1], ident[rs, part * E:part * E + 1])

            dve.wait_ge(consts, 2)
            for t in range(TT):
                u = ("logits", t)
                ready(dve, u)
                ve.tensor_copy(logit[:, t, :], psum[:, bank_of(u), 0:E]).then_inc(read, 1)
                fence()
                ve.max(top8[:, t, :], logit[:, t, :])
                fence()
                ve.tensor_scalar(stat[:, 36 + t:37 + t], top8[:, t, 0:1], -1.0, None, ALU.mult).then_inc(shift_s, 1)
                ve.max_index(topi[:, t, :], top8[:, t, :], logit[:, t, :])
                fence()
                ve.tensor_copy(topf[:, t, :], topi[:, t, :])
                fence()
                ve.tensor_scalar(chosen[:, t, :], exp_no, topf[:, t, 0:1], None, ALU.is_equal)
                for n in range(1, TOPK):
                    fence()
                    last = ve.scalar_tensor_tensor(chosen[:, t, :], exp_no, topf[:, t, n:n + 1], chosen[:, t, :],
                                                   ALU.is_equal, ALU.add)
                last.then_inc(chosen_s, 1)
            fence()
            dve.wait_ge(gate_exp, 1)
            ve.tensor_tensor(gate_w[:, :, 0:E], gate_w[:, :, 0:E], chosen, ALU.mult)
            fence()
            ve.tensor_reduce(stat[:, 46:48], gate_w[:, :, 0:E], AX, ALU.add)
            fence()
            ve.reciprocal(stat[:, 46:48], stat[:, 46:48])
            fence()
            for t in range(TT):
                ve.tensor_scalar(gate_w[:, t, 0:E], gate_w[:, t, 0:E], stat[:, 46 + t:47 + t], None, ALU.mult)
            fence()
            ve.tensor_copy(gate_w[:, :, E:E + 1], gate_w[:, :, 0:1]).then_inc(gates_s, 1)
            u = ("pos",)
            ready(dve, u)
            pp = psum[:, bank_of(u), 0:3 * E].rearrange("p (t e) -> p t e", t=3)
            ve.scalar_tensor_tensor(pos[:, :, 0:E], pp[:, 0:2, :], OFF, chosen, ALU.add, ALU.mult)
            ve.reduce_max(stat[:, 48:49], pp[:, 2, :], AX).then_inc(read, 1)
            fence()
            ve.tensor_scalar(pos[:, :, 0:E], pos[:, :, 0:E], OFF, None, ALU.subtract)
            fence()
            ve.tensor_scalar(pos[:, :, E:E + 1], pos[:, :, 0:1], float(SLOTS), None, ALU.subtract)
            u = ("GT",)
            ready(dve, u)
            ve.tensor_copy(GT[0:E, :], psum[0:E, bank_of(u), 0:S]).then_inc(GT_s, 1)
            fence()
            gain_e = cols[:, R_GAIN + 3 * KD:R_GAIN + 4 * KD].unsqueeze(2).broadcast_to((P, KD, SLOTS))

            def picks(col, b):
                for t in range(TT):
                    ve.tensor_scalar(pick[b][:, t, :], slot_no[:, 0:SLOTS], pos[:, t, col], None, ALU.is_equal)
                ve.tensor_copy(pick_bias[b][0:3 * E, :], expert_rows[0:3 * E, col].broadcast_to((3 * E, SLOTS))).then_inc(pick_s, 1)

            def gathered(i, b):
                dve.wait_ge(gather_s, i + 1)
                ve.tensor_tensor(xeT[b], psum[:, 6, :].rearrange("p (k s) -> p k s", k=KD), gain_e, ALU.mult).then_inc(xe_s, 1)

            picks(slice(0, 1), 0)
            gathered(0, 0)
            ve.tensor_scalar(stat[:, 49:50], stat[:, 48:49], float(SLOTS), 1.0, ALU.is_gt, ALU.add)
            fence()
            for r in range(2, ROUNDS):
                ve.scalar_tensor_tensor(stat[:, 49:50], stat[:, 48:49], float(r * SLOTS), stat[:, 49:50], ALU.is_gt, ALU.add)
                fence()
            ve.tensor_copy(rounds_i[:, :], stat[:, 49:50]).then_inc(rounds_s, 1)

            def expert(i, e, b, first=False):
                picks(bass.ds(e + 1, 1), 1 - b)
                gathered(i + 1, 1 - b)
                dve.wait_ge(gu_used, (i + 1) * KD)
                ve.tensor_scalar(gate_c, psum[:, 4, :], LIMIT, None, ALU.min).then_inc(gate_cs, 1)
                ve.tensor_scalar(up_c, psum[:, 5, :], LIMIT, -LIMIT, ALU.min, ALU.max).then_inc(gu_read, 1)
                fence()
                ve.scalar_tensor_tensor(gated, up_c, 1.0, gate_c, ALU.add, ALU.mult)
                fence()
                dve.wait_ge(tanh_s, i + 1)
                ve.scalar_tensor_tensor(hid, gate_t, 1.0, gated, ALU.add, ALU.mult).then_inc(hid_s, 1)
                if not first:
                    dve.wait_ge(spT_ps, i)
                for t in range(TT):
                    last = ve.tensor_scalar(spread[:, t, :], slot_no, pos[:, t, bass.ds(e, 1)], gate_w[:, t, bass.ds(e, 1)],
                                            ALU.is_equal, ALU.mult)
                last.then_inc(spread_s, 1)

            expert(0, 0, 0, first=True)
            expert(1, 1, 1)
            with dve.Fori(1, E // 2) as e2:
                for b in range(2):
                    expert(e2 * 2 + b, e2 * 2 + b, b)

            def later(r):
                fence()
                ve.tensor_scalar(pos, pos, float(SLOTS), None, ALU.subtract)
                fence()
                with dve.Fori(0, E // 2) as e2:
                    for b in range(2):
                        expert(r * E + e2 * 2 + b, e2 * 2 + b, b)

            later_rounds(dve, later)
            dve.wait_ge(gfin_in, 16)
            for t in range(TT):
                mean_square(5, t)
                dve.wait_ge(rstd_s, 9 + t)
                for hf in range(2):
                    cs = slice(hf * HALF, (hf + 1) * HALF)
                    ve.scalar_tensor_tensor(h[:, t, cs], psum[:, 2 * t + hf, :], stat[:, 4 + t:5 + t], gfin[:, cs],
                                            ALU.mult, ALU.mult).then_inc(outd, 1)

        @block.tensor
        def _(pe):
            te = nc.tensor
            done_blocks = [0]

            def open_unit(u):
                if number[u] >= MM:
                    evacuated(pe, plan[number[u] - MM][0])
                return psum[:, bank_of(u), :]

            def transposes(name, n_norm, t):
                for kq in range(2):
                    ps = open_unit((name, t, kq))
                    pe.wait_ge(xn_s, 2 * n_norm + t - 1)
                    for k in range(4):
                        last = te.transpose(ps[:, k * P:(k + 1) * P], xn[:, t, (4 * kq + k) * P:(4 * kq + k + 1) * P], ident)
                    last.then_inc(mm, 1)

            def next_block():
                n = done_blocks[0]
                done_blocks[0] += 1
                arrived(pe, n)
                return front[n % FW]

            def column_unit(u, w, c, rhs, kn):
                ps = open_unit(u)
                for k in range(kn):
                    last = te.matmul(ps[:, 0:S], w[:, k, c * P:(c + 1) * P], rhs[:, k, :], start=(k == 0), stop=(k == kn - 1))
                last.then_inc(mm, 1)

            pe.wait_ge(consts, 1)
            transposes("nT", 1, 0)
            ps = open_unit(("rows",))
            pe.wait_ge(ldt_rows, 1)
            te.transpose(ps[:, 0:N_ROWS], rows[0:N_ROWS, :], ident[0:N_ROWS, 0:N_ROWS]).then_inc(mm, 1)
            transposes("nT", 1, 1)

            def parameters():
                for w in range(2):
                    ps = open_unit(("Bd", w))
                    pe.wait_ge(bbar_s, 1)
                    for q in range(QG):
                        last = te.transpose(ps[:, q * P:(q + 1) * P], b_bar[:, w, 4 * q:4 * q + 4, :].rearrange("p j c -> p (j c)"), ident)
                    last.then_inc(mm, 1)
                for w in range(2):
                    ps = open_unit(("C", w))
                    pe.wait_ge(c_in, 64)
                    for q in range(QG):
                        last = te.transpose(ps[:, q * P:(q + 1) * P], c_raw[:, w, q, :], ident)
                    last.then_inc(mm, 1)

            evacuated(pe, ("nT", 1, 1))
            for name in ("u", "q", "k"):
                for hf in range(2):
                    w = next_block().rearrange("p (k n) -> p k n", k=KD)
                    for c in range(2):
                        column_unit((name, 2 * hf + c), w, c, nT, KD)
                if name == "q":
                    parameters()
            def drive_in(j):
                if j >= 2:
                    pe.wait_ge(bu_read, j - 1)
                if j % 4 == 0:
                    evacuated(pe, ("u", j // 4))
                o = 32 * (j % 4)
                for w in range(2):
                    last = te.matmul(psum[:, BU + j % 2, w * S:(w + 1) * S], Bd[o:o + 32, w, j // 4, :],
                                     uT[o:o + 32, j // 4, :], start=True, stop=True)
                last.then_inc(bu_s, 1)

            evacuated(pe, ("Bd", 1))
            drive_in(0)
            drive_in(1)
            for hf in range(2):
                w = next_block().rearrange("p (k n) -> p k n", k=KD)
                for t in range(TT):
                    u = ("v", hf, t)
                    ps = open_unit(u)
                    for k in range(KD):
                        last = te.matmul(ps[:, 0:256], nT[:, k, t * P:(t + 1) * P], w[:, k, :], start=(k == 0), stop=(k == KD - 1))
                    last.then_inc(mm, 1)

            def y_out(q):
                pe.wait_ge(prod_s, 4 * (q + 1))
                if q == 0:
                    evacuated(pe, ("C", 1))
                else:
                    pe.wait_ge(skip_s, q)
                for n, (w, m, c) in enumerate(((0, 0, 0), (2, 0, 1), (1, 1, 1), (2, 1, 0))):
                    for jj in range(4):
                        last = te.matmul(psum[32 * jj:32 * jj + 32, Y, 0:S], Ct[:, w, 4 * q + jj, :], prod[:, jj, m, c, :],
                                         start=(n == 0), stop=(n == 3))
                last.then_inc(y_s, 1)

            def scores(hd):
                ps = open_unit(("S", hd))
                o, c = DH * (hd % 2), hd // 2
                if hd % 2 == 0:
                    evacuated(pe, ("k", c))
                te.matmul(ps[:, 0:P], qT[o:o + DH, c, 0:P], kT[o:o + DH, c, 0:P], start=True, stop=True)
                te.matmul(ps[:, P:384], qT[o:o + DH, c, P:S], kT[o:o + DH, c, :], start=True, stop=True).then_inc(mm, 1)

            def probs_T(hd):
                ps = open_unit(("T", hd))
                pe.wait_ge(prob_s, hd + 1)
                b = sc[:, hd % 2]
                for n in range(3):
                    last = te.transpose(ps[:, n * P:(n + 1) * P], b[:, n * P:(n + 1) * P], ident)
                last.then_inc(mm, 1)

            def weighted(hd):
                open_unit(("O", hd))
                evacuated(pe, ("T", hd))
                evacuated(pe, ("v", 1, 1))
                o = DH * (hd % 2)
                ps = psum[o:o + DH, bank_of(("O", hd)), :]
                te.matmul(ps[:, 0:S], v_sb[:, 0, hd * DH:(hd + 1) * DH], scT[:, 0:S], start=True, stop=False)
                te.matmul(ps[:, P:S], v_sb[:, 1, hd * DH:(hd + 1) * DH], scT[:, S:384], start=False, stop=True).then_inc(mm, 1)

            for j in range(STEPS):
                if 2 <= j < PAIRS:
                    drive_in(j)
                if j % 2 == 0 and j < PAIRS:
                    scores(j // 2)
                if j % 2 == 0 and j >= 2:
                    probs_T(j // 2 - 1)
                if j % 2 == 1 and j >= 3:
                    weighted((j - 3) // 2)
                if j < PAIRS:
                    if j % 2 == 0:
                        w = next_block().rearrange("p (k n) -> p k n", k=KD)
                    column_unit(("z", j), w, j % 2, nT, KD)
                if j == PAIRS:
                    for t in range(TT):
                        transposes("memT", 2, t)
                if j % 4 == 0 and 4 <= j < PAIRS:
                    y_out((j - 4) // 4)
            evacuated(pe, ("O", HEADS - 1))
            for hf in range(2):
                w = next_block().rearrange("p (k n) -> p k n", k=4)
                for c in range(4):
                    column_unit(("ya", 4 * hf + c), w, c, attnT, 4)
                if hf == 0:
                    y_out(3)
            pe.wait_ge(gelu_s, 4)
            for hf in range(2):
                wa = next_block().rearrange("p (k n) -> p k n", k=4)
                wb = next_block().rearrange("p (k n) -> p k n", k=4)
                for c in range(4):
                    column_unit(("zb", 4 * hf + c), wa, c, geluT, 4)
                    column_unit(("zg", 4 * hf + c), wb, c, geluT, 4)

            def rows_out(name, src, blocks, source_ready):
                ws = [next_block().rearrange("p (k n) -> p k n", k=2) for _ in range(blocks)]
                for t in range(TT):
                    for hf in range(2):
                        open_unit((name, t, hf))
                    for k in range(2 * blocks):
                        source_ready(k)
                        for hf in range(2):
                            last = te.matmul(psum[:, bank_of((name, t, hf)), :], src[:, k, t * P:(t + 1) * P],
                                             ws[k // 2][:, k % 2, hf * HALF:(hf + 1) * HALF],
                                             start=(k == 0), stop=(k == 2 * blocks - 1))
                            if k == 2 * blocks - 1:
                                last.then_inc(mm, 1)
                        if t == TT - 1 and k % 2 == 1 and k < 2 * blocks - 1:
                            last.then_inc(rows_used, 1)

            rows_out("out", mergedT, 4, lambda k: pe.wait_ge(merged_s, k + 1))
            transposes("n2T", 3, 0)
            for hf in range(2):
                w = next_block().rearrange("p (k n) -> p k n", k=KD)
                for c in range(2):
                    if hf == c == 0:
                        evacuated(pe, ("memT", 1, 1))
                    column_unit(("xk", 2 * hf + c), w, c, nT, KD)
            transposes("n2T", 3, 1)
            evacuated(pe, ("n2T", 1, 1))
            for hf in range(2):
                w = next_block().rearrange("p (k n) -> p k n", k=KD)
                for c in range(2):
                    column_unit(("xq", 2 * hf + c), w, c, n2T, KD)
            for hd in range(XH):
                ps = open_unit(("XS", hd))
                evacuated(pe, ("xq", hd))
                for t in range(TT):
                    last = te.matmul(ps[:, t * S:(t + 1) * S], attnT[:, hd, t * P:(t + 1) * P], kxT[:, hd, :], start=True, stop=True)
                last.then_inc(mm, 1)
            for hf in range(2):
                w = next_block().rearrange("p (k n) -> p k n", k=KD)
                for t in range(TT):
                    ps = open_unit(("xv", hf, t))
                    for k in range(KD):
                        last = te.matmul(ps[:, 0:256], nT[:, k, t * P:(t + 1) * P], w[:, k, :], start=(k == 0), stop=(k == KD - 1))
                    last.then_inc(mm, 1)

            def xprobs_T(hd):
                ps = open_unit(("XT", hd))
                pe.wait_ge(xprob_s, hd + 1)
                for m in range(TT):
                    for t in range(TT):
                        last = te.transpose(ps[:, m * S + t * P:m * S + (t + 1) * P], xp[:, hd, t, m * P:(m + 1) * P], ident)
                last.then_inc(mm, 1)

            xprobs_T(0)
            for hd in range(XH):
                if hd + 1 < XH:
                    xprobs_T(hd + 1)
                ps = open_unit(("XO", hd))
                evacuated(pe, ("XT", hd))
                for m in range(TT):
                    last = te.matmul(ps[:, 0:S], vx[:, m, hd * XDH:(hd + 1) * XDH], xpT[:, hd, m, :], start=(m == 0), stop=(m == 1))
                last.then_inc(mm, 1)
            rows_out("xo", attnT, 2, lambda k: evacuated(pe, ("XO", k)))
            def open_sum(t):
                for hf in range(2):
                    last = te.matmul(psum[:, 2 * t + hf, :], ident, h[:, t, hf * HALF:(hf + 1) * HALF], start=True, stop=False)
                last.then_inc(opened, 1)

            for t in range(TT):
                transposes("n3T", 4, t)
                if t == 0:
                    evacuated(pe, ("xo", TT - 1, 1))
                open_sum(t)
                ps = open_unit(("logits", t))
                pe.wait_ge(router_in, 48)
                evacuated(pe, ("n3T", t, 1))
                for k in range(KD):
                    te.matmul(ps[:, 0:E], nT[:, k, t * P:(t + 1) * P], router[:, k, :], start=(k == 0), stop=False)
                te.matmul(ps[:, 0:E], ones[0:1, 0:P], brt[0:1, :], start=False, stop=True).then_inc(mm, 1)

            def keep_clock_up(n):
                for _ in range(n):
                    te.matmul(psum[:, Y, :], ident, xn[:, 0, 0:HALF], start=True, stop=True)

            evacuated(pe, ("n3T", 1, 0))
            keep_clock_up(2)
            ps = open_unit(("pos",))
            pe.wait_ge(chosen_s, TT)
            te.matmul(ps[:, 0:E], tri, chosen[:, 0, :], start=True, stop=True)
            te.matmul(ps[:, E:2 * E], ones, chosen[:, 0, :], start=True, stop=False)
            te.matmul(ps[:, E:2 * E], tri, chosen[:, 1, :], start=False, stop=True)
            te.matmul(ps[:, 2 * E:3 * E], ones, chosen[:, 0, :], start=True, stop=False)
            te.matmul(ps[:, 2 * E:3 * E], ones, chosen[:, 1, :], start=False, stop=True).then_inc(mm, 1)
            ps = open_unit(("GT",))
            pe.wait_ge(gates_s, 1)
            for t in range(TT):
                last = te.transpose(ps[0:E, t * P:(t + 1) * P], gate_w[:, t, 0:E], ident)
            last.then_inc(mm, 1)

            keep_clock_up(2)

            def gather(i, b):
                pe.wait_ge(pick_s, i + 1)
                for k in range(KD):
                    for t in range(TT):
                        last = te.matmul(psum[:, 6, k * SLOTS:(k + 1) * SLOTS], xn[:, t, k * P:(k + 1) * P], pick[b][:, t, :],
                                         start=(t == 0), stop=(t == TT - 1))
                last.then_inc(gather_s, 1)

            gather(0, 0)
            def combine(tile, stop=False):
                for hf in range(2):
                    last = te.matmul(psum[:, 2 * tile + hf, :], spreadT[hf * SLOTS:(hf + 1) * SLOTS, tile, :],
                                     y_sb[hf * SLOTS:(hf + 1) * SLOTS, :], start=False, stop=stop, skip_group_check=not stop)
                return last

            def gate_up(i, pair, b):
                for gu in range(2):
                    for hf in range(2):
                        te.matmul(psum[hf * SLOTS:(hf + 1) * SLOTS, 4 + gu, :], pick_bias[b][0:3 * E, :],
                                  bgu[0:3 * E, gu * FF + hf * HALF:gu * FF + (hf + 1) * HALF], start=True, stop=False)
                pe.wait_ge(xe_s, i + 1)
                for k in range(KD):
                    w = gu_slots[b][k]
                    pe.wait_ge(gu_in[b][k], 16 * (pair + 1))
                    for gu in range(2):
                        for hf in range(2):
                            last = te.matmul(psum[hf * SLOTS:(hf + 1) * SLOTS, 4 + gu, :], xeT[b][:, k, :],
                                             w[:, gu * FF + hf * HALF:gu * FF + (hf + 1) * HALF],
                                             start=False, stop=(k == KD - 1))
                    last.then_inc(gu_used, 1)
                    if k == 4:
                        gather(i + 1, 1 - b)

            def spread_T():
                for t in range(TT):
                    last = te.transpose(psum[:, 6, t * P:(t + 1) * P], spread[:, t, :], ident)
                last.then_inc(spT_ps, 1)

            def hid_T(i):
                pe.wait_ge(hid_s, i + 1)
                for n in range(4):
                    last = te.transpose(psum[:, 6, n * P:(n + 1) * P], hid[:, n * P:(n + 1) * P], ident)
                last.then_inc(hidT_ps, 1)

            def down(i, between=None):
                pe.wait_ge(hidT_s, i + 1)
                for k in range(FF // P):
                    pe.wait_ge(dn_in[k], 16 * (i + 1))
                    n, c = k % 4, k // 4
                    for hf in range(2):
                        last = te.matmul(psum[hf * SLOTS:(hf + 1) * SLOTS, DN, :], hidT[:, n, c * SLOTS:(c + 1) * SLOTS],
                                         dn_ring[k][:, hf * HALF:(hf + 1) * HALF], start=(k == 0), stop=(k == FF // P - 1))
                    last.then_inc(dn_used, 1)
                    if between and k in between:
                        between[k]()

            def step(i, pair, b, first=False):
                if first:
                    pe.wait_ge(GT_s, 1)
                else:
                    pe.wait_ge(gu_read, i)
                    pe.wait_ge(spT_s, i)
                gate_up(i, pair, b)
                if first:
                    for t in range(TT):
                        for hf in range(2):
                            te.matmul(psum[:, 2 * t + hf, :], GT[0:E, t * P:(t + 1) * P],
                                      bdn[0:E, hf * HALF:(hf + 1) * HALF], start=False, stop=False, skip_group_check=True)
                else:
                    pe.wait_ge(y_ready, i)
                    for t in range(TT):
                        combine(t)
                pe.wait_ge(xe_s, i + 2)
                hid_T(i)
                pe.wait_ge(spread_s, i + 1)
                pe.wait_ge(hidT_s, i + 1)
                spread_T()
                down(i)

            def step_ahead(i, pair, b):
                pe.wait_ge(gu_read, i)
                pe.wait_ge(hidT_s, i)
                gate_up(i, pair, b)
                pe.wait_ge(y_ready, i - 1)
                for t in range(TT):
                    combine(t)
                pe.wait_ge(xe_s, i + 2)
                pe.wait_ge(spread_s, i)
                spread_T()
                down(i - 1)
                pe.wait_ge(spT_s, i)
                hid_T(i)

            step(0, 0, 0, first=True)
            step(1, 0, 1)
            with pe.Fori(1, AHEAD // 2) as e2:
                for b in range(2):
                    step(e2 * 2 + b, e2, b)
            pe.wait_ge(gu_read, AHEAD)
            pe.wait_ge(spT_s, AHEAD)
            gate_up(AHEAD, AHEAD // 2, 0)
            pe.wait_ge(xe_s, AHEAD + 2)
            hid_T(AHEAD)
            step_ahead(AHEAD + 1, AHEAD // 2, 1)
            with pe.Fori(AHEAD // 2 + 1, E // 2) as e2:
                for b in range(2):
                    step_ahead(e2 * 2 + b, e2, b)

            def again(r):
                with pe.Fori(0, E // 2) as e2:
                    for b in range(2):
                        step_ahead(r * E + e2 * 2 + b, r * (E // 2) + e2, b)

            n = later_rounds(pe, again)
            pe.wait_ge(spread_s, n * E)
            down(n * E - 1, {1: lambda: combine(0), 3: lambda: combine(1), 5: spread_T})
            pe.wait_ge(spT_s, n * E)
            pe.wait_ge(y_ready, n * E)
            for t in range(TT):
                combine(t, True).then_inc(acc_s, 1)


_INS = ["x", "mem", "g_mix", "w_in", "a_re", "a_im", "log_dt", "b_re", "b_im", "c_re", "c_im", "d_skip", "w_glu",
        "w_proj_a", "w_out", "g_xattn", "g_mem", "w_xq", "w_xkv", "w_xo", "g_moe", "w_router", "b_router", "w_gu",
        "b_gu", "w_dn", "b_dn", "g_final"]


def kernel(**inputs):
    import numpy as _np
    import concourse.bacc as _bacc
    from concourse import mybir as _mybir
    from concourse.bass_utils import run_bass_kernel_spmd as _run

    nc = _bacc.Bacc("TRN2", target_bir_lowering=False, num_devices=1)
    arrays, args = {}, []
    for name in _INS:
        a = _np.ascontiguousarray(inputs[name])
        arrays[f"in_{name}"] = a
        args.append(nc.dram_tensor(f"in_{name}", a.shape, _mybir.dt.from_np(a.dtype), kind="ExternalInput").ap())
    out = nc.dram_tensor("out_dram", (1, S, D), F32, kind="ExternalOutput").ap()
    build_layer(nc, *args, out)
    r = _run(nc, [arrays], core_ids=[0])
    return r.results[0]["out_dram"]
```
